# Optimizing a Trainium2 kernel written in Bass

```python
import math
import jax, jax.numpy as jnp
from jax import lax
import numpy as np

D_MODEL = 1024
BATCH = 1
SEQ = 1024
DEPTH = 1
DEC_BATCH = 8
DEC_SEQ = 1
PAST_LEN = 8192
PAGE_SIZE = 128

RWKV_WIDTH = D_MODEL // 2
RWKV_HEAD = 64
RWKV_HEADS = RWKV_WIDTH // RWKV_HEAD
DECAY_LORA = 64
AAA_LORA = 64
GATE_LORA = 128
LNX_EPS = 64e-5
S5_WIDTH = D_MODEL // 2
S5_GROUP = 16
S5_GROUPS = S5_WIDTH // S5_GROUP
S5_STATE = 64
FFN_DIM = 2816
NORM_EPS = 1e-6
N_BRANCH = 2
RWKV_COLS = 3 * RWKV_WIDTH + DECAY_LORA + AAA_LORA + GATE_LORA
IN_COLS = RWKV_COLS + S5_WIDTH + N_BRANCH * D_MODEL

kernel_name = 'rwkv7_s5_gated_macaron_step'

def rmsnorm(x, g):
    xf = x.astype(jnp.float32)
    y = xf * lax.rsqrt(jnp.mean(xf * xf, axis=-1, keepdims=True) + NORM_EPS)
    return (y * g.astype(jnp.float32)).astype(x.dtype)

def swiglu(x, w_gate, w_up, w_down):
    return (jax.nn.silu(x @ w_gate) * (x @ w_up)) @ w_down

def token_shift(f, prev):
    return jnp.concatenate([prev[:, None, :], f[:, :-1, :]], axis=1)

def rwkv7_recurrence(r, w, k, v, kk, b, S0):
    def step(S, inp):
        r_t, w_t, k_t, v_t, kk_t, b_t = inp
        sa = jnp.einsum('bhvk,bhk->bhv', S, -kk_t)
        S = (S * w_t[:, :, None, :] + sa[..., None] * b_t[:, :, None, :]
             + v_t[..., None] * k_t[:, :, None, :])
        o = jnp.einsum('bhvk,bhk->bhv', S, r_t)
        return S, o
    xs = tuple(jnp.moveaxis(t, 1, 0) for t in (r, w, k, v, kk, b))
    S, o = lax.scan(step, S0, xs)
    return jnp.moveaxis(o, 0, 1), S

def rwkv7_branch(f, S0, p):
    B, L, _ = f.shape
    H, N, W = RWKV_HEADS, RWKV_HEAD, RWKV_WIDTH
    f = f.astype(jnp.float32)
    r = f[..., 0:W]
    k = f[..., W:2 * W]
    v = f[..., 2 * W:3 * W]
    o0 = 3 * W
    wd = f[..., o0:o0 + DECAY_LORA]
    ad = f[..., o0 + DECAY_LORA:o0 + DECAY_LORA + AAA_LORA]
    gd = f[..., o0 + DECAY_LORA + AAA_LORA:]
    w_log = -jax.nn.softplus(-(p['w0'] + jnp.tanh(wd) @ p['w_up'])) - 0.5
    decay = jnp.exp(-jnp.exp(w_log))
    a = jax.nn.sigmoid(p['a0'] + ad @ p['a_up'])
    g = jax.nn.sigmoid(gd) @ p['g_up']
    heads = lambda t: t.reshape(B, L, H, N)
    kk = heads(k * p['k_k'])
    kk = kk / jnp.maximum(jnp.sqrt(jnp.sum(kk * kk, axis=-1, keepdims=True)), 1e-12)
    k = k * (1.0 + (a - 1.0) * p['k_a'])
    r_h, k_h, v_h, a_h = heads(r), heads(k), heads(v), heads(a)
    o, S = rwkv7_recurrence(r_h, heads(decay), k_h, v_h, kk, kk * a_h, S0.astype(jnp.float32))
    mu = jnp.mean(o, axis=-1, keepdims=True)
    var = jnp.mean(jnp.square(o - mu), axis=-1, keepdims=True)
    o = ((o - mu) * lax.rsqrt(var + LNX_EPS)).reshape(B, L, W) * p['lnx_w'] + p['lnx_b']
    bonus = jnp.sum(r_h * k_h * p['r_k'], axis=-1, keepdims=True) * v_h
    return (o + bonus.reshape(B, L, W)) * g, S

def s5_branch(u, xr0, xi0, p):
    B, L, _ = u.shape
    f32 = jnp.float32
    uf = u.astype(f32)
    ug = uf.reshape(B, L, S5_GROUPS, S5_GROUP)
    lam_r = p['A_re'].astype(f32)
    lam_i = p['A_im'].astype(f32)
    dt = jnp.exp(p['log_dt'].astype(f32))[:, None]
    mag = jnp.exp(lam_r * dt)
    ab_r, ab_i = mag * jnp.cos(lam_i * dt), mag * jnp.sin(lam_i * dt)
    den = lam_r * lam_r + lam_i * lam_i
    q_r = ((ab_r - 1.0) * lam_r + ab_i * lam_i) / den
    q_i = (ab_i * lam_r - (ab_r - 1.0) * lam_i) / den
    B_re, B_im = p['B_re'].astype(f32), p['B_im'].astype(f32)
    bb_r = q_r[..., None] * B_re - q_i[..., None] * B_im
    bb_i = q_r[..., None] * B_im + q_i[..., None] * B_re
    bu_r = jnp.einsum('blgh,gph->blgp', ug, bb_r)
    bu_i = jnp.einsum('blgh,gph->blgp', ug, bb_i)
    xr0 = xr0.astype(f32)
    xi0 = xi0.astype(f32)
    bu_r = bu_r.at[:, 0].add(ab_r * xr0 - ab_i * xi0)
    bu_i = bu_i.at[:, 0].add(ab_r * xi0 + ab_i * xr0)
    a_r = jnp.broadcast_to(ab_r, (1, L, S5_GROUPS, S5_STATE))
    a_i = jnp.broadcast_to(ab_i, (1, L, S5_GROUPS, S5_STATE))

    def combine(e1, e2):
        a1r, a1i, b1r, b1i = e1
        a2r, a2i, b2r, b2i = e2
        return (a2r * a1r - a2i * a1i, a2r * a1i + a2i * a1r,
                a2r * b1r - a2i * b1i + b2r, a2r * b1i + a2i * b1r + b2i)

    _, _, xr, xi = lax.associative_scan(combine, (a_r, a_i, bu_r, bu_i), axis=1)
    C_re, C_im = p['C_re'].astype(f32), p['C_im'].astype(f32)
    y = jnp.einsum('blgp,ghp->blgh', xr, C_re) - jnp.einsum('blgp,ghp->blgh', xi, C_im)
    y = y.reshape(B, L, S5_WIDTH) + p['D_skip'] * uf
    z = jax.nn.gelu(y)
    return z * jax.nn.sigmoid(z @ p['w_glu']), xr[:, -1], xi[:, -1]

def hybrid_layer(x, shift0, wkv0, s5r0, s5i0, p):
    x = x + 0.5 * swiglu(rmsnorm(x, p['g_ffn1']), p['ffn1_gate'], p['ffn1_up'], p['ffn1_down'])
    h = rmsnorm(x, p['g_mix'])
    proj = h @ p['w_in']
    f_rwkv = proj[..., :RWKV_COLS]
    u = proj[..., RWKV_COLS:RWKV_COLS + S5_WIDTH]
    gates = jax.nn.sigmoid(proj[..., RWKV_COLS + S5_WIDTH:].astype(jnp.float32))
    shifted = token_shift(f_rwkv, shift0.astype(f_rwkv.dtype))
    f_mix = f_rwkv + p['mu_shift'] * (shifted - f_rwkv)
    y_a, wkv = rwkv7_branch(f_mix, wkv0, p)
    y_b, s5r, s5i = s5_branch(u, s5r0, s5i0, p)
    merged = gates[..., :D_MODEL] * (y_a @ p['w_a_up']) + gates[..., D_MODEL:] * (y_b @ p['w_b_up'])
    x = x + (merged @ p['w_out']).astype(x.dtype)
    x = x + 0.5 * swiglu(rmsnorm(x, p['g_ffn2']), p['ffn2_gate'], p['ffn2_up'], p['ffn2_down'])
    return x, f_rwkv[:, -1], wkv, s5r, s5i

def setup_inputs(seed: int = 0) -> dict:
    key = jax.random.key(seed)
    ks = iter(jax.random.split(key, 64))
    f32 = jnp.float32

    def nrm(shape, scale):
        return scale * jax.random.normal(next(ks), shape, f32)

    def uni(shape, lo, hi):
        return jax.random.uniform(next(ks), shape, f32, lo, hi)

    W = RWKV_WIDTH
    n_idx = jnp.arange(S5_STATE, dtype=f32)
    return {
        'x_prompt': nrm((BATCH, SEQ, D_MODEL), 1.0),
        'x_sample': nrm((DEC_BATCH, DEC_SEQ, D_MODEL), 1.0),
        'state_shift': nrm((DEPTH, DEC_BATCH, RWKV_COLS), 1.0),
        'state_wkv': nrm((DEPTH, DEC_BATCH, RWKV_HEADS, RWKV_HEAD, RWKV_HEAD), 0.5),
        'state_s5_re': nrm((DEPTH, DEC_BATCH, S5_GROUPS, S5_STATE), 0.5),
        'state_s5_im': nrm((DEPTH, DEC_BATCH, S5_GROUPS, S5_STATE), 0.5),
        'g_ffn1': 1.0 + nrm((DEPTH, D_MODEL), 0.02),
        'ffn1_gate': nrm((DEPTH, D_MODEL, FFN_DIM), D_MODEL ** -0.5),
        'ffn1_up': nrm((DEPTH, D_MODEL, FFN_DIM), D_MODEL ** -0.5),
        'ffn1_down': nrm((DEPTH, FFN_DIM, D_MODEL), FFN_DIM ** -0.5),
        'g_mix': 1.0 + nrm((DEPTH, D_MODEL), 0.02),
        'w_in': nrm((DEPTH, D_MODEL, IN_COLS), D_MODEL ** -0.5),
        'mu_shift': uni((DEPTH, RWKV_COLS), 0.0, 1.0),
        'w0': uni((DEPTH, W), -6.0, -1.0),
        'w_up': nrm((DEPTH, DECAY_LORA, W), 0.1),
        'a0': nrm((DEPTH, W), 0.5),
        'a_up': nrm((DEPTH, AAA_LORA, W), AAA_LORA ** -0.5),
        'g_up': nrm((DEPTH, GATE_LORA, W), GATE_LORA ** -0.5),
        'k_k': 0.85 + nrm((DEPTH, W), 0.05),
        'k_a': 1.0 + nrm((DEPTH, W), 0.05),
        'r_k': nrm((DEPTH, RWKV_HEADS, RWKV_HEAD), 0.1),
        'lnx_w': 1.0 + nrm((DEPTH, W), 0.02),
        'lnx_b': nrm((DEPTH, W), 0.01),
        'A_re': -0.5 * jnp.exp(nrm((DEPTH, S5_GROUPS, S5_STATE), 0.05)),
        'A_im': jnp.pi * n_idx + nrm((DEPTH, S5_GROUPS, S5_STATE), 0.02),
        'log_dt': uni((DEPTH, S5_GROUPS), math.log(0.001), math.log(0.1)),
        'B_re': nrm((DEPTH, S5_GROUPS, S5_STATE, S5_GROUP), (2 * S5_GROUP) ** -0.5),
        'B_im': nrm((DEPTH, S5_GROUPS, S5_STATE, S5_GROUP), (2 * S5_GROUP) ** -0.5),
        'C_re': nrm((DEPTH, S5_GROUPS, S5_GROUP, S5_STATE), (2 * S5_STATE) ** -0.5),
        'C_im': nrm((DEPTH, S5_GROUPS, S5_GROUP, S5_STATE), (2 * S5_STATE) ** -0.5),
        'D_skip': nrm((DEPTH, S5_WIDTH), 1.0),
        'w_glu': nrm((DEPTH, S5_WIDTH, S5_WIDTH), S5_WIDTH ** -0.5),
        'w_a_up': nrm((DEPTH, RWKV_WIDTH, D_MODEL), RWKV_WIDTH ** -0.5),
        'w_b_up': nrm((DEPTH, S5_WIDTH, D_MODEL), S5_WIDTH ** -0.5),
        'w_out': nrm((DEPTH, D_MODEL, D_MODEL), D_MODEL ** -0.5),
        'g_ffn2': 1.0 + nrm((DEPTH, D_MODEL), 0.02),
        'ffn2_gate': nrm((DEPTH, D_MODEL, FFN_DIM), D_MODEL ** -0.5),
        'ffn2_up': nrm((DEPTH, D_MODEL, FFN_DIM), D_MODEL ** -0.5),
        'ffn2_down': nrm((DEPTH, FFN_DIM, D_MODEL), FFN_DIM ** -0.5),
        'g_final': 1.0 + nrm((D_MODEL,), 0.02),
    }

def reference(x_prompt, x_sample, state_shift, state_wkv, state_s5_re, state_s5_im,
              g_ffn1, ffn1_gate, ffn1_up, ffn1_down, g_mix, w_in, mu_shift,
              w0, w_up, a0, a_up, g_up, k_k, k_a, r_k, lnx_w, lnx_b,
              A_re, A_im, log_dt, B_re, B_im, C_re, C_im, D_skip, w_glu,
              w_a_up, w_b_up, w_out, g_ffn2, ffn2_gate, ffn2_up, ffn2_down, g_final):
    p = {'g_ffn1': g_ffn1, 'ffn1_gate': ffn1_gate, 'ffn1_up': ffn1_up, 'ffn1_down': ffn1_down,
         'g_mix': g_mix, 'w_in': w_in, 'mu_shift': mu_shift,
         'w0': w0, 'w_up': w_up, 'a0': a0, 'a_up': a_up, 'g_up': g_up,
         'k_k': k_k, 'k_a': k_a, 'r_k': r_k, 'lnx_w': lnx_w, 'lnx_b': lnx_b,
         'A_re': A_re, 'A_im': A_im, 'log_dt': log_dt, 'B_re': B_re, 'B_im': B_im,
         'C_re': C_re, 'C_im': C_im, 'D_skip': D_skip, 'w_glu': w_glu,
         'w_a_up': w_a_up, 'w_b_up': w_b_up, 'w_out': w_out,
         'g_ffn2': g_ffn2, 'ffn2_gate': ffn2_gate, 'ffn2_up': ffn2_up, 'ffn2_down': ffn2_down}
    bp = x_prompt.shape[0]
    f32 = jnp.float32
    hp, hs = x_prompt, x_sample
    sh_p, wk_p, sr_p, si_p = [], [], [], []
    sh_s, wk_s, sr_s, si_s = [], [], [], []
    for layer in range(DEPTH):
        pl = {name: arr[layer] for name, arr in p.items()}
        hp, a1, a2, a3, a4 = hybrid_layer(
            hp,
            jnp.zeros((bp, RWKV_COLS), f32),
            jnp.zeros((bp, RWKV_HEADS, RWKV_HEAD, RWKV_HEAD), f32),
            jnp.zeros((bp, S5_GROUPS, S5_STATE), f32),
            jnp.zeros((bp, S5_GROUPS, S5_STATE), f32), pl)
        sh_p.append(a1); wk_p.append(a2); sr_p.append(a3); si_p.append(a4)
        hs, b1, b2, b3, b4 = hybrid_layer(
            hs, state_shift[layer], state_wkv[layer], state_s5_re[layer], state_s5_im[layer], pl)
        sh_s.append(b1); wk_s.append(b2); sr_s.append(b3); si_s.append(b4)
    y_prompt = rmsnorm(hp, g_final)
    y_sample = rmsnorm(hs, g_final)
    new_shift_prompt = jnp.stack(sh_p, 0).astype(state_shift.dtype)
    new_wkv_prompt = jnp.stack(wk_p, 0).astype(state_wkv.dtype)
    new_s5_re_prompt = jnp.stack(sr_p, 0).astype(state_s5_re.dtype)
    new_s5_im_prompt = jnp.stack(si_p, 0).astype(state_s5_im.dtype)
    new_shift_sample = jnp.stack(sh_s, 0).astype(state_shift.dtype)
    new_wkv_sample = jnp.stack(wk_s, 0).astype(state_wkv.dtype)
    new_s5_re_sample = jnp.stack(sr_s, 0).astype(state_s5_re.dtype)
    new_s5_im_sample = jnp.stack(si_s, 0).astype(state_s5_im.dtype)
    return (y_prompt, y_sample, new_shift_prompt, new_wkv_prompt, new_s5_re_prompt, new_s5_im_prompt,
            new_shift_sample, new_wkv_sample, new_s5_re_sample, new_s5_im_sample)


_drawn_inputs = setup_inputs


def setup_inputs(seed=0):
    import zlib

    import numpy as np

    out = dict(_drawn_inputs(seed))
    spreads = {}
    factors = {'g_ffn1': 4.413,
     'lnx_w': 52.516,
     'lnx_b': 200.0,
     'g_ffn2': 7.786,
     'g_final': 20.267,
     'r_k': 4.571,
     'C_re': 4.347,
     'C_im': 4.018,
     'w_glu': 3.821}
    for name, (base, spread) in spreads.items():
        noise = np.random.default_rng([zlib.crc32(name.encode()), seed]).standard_normal(out[name].shape)
        drawn = base * np.exp(spread * noise) if base else spread * noise
        out[name] = __import__('jax').numpy.asarray(drawn.astype(out[name].dtype))
    for name, factor in factors.items():
        out[name] = (out[name] * factor).astype(out[name].dtype)
    return out
```

```python
import concourse.bass as bass
from concourse import mybir
import numpy as np

F32 = mybir.dt.float32
F32R = mybir.dt.float32r
I32 = mybir.dt.int32
ALU = mybir.AluOpType
ACT = mybir.ActivationFunctionType
AXX = mybir.AxisListType.X

P = 128
D = 1024
SEQ = 1024
NB = 8
TOK = SEQ + NB
DT = D // P
NBLK = 3
BLK = TOK // NBLK
FT = 2816 // P
FFN_GROUPS = (6, 6, 5, 5)
W = 512
WT = W // P
H = 8
N = 64
RT = 14
UT = 4
CH = 128
NCH = SEQ // CH
J = 16
SS = 86
NSS = TOK // SS
NORM_EPS = 1e-6
LNX_EPS = 64e-5
DECAY = float(np.exp(-0.5))

V_G1, V_GMIX, V_G2, V_GF = 0, 8, 16, 24
V_MU = 32
V_W0, V_A0, V_KK, V_KA, V_RK, V_DS = 46, 50, 54, 58, 62, 66
V_LR, V_LI, V_DT = 70, 86, 102
NVEC = 118

T_ID, T_STRICT, T_INCL, T_L0, T_L0T = 0, 1, 2, 3, 4
T_LEV = 5
T_SEG = 11
T_BLK = 12
T_IST = 13
NTAB = 14

WSLOTS = 2
RSQRT_MAGIC = float(0x5F3759DF)


class Ctx:
    pass


class Steps:

    def __init__(self, eng, sem, start=0):
        self.eng, self.sem, self.n, self.turn = eng, sem, start, 0

    def did(self, ins):
        ins.then_inc(self.sem, 1)
        self.n += 1
        return self.n

    def wait(self, n=None):
        self.eng.wait_ge(self.sem, self.turn + (self.n if n is None else n))

    def do(self, ins):
        self.did(ins)
        self.wait()

    def enter(self, i, per):
        self.first, self.per, self.turn = self.n, per, i * per

    def leave(self, turns):
        used = self.n - self.first
        assert used <= self.per, used
        if used < self.per:
            self.eng.sem_inc(self.sem, self.per - used)
        self.n, self.turn = self.first + self.per * turns, 0


def plan(nc, g):
    base = (nc.sbuf_base + 31) // 32 * 32
    g.limit = nc.sbuf_usable_end - base

    def at(name, off, shape, dt=F32):
        t = nc.alloc_sbuf_tensor_at(name, shape, dt, offset=base + off)
        return t, off + (int(np.prod(shape[1:])) * 4 + 31) // 32 * 32

    g.at = at
    o = 0
    g.wraw, o = at("wraw", o, [P, WSLOTS, 1024])
    g.whi, o = at("whi", o, [P, WSLOTS, 1024], F32R)
    g.wlo, o = at("wlo", o, [P, WSLOTS, 1024], F32R)
    g.vec, o = at("vec", o, [P, NVEC])
    g.ident, o = at("ident", o, [P, P])
    g.seg, o = at("seg", o, [P, P])
    g.small, o = at("small", o, [P, 6, 16])
    g.zero = g.small[:, 5, 0:1]
    g.hhi, o = at("hhi", o, [P, DT, TOK], F32R)
    g.hlo, o = at("hlo", o, [P, DT, TOK], F32R)
    g.h_end = o
    g.x, o = at("x", o, [P, DT, TOK])
    g.x_end = o
    ga = max(FFN_GROUPS)
    g.ahi, o = at("ahi", o, [P, ga, TOK], F32R)
    g.alo, o = at("alo", o, [P, ga, TOK], F32R)
    g.tmp, o = at("tmp", o, [P, 2, TOK])
    g.ssum, o = at("ssum", o, [P, TOK])
    assert o <= g.limit, (o, g.limit)
    g.ps = nc.alloc_psum_tensor("ps", [P, 8, 512], F32)

    S = nc.alloc_semaphore
    g.w_in = [S("weights_in0"), S("weights_in1")]
    g.w_hi = S("weights_hi")
    g.zero_set = S("zero_set")
    g.w_split = S("weights_split")
    g.unit_done = S("unit_done")
    g.set_free = [S("set_free0"), S("set_free1")]
    g.dve_s, g.act_s, g.pool_s = S("dve_steps"), S("act_steps"), S("pool_steps")
    g.x_in, g.c_in, g.out_done = S("x_in"), S("consts_in"), S("out_done")
    g.sq_ready, g.ssum_step, g.norm_ss = S("squares_ready"), S("square_sums"), S("norm_sums")
    g.rstd_ready, g.rstd_b = S("rstd_ready"), S("rstd_broadcast")
    g.hf_ready, g.hhi_ready, g.h_ready = S("h_full"), S("h_hi"), S("h_ready")
    g.silu_done, g.a_ready = S("silu_done"), S("a_ready")
    g.dve_n = g.act_n = g.pool_n = 0
    g.units = 0
    g.uses = [0, 0]
    g.norms = 0
    g.a_tiles = 0


def load_units(eng, g, u0, turns, per, kt, src):
    with eng.Fori(0, turns) as i:
        for j in range(per):
            eng.wait_ge(g.w_split, i * per + (u0 + j + 1))
            eng.dma_start(g.wraw[:, j % 2, 0:kt * P], src(i, j)).then_inc(g.w_in[j % 2], 16)


def split_units(pool, g, u0, turns, per, kt):
    n = kt * P
    with pool.Fori(0, turns) as i:
        for j in range(per):
            s = j % 2
            pool.wait_ge(g.w_in[s], i * (16 * per // 2) + 16 * ((u0 + j) // 2 + 1))
            pool.wait_ge(g.unit_done, i * per + (u0 + j + 1))
            pool.tensor_tensor(g.whi[:, s, 0:n], g.wraw[:, s, 0:n], g.zero.to_broadcast([P, n]),
                               ALU.add).then_inc(g.w_hi, 1)
            pool.wait_ge(g.w_hi, i * per + (u0 + j + 1))
            pool.tensor_tensor(g.wlo[:, s, 0:n], g.wraw[:, s, 0:n], g.whi[:, s, 0:n].bitcast(F32),
                               ALU.subtract).then_inc(g.w_split, 1)


def product(pe, g, i, per, u, kt, bank_set, use, uses_per, xhi, xlo, k_wait=None):
    s = u % 2
    pe.wait_ge(g.w_split, i * per + (u + 1 + WSLOTS))
    pe.wait_ge(g.set_free[bank_set], i * uses_per + (use + 1))
    for k in range(kt):
        if k_wait:
            pe.wait_ge(k_wait[0], k_wait[1](i, k))
        for w, x, first in ((g.whi, xhi, True), (g.whi, xlo, False), (g.wlo, xhi, False)):
            for b in range(NBLK):
                last = pe.matmul(g.ps[:, 3 * bank_set + b, 0:BLK], w[:, s, k * P:(k + 1) * P],
                                 x(k, b), start=(k == 0 and first),
                                 stop=(k == kt - 1 and w is g.wlo))
    last.then_inc(g.unit_done, 1)


def acc(g, bank_set):
    return g.ps[:, 3 * bank_set:3 * bank_set + 3, 0:BLK]


def blocks(ap):
    return ap.rearrange("p (b t) -> p b t", b=NBLK)


def rsqrt(v, st, y, x, t, scale, eps, floor=None):
    if floor is None:
        st.do(v.tensor_scalar(x, x, scale, eps, ALU.mult, ALU.add))
    else:
        st.do(v.tensor_scalar(x, x, scale, floor, ALU.mult, ALU.max))
    st.do(v.tensor_scalar(t.bitcast(I32), x.bitcast(I32), 1, None, ALU.logical_shift_right))
    st.do(v.tensor_scalar(y.bitcast(I32), t.bitcast(I32), -1.0, RSQRT_MAGIC, ALU.mult, ALU.add))
    for _ in range(4):
        st.do(v.scalar_tensor_tensor(t, y, -0.5, y, ALU.mult, ALU.mult))
        st.do(v.tensor_tensor(t, t, x, ALU.mult))
        st.do(v.scalar_tensor_tensor(y, t, 1.5, y, ALU.add, ALU.mult))


def norm_act(act, g, n):
    for k in range(DT):
        if k >= 2:
            act.wait_ge(g.ssum_step, DT * n + k - 1)
        act.activation(g.tmp[:, k % 2, :], g.x[:, k, :], ACT.Square).then_inc(g.sq_ready, 1)


def norm_pe(pe, g, n, use):
    pe.wait_ge(g.ssum_step, DT * (n + 1))
    pe.wait_ge(g.set_free[0], use + 1)
    for j in range(NSS):
        last = pe.matmul(g.ps[0:SS, 6, j:j + 1], g.ssum[:, j * SS:(j + 1) * SS], g.seg[:, 2:3],
                         start=True, stop=True)
    last.then_inc(g.norm_ss, 1)
    pe.wait_ge(g.rstd_ready, n + 1)
    for j in range(NSS):
        last = pe.matmul(g.ps[:, j // 4, (j % 4) * SS:(j % 4 + 1) * SS],
                         g.small[0:SS, 1, j:j + 1].to_broadcast([SS, P]), g.ident[0:SS, 0:SS],
                         start=True, stop=True)
    last.then_inc(g.rstd_b, 1)


def norm_dve(v, g, st, n):
    for k in range(DT):
        v.wait_ge(g.sq_ready, DT * n + k + 1)
        if k == 0:
            v.tensor_copy(g.ssum[:, :], g.tmp[:, 0, :]).then_inc(g.ssum_step, 1)
        else:
            v.wait_ge(g.ssum_step, DT * n + k)
            v.tensor_tensor(g.ssum[:, :], g.ssum[:, :], g.tmp[:, k % 2, :], ALU.add)\
                .then_inc(g.ssum_step, 1)
    v.wait_ge(g.norm_ss, n + 1)
    x, y, t = (g.small[0:SS, a, 0:NSS] for a in range(3))
    st.do(v.tensor_copy(x, g.ps[0:SS, 6, 0:NSS]))
    rsqrt(v, st, y, x, t, 1.0 / D, NORM_EPS)
    v.sem_inc(g.rstd_ready, 1)
    v.wait_ge(g.rstd_b, n + 1)


def h_dve(v, g, gcol, n):

    def low(k):
        v.wait_ge(g.hhi_ready, DT * n + k + 1)
        v.tensor_tensor(g.hlo[:, k, :], g.tmp[:, k % 2, :], g.hhi[:, k, :].bitcast(F32),
                        ALU.subtract).then_inc(g.h_ready, 1)

    for k in range(DT):
        if k >= 2:
            v.wait_ge(g.h_ready, DT * n + k - 1)
        ins = v.scalar_tensor_tensor(blocks(g.tmp[:, k % 2, :]), blocks(g.x[:, k, :]),
                                     g.vec[:, gcol + k:gcol + k + 1], acc(g, 0), ALU.mult, ALU.mult)
        ins.then_inc(g.hf_ready, 1)
        v.wait_ge(g.hf_ready, DT * n + k + 1)
        if k == DT - 1:
            v.sem_inc(g.set_free[0], 1)
        if k:
            low(k - 1)
    low(DT - 1)


def h_act(act, g, n):
    for k in range(DT):
        act.wait_ge(g.hf_ready, DT * n + k + 1)
        act.activation(g.hhi[:, k, :], g.tmp[:, k % 2, :], ACT.Copy).then_inc(g.hhi_ready, 1)


def ffn_block(nc, g, w_up, w_down, gcol, before=None, after=None):
    u0, s0, a0, n0 = g.units, list(g.uses), g.a_tiles, g.norms
    s0[0] += 1

    def groups():
        u, a, k0, use = u0, a0, 0, s0[0]
        use1 = s0[1]
        for size in FFN_GROUPS:
            yield size, k0, u, a, use, use1
            u, a, k0 = u + 2 * size + DT, a + size, k0 + size
            use, use1 = use + size + DT // 2, use1 + size + DT // 2

    with nc.Block() as block:
        @block.sync
        def _(sp):
            if before:
                before["sync"](sp)
            for size, k0, u, a, use, use1 in groups():
                load_units(sp, g, u, size, 2, DT,
                           lambda i, j: w_up[bass.ds(i * 2 + (2 * k0 + j), 1), :, :].rearrange("a p k -> p (a k)"))
                load_units(sp, g, u + 2 * size, DT // 2, 2, size,
                           lambda i, j: w_down[bass.ds(i * 2 + j, 1), :, k0 * P:(k0 + size) * P].rearrange("a p k -> p (a k)"))
            if after:
                after["sync"](sp)

        @block.gpsimd
        def _(pool):
            if before:
                pool.sem_inc(g.w_split, WSLOTS)
                pool.memset(g.zero, 0.0).then_inc(g.zero_set, 1)
                pool.wait_ge(g.zero_set, 1)
            for size, k0, u, a, use, use1 in groups():
                split_units(pool, g, u, size, 2, DT)
                split_units(pool, g, u + 2 * size, DT // 2, 2, size)

        @block.scalar
        def _(act):
            if before:
                before["scalar"](act)
            norm_act(act, g, n0)
            h_act(act, g, n0)
            for size, k0, u, a, use, use1 in groups():
                with act.Fori(0, size) as i:
                    act.wait_ge(g.unit_done, i * 2 + (u + 1 + WSLOTS))
                    act.wait_ge(g.set_free[1], i + (use1 + 1))
                    act.activation(blocks(g.tmp[:, 0, :]), acc(g, 0), ACT.Silu)\
                       .then_inc(g.set_free[0], 1)
            if after:
                after["scalar"](act)

        @block.vector
        def _(v):
            st = Steps(v, g.dve_s, g.dve_n)
            norm_dve(v, g, st, n0)
            h_dve(v, g, gcol, n0)
            for size, k0, u, a, use, use1 in groups():
                with v.Fori(0, size) as i:
                    v.wait_ge(g.set_free[0], i + (use + 2))
                    v.wait_ge(g.unit_done, i * 2 + (u + 2 + WSLOTS))
                    v.tensor_tensor(blocks(g.tmp[:, 1, :]), acc(g, 1), blocks(g.tmp[:, 0, :]),
                                    ALU.mult).then_inc(g.set_free[1], 1)
                    v.wait_ge(g.set_free[1], i + (use1 + 2))
                    st.enter(i, 1)
                    st.do(v.tensor_copy(g.ahi[:, bass.ds(i, 1), :], g.tmp[:, 1:2, :]))
                    v.tensor_tensor(g.alo[:, bass.ds(i, 1), :], g.tmp[:, 1:2, :],
                                    g.ahi[:, bass.ds(i, 1), :].bitcast(F32),
                                    ALU.subtract).then_inc(g.a_ready, 1)
                    v.wait_ge(g.a_ready, i + (a + 1))
                st.leave(size)
                ud = u + 2 * size
                with v.Fori(0, DT // 2) as i:
                    for j in range(2):
                        v.wait_ge(g.unit_done, i * 2 + (ud + j + 1 + WSLOTS))
                        xt = g.x[:, bass.ds(i * 2 + j, 1), :].rearrange("p a (b t) -> p (a b) t", b=NBLK)
                        v.scalar_tensor_tensor(xt, acc(g, j), 0.5, xt, ALU.mult, ALU.add)\
                            .then_inc(g.set_free[j], 1)
            if after:
                after["vector"](v, st)
            g.dve_end = st.n

        @block.tensor
        def _(pe):
            if before:
                pe.sem_inc(g.unit_done, WSLOTS)
                pe.sem_inc(g.set_free[0], 1)
                pe.sem_inc(g.set_free[1], 1)
                pe.wait_ge(g.c_in, 16 * 3)
            norm_pe(pe, g, n0, s0[0] - 1)
            for size, k0, u, a, use, use1 in groups():
                with pe.Fori(0, size) as i:
                    for j in range(2):
                        product(pe, g, i, 2, u + j, DT, j, (use, use1)[j], 1,
                                lambda k, b: g.hhi[:, k, b * BLK:(b + 1) * BLK],
                                lambda k, b: g.hlo[:, k, b * BLK:(b + 1) * BLK],
                                (g.h_ready, lambda i, k: DT * n0 + k + 1) if k0 == 0 else None)
                with pe.Fori(0, DT // 2) as i:
                    for j in range(2):
                        product(pe, g, i, 2, u + 2 * size + j, size, j, (use, use1)[j] + size, 1,
                                lambda k, b: g.ahi[:, k, b * BLK:(b + 1) * BLK],
                                lambda k, b: g.alo[:, k, b * BLK:(b + 1) * BLK],
                                (g.a_ready, lambda i, k: a + k + 1))
            if after:
                after["tensor"](pe)

    g.units = u0 + 2 * FT + len(FFN_GROUPS) * DT
    g.uses = [s0[0] + FT + len(FFN_GROUPS) * DT // 2, s0[1] + FT + len(FFN_GROUPS) * DT // 2]
    g.a_tiles, g.norms, g.dve_n = a0 + FT, n0 + 1, g.dve_end


def plan_mid(nc, g):
    g.u = g.at("u", g.limit // 32 * 32 - UT * TOK * 4, [P, UT, TOK])[0]
    g.u_off = g.limit // 32 * 32 - UT * TOK * 4
    o = g.x_end
    g.raw, o = g.at("fraw", o, [P, 2, TOK + 8])
    g.mix, o = g.at("fmix", o, [P, 2, TOK])
    g.shift, o = g.at("shift", o, [P, RT, NB])
    g.last, o = g.at("last", o, [P, RT, NB + 1])
    assert o <= g.u_off
    S = nc.alloc_semaphore
    g.sh_in, g.raw_ready, g.mix_ready, g.mix_out = S("shift_in"), S("raw_ready"), S("mix_ready"), [S("mix_out0"), S("mix_out1")]
    g.diff_ready, g.last_ready, g.x_out, g.last_out = S("diff_ready"), S("last_ready"), S("x_out"), S("last_out")
    g.zero_ready = S("zero_ready")
    g.ucopy = S("u_ready")


def proj_block(nc, g, w_in, shift, f_dram, x_dram, last_out):
    u0, n0 = g.units, g.norms
    use = [g.uses[0] + 1, g.uses[1]]
    HALF = RT // 2

    with nc.Block() as block:
        @block.sync
        def _(sp):
            sp.dma_start(g.shift[:, :, :], shift).then_inc(g.sh_in, 16)
            load_units(sp, g, u0, HALF + UT // 2, 2, DT,
                       lambda i, j: w_in[bass.ds(i * 2 + j, 1), :, :].rearrange("a p k -> p (a k)"))
            sp.wait_ge(g.last_ready, RT)
            sp.dma_start(last_out, g.last[:, :, :]).then_inc(g.last_out, 16)
            sp.wait_ge(g.last_out, 16)
            sp.wait_ge(g.x_out, 16)
            for j in range(2):
                sp.wait_ge(g.mix_out[j], 16 * (HALF + 1))

        @block.gpsimd
        def _(pool):
            split_units(pool, g, u0, HALF + UT // 2, 2, DT)

        @block.scalar
        def _(act):
            act.dma_start(x_dram, g.x[:, :, :]).then_inc(g.x_out, 16)
            act.sem_inc(g.mix_out[0], 16)
            act.sem_inc(g.mix_out[1], 16)
            norm_act(act, g, n0)
            h_act(act, g, n0)
            act.wait_ge(g.zero_ready, 2)
            act.wait_ge(g.h_ready, DT * (n0 + 1))
            with act.Fori(0, HALF) as i:
                for j in range(2):
                    act.wait_ge(g.unit_done, i * 2 + (u0 + j + 1 + WSLOTS))
                    act.wait_ge(g.mix_ready, i * 2 + (j + 1))
                    act.activation(blocks(g.raw[:, j, 8:8 + TOK]), acc(g, j), ACT.Copy)\
                       .then_inc(g.set_free[j], 1)
                    act.wait_ge(g.set_free[j], i + (use[j] + 2))
                    act.activation(g.last[:, bass.ds(i * 2 + j, 1), :],
                                   g.raw[:, j:j + 1, 7 + SEQ:8 + TOK], ACT.Copy).then_inc(g.last_ready, 1)
                    act.wait_ge(g.mix_ready, i * 2 + (j + 3))
                    act.dma_start(f_dram[bass.ds(i * 2 + j, 1), :, :].rearrange("a p k -> p (a k)"),
                                  g.mix[:, j, :]).then_inc(g.mix_out[j], 16)
            for n in range(UT):
                j = n % 2
                act.wait_ge(g.unit_done, u0 + RT + n + 1 + WSLOTS)
                act.activation(blocks(g.u[:, n, :]), acc(g, j), ACT.Copy).then_inc(g.set_free[j], 1)

        @block.vector
        def _(v):
            st = Steps(v, g.dve_s, g.dve_n)
            for j in range(2):
                v.memset(g.raw[:, j, 7:8], 0.0).then_inc(g.zero_ready, 1)
            norm_dve(v, g, st, n0)
            h_dve(v, g, V_GMIX, n0)
            v.sem_inc(g.mix_ready, 2)
            v.wait_ge(g.sh_in, 16)
            with v.Fori(0, HALF) as i:
                for j in range(2):
                    r = g.raw[:, j, :]
                    v.wait_ge(g.set_free[j], i + (use[j] + 2))
                    v.wait_ge(g.last_ready, i * 2 + (j + 1))
                    v.wait_ge(g.mix_out[j], i * 16 + 16)
                    v.tensor_tensor(g.mix[:, j, 0:SEQ], r[:, 7:7 + SEQ], r[:, 8:8 + SEQ],
                                    ALU.subtract).then_inc(g.diff_ready, 1)
                    v.tensor_tensor(g.mix[:, j:j + 1, SEQ:TOK], g.shift[:, bass.ds(i * 2 + j, 1), :],
                                    g.raw[:, j:j + 1, 8 + SEQ:8 + TOK], ALU.subtract).then_inc(g.diff_ready, 1)
                    v.wait_ge(g.diff_ready, i * 4 + (2 * j + 2))
                    v.scalar_tensor_tensor(g.mix[:, j, :], g.mix[:, j, :],
                                           g.vec[:, bass.ds(i * 2 + (V_MU + j), 1)],
                                           r[:, 8:8 + TOK], ALU.mult, ALU.add).then_inc(g.mix_ready, 1)
            g.dve_end = st.n

        @block.tensor
        def _(pe):
            norm_pe(pe, g, n0, use[0] - 1)
            with pe.Fori(0, HALF + UT // 2) as i:
                for j in range(2):
                    product(pe, g, i, 2, u0 + j, DT, j, use[j], 1,
                            lambda k, b: g.hhi[:, k, b * BLK:(b + 1) * BLK],
                            lambda k, b: g.hlo[:, k, b * BLK:(b + 1) * BLK],
                            (g.h_ready, lambda i, k: DT * n0 + k + 1))

    g.units, g.norms, g.dve_n = u0 + RT + UT, n0 + 1, g.dve_end
    g.uses = [use[0] + HALF + UT // 2, use[1] + HALF + UT // 2]


def gate_products(pe, g, i):
    u, m = g.units, g.gates * NBLK
    pe.wait_ge(g.w_split, i * 2 + (u + 2 + WSLOTS))
    for b in range(NBLK):
        pe.wait_ge(g.gate_free, i * NBLK + (m + b + (2, 1, 1)[b]))
        for k in range(DT):
            s, kk = k // 4, k % 4
            for w, x in ((g.whi, g.hhi), (g.whi, g.hlo), (g.wlo, g.hhi)):
                last = pe.matmul(g.ps[:, b % 2, 0:BLK], w[:, s, kk * P:(kk + 1) * P],
                                 x[:, k, b * BLK:(b + 1) * BLK],
                                 start=(k == 0 and w is g.whi and x is g.hhi),
                                 stop=(k == DT - 1 and w is g.wlo))
                if k < DT - 1 or w is g.whi:
                    yield
        last.then_inc(g.gate_done, 1)
        yield
    pe.wait_ge(g.gate_done, i * NBLK + (m + NBLK))
    pe.sem_inc(g.unit_done, 2)


def run(ops, n):
    for _ in range(n):
        next(ops, None)


def gate_take(act, g, i, b):
    m = g.gates * NBLK
    if b == 0:
        act.wait_ge(g.gate_out, i * 16 + (g.gates + 1) * 16)
    act.wait_ge(g.gate_done, i * NBLK + (m + b + 1))
    act.activation(g.gout[:, b * BLK:(b + 1) * BLK], g.ps[:, b % 2, 0:BLK], ACT.Tanh, scale=0.5)\
       .then_inc(g.gate_free, 1)


def gate_stream(sp, g, w_gate, gate_dram):
    u, m = g.units, g.gates * NBLK
    with sp.Fori(0, NCH) as i:
        for j in range(2):
            sp.wait_ge(g.w_split, i * 2 + (u + j + 1))
            sp.dma_start(g.wraw[:, j, 0:4 * P],
                         w_gate[bass.ds(i + g.gates, 1), :, j * 4 * P:(j + 1) * 4 * P].rearrange("a p k -> p (a k)"))\
              .then_inc(g.w_in[j], 16)
        sp.wait_ge(g.gate_free, i * NBLK + (m + NBLK + 2))
        sp.dma_start(gate_dram[bass.ds(i + g.gates, 1), :, :].rearrange("a p k -> p (a k)"), g.gout[:, :])\
          .then_inc(g.gate_out, 16)


def gates_done(g):
    g.units += 2 * NCH
    g.gates += NCH


def plan_s5(nc, g):
    o = g.x_off = g.h_end
    g.s5c, o = g.at("s5_cos", o, [P, J, CH])
    g.s5s, o = g.at("s5_sin", o, [P, J, CH])
    g.BT = []
    g.CT = []
    for n in range(2):
        t, o = g.at(f"s5_b{n}", o, [P, J, P]); g.BT.append(t)
    for n in range(2):
        t, o = g.at(f"s5_c{n}", o, [P, J, 32]); g.CT.append(t)
    g.rot, o = g.at("s5_rot", o, [P, 4, 4, 4, CH])
    g.z, o = g.at("s5_z", o, [P, 2, 2, 4, CH])
    g.xs, o = g.at("s5_x", o, [P, 2, 2, 4, CH])
    g.uc, o = g.at("s5_u", o, [P, UT, CH])
    g.gout, o = g.at("gate_out_s", o, [P, TOK])
    g.xl, o = g.at("s5_last", o, [P, 2, J])
    g.par, o = g.at("s5_par", o, [P, 12, J])
    assert o <= g.u_off, (o, g.u_off)
    off = g.x_off + 2 * J * CH * 4 + 2 * J * P * 4 + 2 * J * 32 * 4
    g.braw, off = g.at("b_raw", off, [P, 2, J, 16])
    g.bbar, off = g.at("b_bar", off, [P, 2, J, 16])
    g.bm, off = g.at("b_masked", off, [P, 2, J, 32])
    g.craw, off = g.at("c_raw", off, [P, 2, J, 16])
    g.stm, off = g.at("s5_tmp", off, [P, 4, J, P // 2])
    g.x0, off = g.at("s5_x0", g.x_off + 2 * J * CH * 4 + 2 * J * P * 4 + 2 * J * 32 * 4, [P, 2, J, NB])
    g.x1, off = g.at("s5_x1", off, [P, 2, J, NB])
    g.xt, off = g.at("s5_xt", off, [P, 2, J, NB])
    S = nc.alloc_semaphore
    g.gate_free, g.gate_done, g.gate_out = S("gate_free"), S("gate_done"), S("gate_out")
    g.s5_in, g.s5_fwd, g.s5_tr, g.s5_bt = S("s5_in"), S("s5_bbar"), S("s5_transposed"), S("s5_set_up")
    g.uc_ready, g.bu_done, g.bu_free = S("s5_u_ready"), S("s5_bu_done"), S("s5_bu_free")
    g.rin, g.w_ready, g.z_ready, g.xc_ready, g.c_done = (S("s5_turned"), S("s5_w"), S("s5_z_ready"),
                                                         S("s5_x_ready"), S("s5_c_done"))
    g.y_free, g.x0_in, g.xs_ready, g.s5_out = S("s5_y_taken"), S("s5_x0_in"), S("s5_xs"), S("s5_out")
    g.s5_zero = S("s5_zero")
    g.gates = 0


def s5_exp(v, st, y, x, a, b):
    st.do(v.tensor_scalar(a, x, float(1 / np.log(2)), None, ALU.mult))
    st.do(v.tensor_scalar(a, a, 12582912.0, None, ALU.add))
    st.do(v.tensor_scalar(a, a, -12582912.0, None, ALU.add))
    st.do(v.scalar_tensor_tensor(b, a, -0.693359375, x, ALU.mult, ALU.add))
    st.do(v.scalar_tensor_tensor(b, a, 2.12194440e-4, b, ALU.mult, ALU.add))
    st.do(v.tensor_scalar(y, b, 1.0 / 9, 1.0, ALU.mult, ALU.add))
    for n in range(8, 0, -1):
        st.do(v.scalar_tensor_tensor(y, y, 1.0 / n, b, ALU.mult, ALU.mult))
        st.do(v.tensor_scalar(y, y, 1.0, None, ALU.add))
    st.do(v.tensor_scalar(b.bitcast(I32), a, float(1 << 23), float(127 << 23), ALU.mult, ALU.add))
    st.do(v.tensor_tensor(y, y, b, ALU.mult))


def s5_sincos(v, st, s, c, x, a, b):
    st.do(v.tensor_scalar(a, x, float(1 / (2 * np.pi)), None, ALU.mult))
    st.do(v.tensor_scalar(a, a, 12582912.0, None, ALU.add))
    st.do(v.tensor_scalar(a, a, -12582912.0, None, ALU.add))
    c1 = 6.28125
    c2 = float(np.float32(np.round((2 * np.pi - c1) * 2 ** 20) / 2 ** 20))
    c3 = float(2 * np.pi - c1 - c2)
    st.do(v.scalar_tensor_tensor(b, a, -c1, x, ALU.mult, ALU.add))
    st.do(v.scalar_tensor_tensor(b, a, -c2, b, ALU.mult, ALU.add))
    st.do(v.scalar_tensor_tensor(b, a, -c3, b, ALU.mult, ALU.add))
    st.do(v.tensor_scalar(b, b, 0.25, None, ALU.mult))
    st.do(v.tensor_tensor(a, b, b, ALU.mult))
    for y, divs in ((s, (110, 72, 42, 20, 6)), (c, (90, 56, 30, 12, 2))):
        st.do(v.tensor_scalar(y, a, -1.0 / divs[0], 1.0, ALU.mult, ALU.add))
        for n in divs[1:]:
            st.do(v.scalar_tensor_tensor(y, y, -1.0 / n, a, ALU.mult, ALU.mult))
            st.do(v.tensor_scalar(y, y, 1.0, None, ALU.add))
    st.do(v.tensor_tensor(s, s, b, ALU.mult))
    for _ in range(2):
        st.do(v.tensor_tensor(b, s, s, ALU.mult))
        st.do(v.scalar_tensor_tensor(s, s, 2.0, c, ALU.mult, ALU.mult))
        st.do(v.tensor_scalar(c, b, -2.0, 1.0, ALU.mult, ALU.add))


def cmul(v, st, outr, outi, ar, ai, br, bi, t0, t1):
    st.do(v.tensor_tensor(t0, ar, br, ALU.mult))
    st.do(v.tensor_tensor(t1, ai, bi, ALU.mult))
    st.do(v.tensor_tensor(outr, t0, t1, ALU.subtract))
    st.do(v.tensor_tensor(t0, ar, bi, ALU.mult))
    st.do(v.tensor_tensor(t1, ai, br, ALU.mult))
    st.do(v.tensor_tensor(outi, t0, t1, ALU.add))


def s5_setup_dve(v, g, st):
    par = [g.par[:, n, :] for n in range(12)]
    dt, m, th, s, c, a, b, abr, abi, qr, qi, den = par
    lr, li, ldt = (g.vec[:, o:o + J] for o in (V_LR, V_LI, V_DT))
    s5_exp(v, st, dt, ldt, a, b)
    st.do(v.tensor_tensor(th, li, dt, ALU.mult))
    st.do(v.tensor_tensor(den, lr, dt, ALU.mult))
    s5_exp(v, st, m, den, a, b)
    s5_sincos(v, st, s, c, th, a, b)
    st.do(v.tensor_tensor(abr, m, c, ALU.mult))
    st.do(v.tensor_tensor(abi, m, s, ALU.mult))
    st.do(v.tensor_tensor(den, lr, lr, ALU.mult))
    st.do(v.tensor_tensor(a, li, li, ALU.mult))
    st.do(v.tensor_tensor(den, den, a, ALU.add))
    st.do(v.reciprocal(den, den))
    st.do(v.tensor_scalar(a, abr, -1.0, None, ALU.add))
    st.do(v.tensor_tensor(qr, a, lr, ALU.mult))
    st.do(v.tensor_tensor(b, abi, li, ALU.mult))
    st.do(v.tensor_tensor(qr, qr, b, ALU.add))
    st.do(v.tensor_tensor(qr, qr, den, ALU.mult))
    st.do(v.tensor_tensor(qi, abi, lr, ALU.mult))
    st.do(v.tensor_tensor(b, a, li, ALU.mult))
    st.do(v.tensor_tensor(qi, qi, b, ALU.subtract))
    st.do(v.tensor_tensor(qi, qi, den, ALU.mult))
    v.wait_ge(g.s5_in, 16 * 2)
    full = lambda x: x.unsqueeze(2).to_broadcast([P, J, 16])
    cmul(v, st, g.bbar[:, 0], g.bbar[:, 1], full(qr), full(qi), g.braw[:, 0], g.braw[:, 1],
         g.stm[:, 0, :, 0:16], g.stm[:, 1, :, 0:16])
    st.do(v.memset(g.bm[:, :, :, :], 0.0))
    for n in range(2):
        st.do(v.memset(g.BT[n][:, :, :], 0.0))
        st.do(v.memset(g.CT[n][:, :, :], 0.0))
        for q in range(2):
            rows = slice(64 * q, 64 * q + 64)
            st.do(v.tensor_copy(g.bm[rows, n, :, 16 * q:16 * q + 16], g.bbar[rows, n]))
            st.do(v.tensor_scalar(g.CT[n][rows, :, 16 * q:16 * q + 16], g.craw[rows, n], 1.0 - 2 * n, None, ALU.mult))
    v.sem_inc(g.s5_fwd, 1)
    st.do(v.tensor_copy(g.s5c[:, :, 0:1], c.unsqueeze(2)))
    st.do(v.tensor_copy(g.s5s[:, :, 0:1], s.unsqueeze(2)))
    n = 1
    while n < CH:
        er, ei = (t[:, :, n - 1:n].to_broadcast([P, J, n]) for t in (g.s5c, g.s5s))
        cmul(v, st, g.s5c[:, :, n:2 * n], g.s5s[:, :, n:2 * n], g.s5c[:, :, 0:n], g.s5s[:, :, 0:n],
             er, ei, g.stm[:, 0, :, 0:n], g.stm[:, 1, :, 0:n])
        n *= 2
    v.wait_ge(g.s5_tr, 1)
    for n in range(2):
        for q in range(4):
            rows = slice(32 * q, 32 * q + 32)
            st.do(v.tensor_copy(g.BT[n][rows, q:J:4, :],
                                g.ps[rows, 2 + n, :].rearrange("p (t c) -> p t c", t=4)))
    st.do(v.memset(g.xl[:, :, :], 0.0))
    v.sem_inc(g.s5_bt, 1)


def s5_block(nc, g, w_gate, gate_dram, b_in, c_in, x0_in, s5p_out, s5s_out):
    per_x = UT

    with nc.Block() as block:
        @block.sync
        def _(sp):
            sp.dma_start(g.braw[:, :, :, :], b_in).then_inc(g.s5_in, 16)
            sp.dma_start(g.craw[:, :, :, :], c_in).then_inc(g.s5_in, 16)
            gate_stream(sp, g, w_gate, gate_dram)
            sp.wait_ge(g.xc_ready, UT * NCH + 2)
            sp.dma_start(g.x0[:, :, :, :], x0_in).then_inc(g.x0_in, 16)
            sp.dma_start(s5p_out, g.xl[:, :, :]).then_inc(g.s5_out, 16)
            sp.wait_ge(g.xs_ready, 1)
            sp.dma_start(s5s_out, g.x1[:, :, :, :]).then_inc(g.s5_out, 16)
            sp.wait_ge(g.s5_out, 32)
            sp.wait_ge(g.gate_out, 16 * (g.gates + NCH + 1))

        @block.gpsimd
        def _(pool):
            st = Steps(pool, g.pool_s, g.pool_n)

            def w_piece(i, p):
                t = [g.rot[:, p, n].rearrange("p a c -> p (a c)") for n in range(4)]
                z = [g.z[:, n, p % 2].rearrange("p a c -> p (a c)") for n in range(2)]
                pool.wait_ge(g.rin, i * 4 + (p + 1))
                pool.wait_ge(g.xc_ready, i * 4 + (p + 1))
                st.do(pool.tensor_tensor(z[0], t[0], t[1], ALU.add))
                pool.tensor_tensor(z[1], t[2], t[3], ALU.subtract).then_inc(g.w_ready, 1)

            def x_piece(i, p):
                t = [g.rot[:, p, n].rearrange("p a c -> p (a c)") for n in range(4)]
                z = [g.z[:, n, p % 2].rearrange("p a c -> p (a c)") for n in range(2)]
                x = [g.xs[:, n, p % 2].rearrange("p a c -> p (a c)") for n in range(2)]
                cos, sin = (t_[:, 4 * p:4 * p + 4, :].rearrange("p a c -> p (a c)") for t_ in (g.s5c, g.s5s))
                pool.wait_ge(g.z_ready, i * 4 + (p + 1))
                st.do(pool.tensor_tensor(t[1], sin, z[1], ALU.mult))
                st.do(pool.tensor_tensor(t[3], cos, z[1], ALU.mult))
                pool.wait_ge(g.c_done, i * 4 + (p + 1))
                st.do(pool.tensor_tensor(x[0], t[0], t[1], ALU.subtract))
                st.do(pool.tensor_tensor(x[1], t[2], t[3], ALU.add))
                pool.tensor_tensor(g.xl[:, :, 4 * p:4 * p + 4], g.xs[:, :, p % 2, :, CH - 1],
                                   g.zero.unsqueeze(2).to_broadcast([P, 2, 4]), ALU.add)\
                    .then_inc(g.xc_ready, 1)

            pool.sem_inc(g.xc_ready, 2)
            pool.wait_ge(g.s5_bt, 1)
            u0 = g.units
            w_piece(0, 0)
            w_piece(0, 1)

            def turn(i, more):
                split_turn(pool, g, i, u0, 4)
                x_piece(i, 0)
                w_piece(i, 2)
                x_piece(i, 1)
                w_piece(i, 3)
                x_piece(i, 2)
                if more:
                    w_piece(i + 1, 0)
                x_piece(i, 3)
                if more:
                    w_piece(i + 1, 1)

            with pool.Fori(0, NCH - 1) as i:
                st.enter(i, 24)
                turn(i, True)
                st.leave(NCH - 1)
            turn(NCH - 1, False)
            g.pool_end = st.n

        @block.scalar
        def _(act):
            act.sem_inc(g.gate_free, 2)
            act.sem_inc(g.gate_out, 16)
            act.wait_ge(g.s5_bt, 1)
            act.activation(g.uc[:, :, :], g.u[:, :, 0:CH], ACT.Copy).then_inc(g.uc_ready, 1)

            def turn(i, more):
                gate_take(act, g, i, 0)
                if more:
                    act.wait_ge(g.bu_done, i * 4 + 8)
                    act.activation(g.uc[:, :, :], g.u[:, :, bass.ds(i * CH + CH, CH)], ACT.Copy)\
                       .then_inc(g.uc_ready, 1)
                gate_take(act, g, i, 1)
                gate_take(act, g, i, 2)

            with act.Fori(0, NCH - 1) as i:
                turn(i, True)
            turn(NCH - 1, False)
            act.wait_ge(g.bu_done, NCH * 4 + 4)
            act.activation(g.uc[:, :, 0:NB], g.u[:, :, SEQ:TOK], ACT.Copy).then_inc(g.uc_ready, 1)

        @block.vector
        def _(v):
            st = Steps(v, g.dve_s, g.dve_n)
            s5_setup_dve(v, g, st)
            v.sem_inc(g.bu_free, 2)
            v.sem_inc(g.y_free, 1)

            def turn_in(i, p):
                t = [g.rot[:, p, n].rearrange("p a c -> p (a c)") for n in range(4)]
                cos, sin = (t_[:, 4 * p:4 * p + 4, :].rearrange("p a c -> p (a c)") for t_ in (g.s5c, g.s5s))
                br, bi = g.ps[:, 2 + 2 * (p % 2), :], g.ps[:, 3 + 2 * (p % 2), :]
                v.wait_ge(g.bu_done, i * 4 + (p + 5))
                if not isinstance(i, int) or i > 0:
                    v.wait_ge(g.xc_ready, i * 4 + (p - 1))
                st.do(v.tensor_tensor(t[0], cos, br, ALU.mult))
                st.do(v.tensor_tensor(t[1], sin, bi, ALU.mult))
                st.do(v.tensor_tensor(t[2], cos, bi, ALU.mult))
                st.do(v.tensor_tensor(t[3], sin, br, ALU.mult))
                v.sem_inc(g.bu_free, 1)
                v.sem_inc(g.rin, 1)

            def scans(i, p):
                t = [g.rot[:, p, n].rearrange("p a c -> p (a c)") for n in range(4)]
                cos, sin = (t_[:, 4 * p:4 * p + 4, :].rearrange("p a c -> p (a c)") for t_ in (g.s5c, g.s5s))
                v.wait_ge(g.w_ready, i * 4 + (p + 1))
                for n in range(2):
                    for a in range(4):
                        zt = g.z[:, n, p % 2, a, :]
                        st.did(v.tensor_tensor_scan(zt, g.par[:, 1, 4 * p + a:4 * p + a + 1].to_broadcast([P, CH]), zt,
                                                    g.xl[:, n, 4 * p + a:4 * p + a + 1], ALU.mult, ALU.add))
                st.wait()
                z0 = g.z[:, 0, p % 2].rearrange("p a c -> p (a c)")
                st.do(v.tensor_tensor(t[0], cos, z0, ALU.mult))
                st.do(v.tensor_tensor(t[2], sin, z0, ALU.mult))
                v.sem_inc(g.z_ready, 1)

            turn_in(0, 0)
            turn_in(0, 1)

            def turn(i, more):
                for p in range(4):
                    scans(i, p)
                    if p + 2 < 4:
                        turn_in(i, p + 2)
                    elif more:
                        turn_in(i + 1, p - 2)
                v.wait_ge(g.c_done, i * 4 + 6)
                for p in range(4):
                    uv = g.u[:, p:p + 1, bass.ds(i * CH, CH)]
                    st.did(v.scalar_tensor_tensor(uv, uv, g.vec[:, V_DS + p:V_DS + p + 1],
                                                  g.ps[:, 6:7, p * CH:(p + 1) * CH], ALU.mult, ALU.add))
                st.wait()
                v.sem_inc(g.y_free, 1)

            with v.Fori(0, NCH - 1) as i:
                st.enter(i, 64)
                turn(i, True)
                st.leave(NCH - 1)
            turn(NCH - 1, False)
            abr, abi = (g.par[:, n, :].unsqueeze(2).to_broadcast([P, J, NB]) for n in (7, 8))
            v.wait_ge(g.x0_in, 16)
            cmul(v, st, g.x1[:, 0], g.x1[:, 1], abr, abi, g.x0[:, 0], g.x0[:, 1], g.xt[:, 0], g.xt[:, 1])
            v.wait_ge(g.bu_done, (NCH + 1) * 4 + 1)
            for n in range(2):
                st.do(v.tensor_tensor(g.x1[:, n], g.x1[:, n],
                                      g.ps[:, 2 + n, 0:P].rearrange("p (j b) -> p j b", j=J), ALU.add))
            v.sem_inc(g.xs_ready, 1)
            v.wait_ge(g.c_done, NCH * 4 + 3)
            for p in range(4):
                st.did(v.scalar_tensor_tensor(g.u[:, p, SEQ:TOK], g.u[:, p, SEQ:TOK],
                                              g.vec[:, V_DS + p:V_DS + p + 1],
                                              g.ps[:, 6, p * NB:(p + 1) * NB], ALU.mult, ALU.add))
            st.wait()
            g.dve_end = st.n

        @block.tensor
        def _(pe):
            pe.wait_ge(g.s5_fwd, 1)
            for n in range(2):
                for t in range(4):
                    last = pe.transpose(g.ps[:, 2 + n, t * P:(t + 1) * P],
                                        g.bm[:, n, 4 * t:4 * t + 4, :].rearrange("p a c -> p (a c)"),
                                        g.ident[:, :])
            last.then_inc(g.s5_tr, 1)
            pe.sem_inc(g.bu_done, 4)
            pe.sem_inc(g.c_done, 2)
            pe.wait_ge(g.s5_bt, 1)

            def bu(i, p):
                if p == 0:
                    pe.wait_ge(g.uc_ready, i + 1)
                pe.wait_ge(g.bu_free, i * 4 + (p + 1))
                for a in range(4):
                    for n in range(2):
                        last = pe.matmul(g.ps[:, 2 + 2 * (p % 2) + n, a * CH:(a + 1) * CH],
                                         g.BT[n][:, 4 * p + a, :], g.uc[:, p, :], start=True, stop=True)
                last.then_inc(g.bu_done, 1)

            def c(i, p):
                if p == 0:
                    pe.wait_ge(g.y_free, i + 1)
                pe.wait_ge(g.xc_ready, i * 4 + (p + 3))
                for n in range(2):
                    for a in range(4):
                        last = pe.matmul(g.ps[32 * a:32 * a + 32, 6, p * CH:(p + 1) * CH],
                                         g.CT[n][:, 4 * p + a, :], g.xs[:, n, p % 2, a, :],
                                         start=n == 0, stop=n == 1, skip_group_check=True)
                last.then_inc(g.c_done, 1)

            bu(0, 0)
            bu(0, 1)

            def turn(i, more):
                ops = gate_products(pe, g, i)
                bu(i, 2)
                run(ops, 24)
                c(i, 0)
                bu(i, 3)
                run(ops, 12)
                c(i, 1)
                if more:
                    bu(i + 1, 0)
                run(ops, 16)
                c(i, 2)
                if more:
                    bu(i + 1, 1)
                run(ops, 200)
                c(i, 3)

            with pe.Fori(0, NCH - 1) as i:
                turn(i, True)
            turn(NCH - 1, False)
            pe.wait_ge(g.uc_ready, NCH + 1)
            pe.wait_ge(g.bu_free, NCH * 4 + 2)
            for a in range(J):
                for n in range(2):
                    last = pe.matmul(g.ps[:, 2 + n, a * NB:(a + 1) * NB], g.BT[n][:, a, :],
                                     g.uc[:, a // 4, 0:NB], start=True, stop=True)
            last.then_inc(g.bu_done, 1)
            pe.wait_ge(g.xs_ready, 1)
            pe.wait_ge(g.y_free, NCH + 1)
            for p in range(4):
                for n in range(2):
                    for a in range(4):
                        last = pe.matmul(g.ps[32 * a:32 * a + 32, 6, p * NB:(p + 1) * NB],
                                         g.CT[n][:, 4 * p + a, :], g.x1[:, n, 4 * p + a, :],
                                         start=n == 0, stop=n == 1, skip_group_check=True)
            last.then_inc(g.c_done, 1)

    gates_done(g)
    g.dve_n, g.pool_n = g.dve_end, g.pool_end


def split_turn(pool, g, i, u0, kt):
    n = kt * P
    for s in range(2):
        pool.wait_ge(g.w_in[s], i * 16 + 16 * (u0 // 2 + 1))
        pool.wait_ge(g.unit_done, i * 2 + (u0 + s + 1))
        pool.tensor_tensor(g.whi[:, s, 0:n], g.wraw[:, s, 0:n], g.zero.to_broadcast([P, n]),
                               ALU.add).then_inc(g.w_hi, 1)
        pool.wait_ge(g.w_hi, i * 2 + (u0 + s + 1))
        pool.tensor_tensor(g.wlo[:, s, 0:n], g.wraw[:, s, 0:n], g.whi[:, s, 0:n].bitcast(F32),
                           ALU.subtract).then_inc(g.w_split, 1)


class Events:

    def __init__(self, sem, names):
        self.sem, self.names, self.k = sem, names, 0

    def on(self, ins, name):
        assert self.names[self.k % len(self.names)] == name, name
        self.k += 1
        ins.then_inc(self.sem, 1)

    def mark(self, eng, name):
        assert self.names[self.k % len(self.names)] == name, name
        self.k += 1
        eng.sem_inc(self.sem, 1)

    def wait(self, eng, i, name):
        n = len(self.names)
        eng.wait_ge(self.sem, i * n + (n + self.names.index(name) + 1))


LEVELS = range(1, 7)
LEV = [f"{a}{j}{n}" for j in LEVELS for a in "xt" for n in range(2)]
PE_NAMES = ["lora", "norms", "rn", "bonus", "tok", "score0", "score1", "score2", "score3", "m"] + LEV + [
    "r0", "sa", "o", "s", "g", "yt"]
ACT_NAMES = ["th", "tanh", "exp", "sq", "tok", "r0", "sa", "o", "osq", "g"]
DVE_NAMES = ["th", "cum", "kraw", "rn", "kr", "rk", "bonus", "score0", "score1", "score2", "score3",
             "m0", "m1", "state"] + LEV + ["s", "oc", "y", "yt"]


def plan_rwkv(nc, g):
    o = g.x_off
    g.fc, o = g.at("rw_f", o, [P, 2, RT, CH])
    g.th, o = g.at("rw_lora", o, [P, 2, CH])
    g.E = []
    for n in range(8):
        t, o = g.at(f"rw_e{n}", o, [P, 4, CH])
        g.E.append(t)
    g.KR, o = g.at("rw_kr", o, [P, 4, 2, CH])
    g.ktok, o = g.at("rw_ktok", o, [P, W])
    g.btok, o = g.at("rw_btok", o, [P, W])
    g.vtok, o = g.at("rw_vtok", o, [P, W])
    g.SC, o = g.at("rw_scores", o, [P, H, 2, 2, CH])
    g.T, o = g.at("rw_t", o, [P, H, CH])
    g.TT, o = g.at("rw_tt", o, [P, H, CH])
    g.X, o = g.at("rw_x", o, [P, H, CH])
    g.r0, o = g.at("rw_r0", o, [P, 2, 4 * N])
    g.sa, o = g.at("rw_sa", o, [P, 2, 4 * N])
    g.S, o = g.at("rw_s", o, [P, 4, N])
    g.rtab, o = g.at("rw_tab", o, [P, NTAB, P])
    g.wa, o = g.at("rw_wa", o, [P, W])
    g.gup, o = g.at("rw_gup", o, [P, W])
    g.lnw, o = g.at("rw_lnw", o, [P, W])
    g.lnb, o = g.at("rw_lnb", o, [P, W])
    g.rs, o = g.at("rw_small", o, [P, 12, 8])
    g.yt, o = g.at("rw_y", o, [P, 4, CH])
    g.goutr, o = g.at("gate_out_r", o, [P, TOK])
    assert o <= g.u_off, (o, g.u_off)
    g.oc, g.osq, g.gs = g.E[1], g.E[4], g.E[7]
    S = nc.alloc_semaphore
    g.rw_in, g.f_in, g.ya_out, g.rw_out = S("rwkv_consts_in"), [S("f_in0"), S("f_in1")], S("ya_out"), S("wkv_out")
    g.rw_set = S("rwkv_set_up")
    g.pe_ev, g.act_ev, g.dve_ev = (Events(S("rwkv_pe"), PE_NAMES), Events(S("rwkv_act"), ACT_NAMES),
                                   Events(S("rwkv_dve"), DVE_NAMES))


def bc(ap, n):
    return ap.unsqueeze(2).to_broadcast([ap.shape[0], ap.shape[1], n])


def flat(ap):
    return ap.rearrange("p a c -> p (a c)")


def group_norm(v, g, st, rows, on_centred, squared):
    r = slice(0, rows)
    rs = [g.rs[r, n, :] for n in range(12)]
    o2, q2 = flat(g.oc[:, :, :])[r], flat(g.osq[:, :, :])[r]
    oh, qh = (x.rearrange("p (h c) -> p h c", h=H) for x in (o2, q2))
    st.do(v.tensor_reduce(rs[5], oh, AXX, ALU.add))
    st.do(v.tensor_scalar(rs[5], rs[5], -1.0 / N, None, ALU.mult))
    st.do(v.tensor_tensor(oh, oh, bc(rs[5], N), ALU.add))
    on_centred()
    squared()
    st.do(v.tensor_reduce(rs[6], qh, AXX, ALU.add))
    rsqrt(v, st, rs[7], rs[6], rs[4], 1.0 / N, LNX_EPS)
    st.do(v.tensor_tensor(oh, oh, bc(rs[7], N), ALU.mult))
    st.do(v.tensor_tensor(o2, o2, g.lnw[r, :], ALU.mult))
    st.do(v.tensor_tensor(o2, o2, g.lnb[r, :], ALU.add))
    st.do(v.tensor_tensor(qh, g.vtok[r, :].rearrange("p (h c) -> p h c", h=H), bc(rs[11], N), ALU.mult))
    st.do(v.tensor_tensor(oh, oh, qh, ALU.add))


def rwkv_block(nc, g, w_gate, gate_dram, f_dram, tabs, wa_in, gup_in, lnw_in, lnb_in, ya_dram, wkvp_out):
    E = g.E
    pe_ev, act_ev, dve_ev = g.pe_ev, g.act_ev, g.dve_ev
    g.gout = g.goutr
    one = g.seg[:, 2:3]

    def bank(n, a=4):
        return g.ps[:, n, :].rearrange("p (a c) -> p a c", a=a)

    def rows(q):
        return slice(64 * q, 64 * q + 64)

    with nc.Block() as block:
        @block.sync
        def _(sp):
            for dst, src in ((g.rtab[:, :, :], tabs), (g.wa[:, :], wa_in), (g.gup[:, :], gup_in),
                             (g.lnw[:, :], lnw_in.to_broadcast([P, W])), (g.lnb[:, :], lnb_in.to_broadcast([P, W]))):
                sp.dma_start(dst, src).then_inc(g.rw_in, 16)
            u, m = g.units, g.gates * NBLK

            def load(i, par):
                sp.dma_start(g.fc[:, par, :, :],
                             f_dram[:, :, bass.ds(i * CH, CH)].rearrange("a p k -> p a k")).then_inc(g.f_in[par], 16)

            def rest(i):
                for j in range(2):
                    sp.wait_ge(g.w_split, i * 2 + (u + j + 1))
                    sp.dma_start(g.wraw[:, j, 0:4 * P],
                                 w_gate[bass.ds(i + g.gates, 1), :, j * 4 * P:(j + 1) * 4 * P].rearrange("a p k -> p (a k)"))\
                      .then_inc(g.w_in[j], 16)
                sp.wait_ge(g.gate_free, i * NBLK + (m + NBLK + 2))
                sp.dma_start(gate_dram[bass.ds(i + g.gates, 1), :, :].rearrange("a p k -> p (a k)"), g.gout[:, :])\
                  .then_inc(g.gate_out, 16)
                dve_ev.wait(sp, i, "yt")
                sp.dma_start(ya_dram[:, :, bass.ds(i * CH, CH)], g.yt[:, :, :]).then_inc(g.ya_out, 16)

            load(0, 0)
            load(1, 1)
            with sp.Fori(0, NCH // 2 - 1) as ii:
                for par in range(2):
                    rest(ii * 2 + par)
                    load(ii * 2 + (par + 2), par)
            rest(NCH - 2)
            rest(NCH - 1)
            sp.dma_start(wkvp_out, g.S[:, :, :]).then_inc(g.rw_out, 16)
            sp.wait_ge(g.rw_out, 16)
            sp.wait_ge(g.ya_out, 16 * (NCH + 1))
            sp.wait_ge(g.gate_out, 16 * (g.gates + NCH + 1))

        @block.gpsimd
        def _(pool):
            with pool.Fori(0, NCH) as i:
                split_turn(pool, g, i, g.units, 4)

        @block.scalar
        def _(act):
            act.sem_inc(act_ev.sem, len(ACT_NAMES))
            act.wait_ge(g.rw_in, 16 * 5)
            act.wait_ge(g.rw_set, 1)

            def turn(i, par, count):
                f = g.fc[:, par]
                act.wait_ge(g.f_in[par], count)
                pe_ev.wait(act, i - 1, "yt")
                act.activation(g.th[64:P, 0, :], f[64:P, 12, :], ACT.Copy)
                act.activation(g.th[0:64, 0, :], f[0:64, 12, :], ACT.Tanh)
                act_ev.on(act.activation(g.th[:, 1, :], f[:, 13, :], ACT.Tanh, scale=0.5), "th")
                pe_ev.wait(act, i, "lora")
                dve_ev.wait(act, i - 1, "yt")
                for p in range(4):
                    act.activation(E[0][:, p, :], g.ps[:, 2, p * CH:(p + 1) * CH], ACT.Tanh,
                                   bias=g.rs[:, 8, p:p + 1], scale=0.5)
                    ins = act.activation(E[5][:, p, :], g.ps[:, 3, p * CH:(p + 1) * CH], ACT.Tanh,
                                         bias=g.rs[:, 8, 4 + p:5 + p], scale=0.5)
                act_ev.on(ins, "tanh")
                dve_ev.wait(act, i, "cum")
                act.activation(E[2][:, :, :], E[1][:, :, :], ACT.Exp, scale=-DECAY)
                act.activation(E[3][:, :, :], E[1][:, :, :], ACT.Exp, scale=DECAY)
                act.activation(g.rs[:, 1, 0:4], g.rs[:, 0, 0:4], ACT.Exp, scale=-DECAY)
                act_ev.on(act.activation(E[4][:, :, :], E[4][:, :, :], ACT.Exp, scale=-DECAY), "exp")
                dve_ev.wait(act, i, "kraw")
                act_ev.on(act.activation(E[7][:, :, :], E[6][:, :, :], ACT.Square), "sq")
                gate_take(act, g, i, 0)
                pe_ev.wait(act, i, "tok")
                act.activation(g.vtok[:, :], g.ps[:, 2, :], ACT.Copy)
                act.activation(g.ktok[:, :], g.ps[:, 3, :], ACT.Copy)
                act_ev.on(act.activation(g.btok[:, :], g.ps[:, 4, :], ACT.Copy), "tok")
                gate_take(act, g, i, 1)
                pe_ev.wait(act, i, "r0")
                act_ev.on(act.activation(g.r0[:, :, :], g.ps[:, 2:4, 0:4 * N], ACT.Copy, scale=-1.0), "r0")
                pe_ev.wait(act, i, "sa")
                act_ev.on(act.activation(g.sa[:, :, :].rearrange("p a c -> p (a c)"), g.ps[:, 4, :], ACT.Copy), "sa")
                gate_take(act, g, i, 2)
                pe_ev.wait(act, i, "o")
                act_ev.on(act.activation(flat(g.oc[:, :, :]).rearrange("p (a q c) -> p q a c", q=2, c=N),
                                         g.ps[:, 5:7, 0:4 * N].rearrange("p q (a c) -> p q a c", a=4), ACT.Copy), "o")
                dve_ev.wait(act, i, "oc")
                act_ev.on(act.activation(g.osq[:, :, :], g.oc[:, :, :], ACT.Square), "osq")
                pe_ev.wait(act, i, "g")
                act_ev.on(act.activation(flat(g.gs[:, :, :]), g.ps[:, 2, :], ACT.Copy), "g")

            with act.Fori(0, NCH // 2) as ii:
                for par in range(2):
                    turn(ii * 2 + par, par, ii * 16 + 16)

        @block.vector
        def _(v):
            st = Steps(v, g.dve_s, g.dve_n)
            v.sem_inc(dve_ev.sem, len(DVE_NAMES))
            v.sem_inc(g.ya_out, 16)
            v.wait_ge(g.rw_in, 16 * 5)
            st.do(v.tensor_scalar(g.rs[:, 8, :], g.vec[:, V_W0:V_W0 + 8], 0.5, None, ALU.mult))
            for p in range(4):
                st.do(v.tensor_scalar(g.rs[:, 9, 2 * p:2 * p + 2], g.seg[:, 0:2], g.vec[:, V_RK + p:V_RK + p + 1],
                                      None, ALU.mult))
            st.do(v.memset(g.S[:, :, :], 0.0))
            v.sem_inc(g.rw_set, 2)
            mask2 = g.rtab[:, T_STRICT:T_INCL + 1, :].unsqueeze(1).to_broadcast([P, 2, 2, CH])

            def mk(t):
                return g.rtab[:, t:t + 1, :].to_broadcast([P, 4, CH])

            def tt(o, a, b, op):
                st.do(v.tensor_tensor(o, a, b, op))

            def turn(i, par):
                f = g.fc[:, par]
                r, k = f[:, 0:4, :], f[:, 4:8, :]
                act_ev.wait(v, i, "th")
                st.do(v.tensor_scalar(g.th[:, 1, :], g.th[:, 1, :], 0.5, 0.5, ALU.mult, ALU.add))
                dve_ev.mark(v, "th")
                act_ev.wait(v, i, "tanh")
                st.do(v.tensor_scalar(E[0][:, :, :], E[0][:, :, :], 0.5, 0.5, ALU.mult, ALU.add))
                for p in range(4):
                    st.did(v.tensor_tensor_scan(E[1][:, p, :], one.to_broadcast([P, CH]), E[0][:, p, :], 0.0,
                                                ALU.mult, ALU.add))
                st.wait()
                st.do(v.tensor_copy(g.rs[:, 0, 0:4], E[1][:, :, CH // 2 - 1]))
                tt(E[1][:, :, :], E[1][:, :, :], bc(g.rs[:, 0, 0:4], CH), ALU.subtract)
                tt(E[4][:, :, :], E[1][:, :, :], E[0][:, :, :], ALU.subtract)
                dve_ev.mark(v, "cum")
                tt(E[6][:, :, :], k, bc(g.vec[:, V_KK:V_KK + 4], CH), ALU.mult)
                dve_ev.mark(v, "kraw")
                st.do(v.tensor_scalar(E[5][:, :, :], E[5][:, :, :], 0.5, 0.5, ALU.mult, ALU.add))
                pe_ev.wait(v, i, "norms")
                st.do(v.tensor_copy(g.rs[:, 2, :], g.ps[:, 5, 0:8]))
                rsqrt(v, st, g.rs[:, 3, :], g.rs[:, 2, :], g.rs[:, 4, :], 1.0, 0.0, floor=1e-24)
                dve_ev.mark(v, "rn")
                st.do(v.scalar_tensor_tensor(E[7][:, :, :], E[5][:, :, :], -1.0, bc(g.vec[:, V_KA:V_KA + 4], CH),
                                             ALU.add, ALU.mult))
                st.do(v.scalar_tensor_tensor(E[7][:, :, :], E[7][:, :, :], 1.0, k, ALU.add, ALU.mult))
                pe_ev.wait(v, i, "rn")
                tt(E[6][:, :, :], E[6][:, :, :], bank(6), ALU.mult)
                tt(E[5][:, :, :], E[6][:, :, :], E[5][:, :, :], ALU.mult)
                act_ev.wait(v, i, "exp")
                tt(g.KR[:, :, 0, :], E[6][:, :, :], E[4][:, :, :], ALU.mult)
                tt(g.KR[:, :, 1, :], r, E[2][:, :, :], ALU.mult)
                tt(E[5][:, :, :], E[5][:, :, :], E[3][:, :, :], ALU.mult)
                tt(E[3][:, :, :], E[7][:, :, :], E[3][:, :, :], ALU.mult)
                dve_ev.mark(v, "kr")
                tt(E[0][:, :, :], r, E[7][:, :, :], ALU.mult)
                dve_ev.mark(v, "rk")
                pe_ev.wait(v, i, "bonus")
                st.do(v.tensor_copy(g.rs[:, 11, :], g.ps[:, 5, 0:8]))
                dve_ev.mark(v, "bonus")
                for n in range(4):
                    pe_ev.wait(v, i, f"score{n}")
                    for q in range(2):
                        tt(g.SC[:, 4 * q + n], g.ps[:, 4 + 2 * (n % 2) + q, :].rearrange("p (x a c) -> p x a c", x=2, a=2),
                           mask2, ALU.mult)
                    dve_ev.mark(v, f"score{n}")
                pe_ev.wait(v, i, "m")
                for n in range(2):
                    hs = slice(4 * n, 4 * n + 4)
                    tt(g.T[:, hs], bank(2 + n), mk(T_L0), ALU.mult)
                    tt(g.T[:, hs], g.T[:, hs], mk(T_ID), ALU.add)
                    tt(g.TT[:, hs], g.SC[:, hs, 1, 0, :], mk(T_L0T), ALU.mult)
                    tt(g.TT[:, hs], g.TT[:, hs], mk(T_ID), ALU.add)
                    dve_ev.mark(v, f"m{n}")
                tt(g.S[:, :, :], g.S[:, :, :], bc(g.rs[:, 1, 0:4], N), ALU.mult)
                dve_ev.mark(v, "state")
                for j in LEVELS:
                    for n in range(2):
                        pe_ev.wait(v, i, f"x{j}{n}")
                        tt(g.X[:, 4 * n:4 * n + 4], bank(2 + n), mk(T_LEV + j - 1), ALU.mult)
                        dve_ev.mark(v, f"x{j}{n}")
                    for n in range(2):
                        hs = slice(4 * n, 4 * n + 4)
                        pe_ev.wait(v, i, f"t{j}{n}")
                        if j < 6:
                            tt(g.T[:, hs], g.T[:, hs], bank(4 + 2 * n), ALU.add)
                        tt(g.TT[:, hs], g.TT[:, hs], bank(5 + 2 * n), ALU.add)
                        dve_ev.mark(v, f"t{j}{n}")
                pe_ev.wait(v, i, "s")
                tt(g.S[:, :, :], g.S[:, :, :], g.ps[:, 7, 0:4 * N].rearrange("p (a c) -> p a c", a=4), ALU.add)
                tt(g.S[:, :, :], g.S[:, :, :], E[2][:, :, CH - 1:CH].to_broadcast([P, 4, N]), ALU.mult)
                dve_ev.mark(v, "s")
                act_ev.wait(v, i, "o")
                group_norm(v, g, st, P, lambda: dve_ev.mark(v, "oc"), lambda: act_ev.wait(v, i, "osq"))
                dve_ev.mark(v, "y")
                pe_ev.wait(v, i, "yt")
                act_ev.wait(v, i, "g")
                v.wait_ge(g.ya_out, i * 16 + 16)
                tt(g.yt[:, :, :], g.gs[:, :, :], bank(3), ALU.mult)
                dve_ev.mark(v, "yt")

            with v.Fori(0, NCH // 2) as ii:
                st.enter(ii, 240)
                for par in range(2):
                    turn(ii * 2 + par, par)
                st.leave(NCH // 2)
            g.dve_end = st.n

        @block.tensor
        def _(pe):
            pe.sem_inc(pe_ev.sem, len(PE_NAMES))
            pe.wait_ge(g.rw_set, 2)

            def turn(i, par):
                ops = gate_products(pe, g, i)
                f = g.fc[:, par]
                act_ev.wait(pe, i, "th")
                dve_ev.wait(pe, i - 1, "yt")
                for p in range(4):
                    pe.matmul(g.ps[:, 2, p * CH:(p + 1) * CH], g.wa[0:64, p * P:(p + 1) * P], g.th[0:64, 0, :],
                              start=True, stop=True)
                    last = pe.matmul(g.ps[:, 3, p * CH:(p + 1) * CH], g.wa[64:P, p * P:(p + 1) * P],
                                     g.th[64:P, 0, :], start=True, stop=True)
                pe_ev.on(last, "lora")
                run(ops, 10)
                act_ev.wait(pe, i, "sq")
                for p in range(4):
                    last = pe.matmul(g.ps[:, 5, 2 * p:2 * p + 2], E[7][:, p, :], g.seg[:, 0:2], start=True, stop=True)
                pe_ev.on(last, "norms")
                run(ops, 14)
                dve_ev.wait(pe, i, "rn")
                for p in range(4):
                    for q in range(2):
                        last = pe.matmul(g.ps[rows(q), 6, p * CH:(p + 1) * CH],
                                         g.rs[:, 3, 2 * p + q:2 * p + q + 1].to_broadcast([P, 64]),
                                         g.ident[:, :], start=True, stop=True)
                pe_ev.on(last, "rn")
                run(ops, 12)
                dve_ev.wait(pe, i, "rk")
                for p in range(4):
                    last = pe.matmul(g.ps[:, 5, 2 * p:2 * p + 2], E[0][:, p, :], g.rs[:, 9, 2 * p:2 * p + 2],
                                     start=True, stop=True)
                pe_ev.on(last, "bonus")
                for n, src in enumerate((f[:, 8:12], E[3], E[5])):
                    for p in range(4):
                        last = pe.transpose(g.ps[:, 2 + n, p * P:(p + 1) * P], src[:, p, :], g.ident[:, :])
                pe_ev.on(last, "tok")
                run(ops, 12)
                dve_ev.wait(pe, i, "bonus")
                act_ev.wait(pe, i, "tok")
                for p in range(4):
                    if p >= 2:
                        dve_ev.wait(pe, i, f"score{p - 2}")
                    for x, src in enumerate((E[3], E[5])):
                        for q in range(2):
                            last = pe.matmul(g.ps[:, 4 + 2 * (p % 2) + q, 256 * x:256 * x + 256], src[rows(q), p, :],
                                             g.KR[rows(q), p, :, :].rearrange("p a c -> p (a c)"), start=True, stop=True)
                    pe_ev.on(last, f"score{p}")
                for p in range(4):
                    for q in range(2):
                        last = pe.matmul(g.ps[:, 2 + q, p * CH:(p + 1) * CH], g.KR[rows(q), p, 0, :], E[5][rows(q), p, :],
                                         start=True, stop=True)
                pe_ev.on(last, "m")
                for j in LEVELS:
                    for n in range(2):
                        dve_ev.wait(pe, i, f"m{n}" if j == 1 else f"t{j - 1}{n}")
                        for p in range(4):
                            h = 4 * n + p
                            last = pe.matmul(g.ps[:, 2 + n, p * CH:(p + 1) * CH], g.SC[:, h, 1, 0, :], g.T[:, h, :],
                                             start=True, stop=True)
                        pe_ev.on(last, f"x{j}{n}")
                    for n in range(2):
                        dve_ev.wait(pe, i, f"x{j}{n}")
                        for p in range(4):
                            h = 4 * n + p
                            if j < 6:
                                pe.matmul(g.ps[:, 4 + 2 * n, p * CH:(p + 1) * CH], g.TT[:, h, :], g.X[:, h, :],
                                          start=True, stop=True)
                            last = pe.matmul(g.ps[:, 5 + 2 * n, p * CH:(p + 1) * CH], g.X[:, h, :], g.TT[:, h, :],
                                             start=True, stop=True)
                        pe_ev.on(last, f"t{j}{n}")
                dve_ev.wait(pe, i, "state")
                for p in range(4):
                    for q in range(2):
                        h = 2 * p + q
                        pe.matmul(g.ps[:, 2 + q, p * N:(p + 1) * N], g.KR[rows(q), p, 0, :], g.S[rows(q), p, :],
                                  start=True, stop=False)
                    for q in range(2):
                        h = 2 * p + q
                        last = pe.matmul(g.ps[:, 2 + q, p * N:(p + 1) * N], g.SC[:, 4 * q + p, 0, 0, :],
                                         g.vtok[:, h * N:(h + 1) * N], start=False, stop=True)
                pe_ev.on(last, "r0")
                run(ops, 12)
                act_ev.wait(pe, i, "r0")
                dve_ev.wait(pe, i, "t61")
                for h in range(H):
                    last = pe.matmul(g.ps[:, 4, h * N:(h + 1) * N], g.TT[:, h, :],
                                     flat(g.r0[:, :, :])[:, h * N:(h + 1) * N], start=True, stop=True)
                pe_ev.on(last, "sa")
                run(ops, 200)
                act_ev.wait(pe, i, "sa")
                for p in range(4):
                    for q in range(2):
                        pe.matmul(g.ps[:, 5 + q, p * N:(p + 1) * N], g.KR[rows(q), p, 1, :], g.S[rows(q), p, :],
                                  start=True, stop=False)
                    for q in range(2):
                        h, hq = 2 * p + q, 4 * q + p
                        pe.matmul(g.ps[:, 5 + q, p * N:(p + 1) * N], g.SC[:, hq, 0, 1, :],
                                  g.vtok[:, h * N:(h + 1) * N], start=False, stop=False)
                        last = pe.matmul(g.ps[:, 5 + q, p * N:(p + 1) * N], g.SC[:, hq, 1, 1, :],
                                         flat(g.sa[:, :, :])[:, hq * N:(hq + 1) * N], start=False, stop=True)
                pe_ev.on(last, "o")
                for p in range(4):
                    for q in range(2):
                        h, hq = 2 * p + q, 4 * q + p
                        pe.matmul(g.ps[rows(q), 7, p * N:(p + 1) * N], g.ktok[:, h * N:(h + 1) * N],
                                  g.vtok[:, h * N:(h + 1) * N], start=True, stop=False)
                        last = pe.matmul(g.ps[rows(q), 7, p * N:(p + 1) * N], g.btok[:, h * N:(h + 1) * N],
                                         flat(g.sa[:, :, :])[:, hq * N:(hq + 1) * N], start=False, stop=True)
                pe_ev.on(last, "s")
                dve_ev.wait(pe, i, "th")
                for p in range(4):
                    last = pe.matmul(g.ps[:, 2, p * CH:(p + 1) * CH], g.gup[:, p * P:(p + 1) * P], g.th[:, 1, :],
                                     start=True, stop=True)
                pe_ev.on(last, "g")
                dve_ev.wait(pe, i, "y")
                for p in range(4):
                    last = pe.transpose(g.ps[:, 3, p * CH:(p + 1) * CH], g.oc[:, p, :], g.ident[:, :])
                pe_ev.on(last, "yt")

            with pe.Fori(0, NCH // 2) as ii:
                for par in range(2):
                    turn(ii * 2 + par, par)
    gates_done(g)
    g.dve_n = g.dve_end


def plan_sample(nc, g):
    o = g.h_end - 2 * DT * TOK * 4
    g.sS, o = g.at("sm_state", o, [P, 4 * NB, N])
    g.sK, o = g.at("sm_kappa", o, [P, 4 * NB, P])
    g.sV, o = g.at("sm_v", o, [P, 4 * NB, N])
    g.sT, o = g.at("sm_tmp", o, [P, 4 * NB, N])
    g.sR, o = g.at("sm_r", o, [P, 2, 4, NB * NB])
    g.sF, o = g.at("sm_f", o, [P, RT, NB])
    assert o <= g.h_end
    S = nc.alloc_semaphore
    g.sm_in, g.sm_act, g.sm_pe, g.sm_dve, g.sm_out = (S("sample_in"), S("sample_act"), S("sample_pe"),
                                                      S("sample_dve"), S("sample_out"))


SM_ACT = ["th", "tanh", "exp", "sq", "tok", "o", "osq", "g"]
SM_PE = ["lora", "norms", "rn", "bonus", "tok", "sa", "o", "g", "yt"]
SM_DVE = ["th", "xw", "kraw", "rn", "rk", "bonus", "kv", "state", "r", "oc", "y", "yt"]


def sample_block(nc, g, f_dram, wkv_in, ya_dram, wkv_out):
    E = g.E
    a_ev, p_ev, d_ev = Events(g.sm_act, SM_ACT), Events(g.sm_pe, SM_PE), Events(g.sm_dve, SM_DVE)
    f = g.sF
    C8 = slice(0, NB)
    st32 = lambda t: t[:, :, :].rearrange("p (a b) c -> p a b c", a=4)

    def over(ap, n):
        return ap.unsqueeze(3).to_broadcast([P, 4, NB, n])

    def rows(q):
        return slice(64 * q, 64 * q + 64)

    with nc.Block() as block:
        @block.sync
        def _(sp):
            sp.dma_start(f[:, :, :], f_dram[:, :, SEQ:TOK].rearrange("a p k -> p a k")).then_inc(g.sm_in, 16)
            sp.dma_start(g.sS[:, :, :], wkv_in).then_inc(g.sm_in, 16)
            d_ev.wait(sp, 0, "state")
            sp.dma_start(wkv_out, g.sS[:, :, :]).then_inc(g.sm_out, 16)
            d_ev.wait(sp, 0, "yt")
            sp.dma_start(ya_dram[:, :, SEQ:TOK], g.yt[:, :, C8]).then_inc(g.sm_out, 16)
            sp.wait_ge(g.sm_out, 32)

        @block.scalar
        def _(act):
            act.sem_inc(g.sm_act, len(SM_ACT))
            act.wait_ge(g.sm_in, 32)
            act.activation(g.th[64:P, 0, C8], f[64:P, 12, :], ACT.Copy)
            act.activation(g.th[0:64, 0, C8], f[0:64, 12, :], ACT.Tanh)
            a_ev.on(act.activation(g.th[:, 1, C8], f[:, 13, :], ACT.Tanh, scale=0.5), "th")
            p_ev.wait(act, 0, "lora")
            for p in range(4):
                act.activation(E[0][:, p, C8], g.ps[:, 2, p * NB:(p + 1) * NB], ACT.Tanh,
                               bias=g.rs[:, 8, p:p + 1], scale=0.5)
                ins = act.activation(E[5][:, p, C8], g.ps[:, 3, p * NB:(p + 1) * NB], ACT.Tanh,
                                     bias=g.rs[:, 8, 4 + p:5 + p], scale=0.5)
            a_ev.on(ins, "tanh")
            d_ev.wait(act, 0, "xw")
            a_ev.on(act.activation(E[2][:, :, C8], E[0][:, :, C8], ACT.Exp, scale=-DECAY), "exp")
            d_ev.wait(act, 0, "kraw")
            a_ev.on(act.activation(E[7][:, :, C8], E[6][:, :, C8], ACT.Square), "sq")
            p_ev.wait(act, 0, "tok")
            a_ev.on(act.activation(g.vtok[C8, :], g.ps[C8, 2, :], ACT.Copy), "tok")
            p_ev.wait(act, 0, "o")
            a_ev.on(act.activation(flat(g.oc[:, :, :])[C8], g.ps[C8, 0, :], ACT.Copy), "o")
            d_ev.wait(act, 0, "oc")
            a_ev.on(act.activation(flat(g.osq[:, :, :])[C8], flat(g.oc[:, :, :])[C8], ACT.Square), "osq")
            p_ev.wait(act, 0, "g")
            a_ev.on(act.activation(flat(g.gs[:, :, :])[:, 0:4 * NB], g.ps[:, 1, 0:4 * NB], ACT.Copy), "g")

        @block.vector
        def _(v):
            st = Steps(v, g.dve_s, g.dve_n)
            v.sem_inc(g.sm_dve, len(SM_DVE))
            v.wait_ge(g.sm_in, 32)
            r, k, vv = f[:, 0:4, :], f[:, 4:8, :], f[:, 8:12, :]
            e = [t[:, :, C8] for t in E]

            def tt(o, a, b, op):
                st.do(v.tensor_tensor(o, a, b, op))

            a_ev.wait(v, 0, "th")
            st.do(v.tensor_scalar(g.th[:, 1, C8], g.th[:, 1, C8], 0.5, 0.5, ALU.mult, ALU.add))
            d_ev.mark(v, "th")
            a_ev.wait(v, 0, "tanh")
            st.do(v.tensor_scalar(e[0], e[0], 0.5, 0.5, ALU.mult, ALU.add))
            d_ev.mark(v, "xw")
            tt(e[6], k, bc(g.vec[:, V_KK:V_KK + 4], NB), ALU.mult)
            d_ev.mark(v, "kraw")
            st.do(v.tensor_scalar(e[5], e[5], 0.5, 0.5, ALU.mult, ALU.add))
            p_ev.wait(v, 0, "norms")
            st.do(v.tensor_copy(g.rs[C8, 2, :], g.ps[C8, 5, 0:8]))
            rsqrt(v, st, g.rs[C8, 3, :], g.rs[C8, 2, :], g.rs[C8, 4, :], 1.0, 0.0, floor=1e-24)
            d_ev.mark(v, "rn")
            st.do(v.scalar_tensor_tensor(e[7], e[5], -1.0, bc(g.vec[:, V_KA:V_KA + 4], NB), ALU.add, ALU.mult))
            st.do(v.scalar_tensor_tensor(e[7], e[7], 1.0, k, ALU.add, ALU.mult))
            p_ev.wait(v, 0, "rn")
            tt(e[6], e[6], g.ps[:, 6, 0:4 * NB].rearrange("p (a c) -> p a c", a=4), ALU.mult)
            tt(e[5], e[6], e[5], ALU.mult)
            a_ev.wait(v, 0, "exp")
            tt(e[0], r, e[7], ALU.mult)
            d_ev.mark(v, "rk")
            p_ev.wait(v, 0, "bonus")
            st.do(v.tensor_copy(g.rs[C8, 11, :], g.ps[C8, 5, 0:8]))
            d_ev.mark(v, "bonus")
            st.do(v.tensor_scalar(e[6], e[6], -1.0, None, ALU.mult))
            blk = g.rtab[:, T_BLK, :].unsqueeze(1).unsqueeze(1).to_broadcast([P, 4, NB, P])
            eye = g.rtab[:, T_IST, 0:N].unsqueeze(1).unsqueeze(1).to_broadcast([P, 4, NB, N])
            tt(st32(g.sK), blk, over(e[6], P), ALU.mult)
            tt(st32(g.sV), eye, over(vv, N), ALU.mult)
            d_ev.mark(v, "kv")
            S, T = st32(g.sS), st32(g.sT)
            p_ev.wait(v, 0, "sa")
            tt(S, S, over(e[2], N), ALU.mult)
            for first, x in ((0, e[5]), (4, e[7])):
                tt(T, g.ps[:, first:first + 4, :].rearrange("p a (b c) -> p a b c", b=NB), over(x, N), ALU.mult)
                tt(S, S, T, ALU.add)
            d_ev.mark(v, "state")
            eye8 = g.seg[:, 8:72].rearrange("p (b c) -> p b c", b=NB).unsqueeze(1).to_broadcast([P, 4, NB, NB])
            for q in range(2):
                R = g.sR[:, q, :, :].rearrange("p a (b c) -> p a b c", b=NB)
                tt(R, eye8, over(r, NB), ALU.mult)
                st.do(v.tensor_scalar(g.sR[:, q, :, :], g.sR[:, q, :, :], g.seg[:, q:q + 1], None, ALU.mult))
            d_ev.mark(v, "r")
            a_ev.wait(v, 0, "o")
            group_norm(v, g, st, NB, lambda: d_ev.mark(v, "oc"), lambda: a_ev.wait(v, 0, "osq"))
            d_ev.mark(v, "y")
            p_ev.wait(v, 0, "yt")
            a_ev.wait(v, 0, "g")
            tt(g.yt[:, :, C8], flat(g.gs[:, :, :])[:, 0:4 * NB].rearrange("p (a c) -> p a c", a=4),
               g.ps[:, 2, 0:4 * NB].rearrange("p (a c) -> p a c", a=4), ALU.mult)
            d_ev.mark(v, "yt")
            g.dve_end = st.n

        @block.tensor
        def _(pe):
            pe.sem_inc(g.sm_pe, len(SM_PE))
            a_ev.wait(pe, 0, "th")
            for p in range(4):
                pe.matmul(g.ps[:, 2, p * NB:(p + 1) * NB], g.wa[0:64, p * P:(p + 1) * P], g.th[0:64, 0, C8],
                          start=True, stop=True)
                last = pe.matmul(g.ps[:, 3, p * NB:(p + 1) * NB], g.wa[64:P, p * P:(p + 1) * P],
                                 g.th[64:P, 0, C8], start=True, stop=True)
            p_ev.on(last, "lora")
            a_ev.wait(pe, 0, "sq")
            for p in range(4):
                last = pe.matmul(g.ps[C8, 5, 2 * p:2 * p + 2], E[7][:, p, C8], g.seg[:, 0:2], start=True, stop=True)
            p_ev.on(last, "norms")
            d_ev.wait(pe, 0, "rn")
            for p in range(4):
                for q in range(2):
                    last = pe.matmul(g.ps[rows(q), 6, p * NB:(p + 1) * NB],
                                     g.rs[C8, 3, 2 * p + q:2 * p + q + 1].to_broadcast([NB, 64]),
                                     g.ident[C8, C8], start=True, stop=True)
            p_ev.on(last, "rn")
            d_ev.wait(pe, 0, "rk")
            for p in range(4):
                last = pe.matmul(g.ps[C8, 5, 2 * p:2 * p + 2], E[0][:, p, C8], g.rs[:, 9, 2 * p:2 * p + 2],
                                 start=True, stop=True)
            p_ev.on(last, "bonus")
            for p in range(4):
                last = pe.transpose(g.ps[C8, 2, p * P:(p + 1) * P], f[:, 8 + p, :], g.ident[:, :])
            p_ev.on(last, "tok")
            d_ev.wait(pe, 0, "kv")
            a_ev.wait(pe, 0, "tok")
            for n in range(4 * NB):
                pe.matmul(g.ps[:, n // NB, (n % NB) * N:(n % NB + 1) * N], g.sK[:, n, :], g.sS[:, n, :],
                          start=True, stop=True)
            for p in range(4):
                last = pe.matmul(g.ps[:, 4 + p, :], g.rtab[:, T_BLK, :],
                                 flat(g.sV[:, p * NB:(p + 1) * NB, :]), start=True, stop=True)
            p_ev.on(last, "sa")
            d_ev.wait(pe, 0, "r")
            for p in range(4):
                for q in range(2):
                    for b in range(NB):
                        last = pe.matmul(g.ps[C8, 0, (2 * p + q) * N:(2 * p + q + 1) * N],
                                         g.sR[:, q, p, b * NB:(b + 1) * NB], g.sS[:, p * NB + b, :],
                                         start=b == 0, stop=b == NB - 1)
            p_ev.on(last, "o")
            for p in range(4):
                last = pe.matmul(g.ps[:, 1, p * NB:(p + 1) * NB], g.gup[:, p * P:(p + 1) * P], g.th[:, 1, C8],
                                 start=True, stop=True)
            p_ev.on(last, "g")
            d_ev.wait(pe, 0, "y")
            for p in range(4):
                last = pe.transpose(g.ps[:, 2, p * NB:(p + 1) * NB], g.oc[C8, p, :], g.ident[C8, C8])
            p_ev.on(last, "yt")
    g.dve_n = g.dve_end


def make_tables():
    tab = np.zeros((P, NTAB, P), np.float32)
    a, b = np.meshgrid(np.arange(P), np.arange(P), indexing="ij")
    tab[:, T_ID] = a == b
    tab[:, T_STRICT] = a < b
    tab[:, T_INCL] = a <= b
    low = lambda j: (a >> (j + 1) == b >> (j + 1)) & ((a >> j) & 1 == 1) & ((b >> j) & 1 == 0)
    tab[:, T_L0] = -1.0 * low(0)
    tab[:, T_L0T] = -1.0 * low(0).T
    for j in LEVELS:
        tab[:, T_LEV + j - 1] = -1.0 * low(j)
    tab[:64, T_SEG, 0] = 1
    tab[64:, T_SEG, 1] = 1
    tab[:, T_SEG, 2] = 1
    tab[:, T_SEG, 8:72] = np.eye(8).reshape(1, 64)
    tab[:, T_BLK] = a // 64 == b // 64
    tab[:, T_IST, 0:64] = a[:, 0:64] % 64 == b[:, 0:64]
    return tab


GLU_IN, GLU_CUBE = 0.7978845608028654, 0.044715


def plan_merge(nc, g):
    o = g.h_end
    g.yahi, o = g.at("ya_hi", o, [P, WT, TOK], F32R)
    g.yalo, o = g.at("ya_lo", o, [P, WT, TOK], F32R)
    assert o <= g.x_end
    o = g.x_end
    g.ybhi, o = g.at("yb_hi", o, [P, WT, TOK], F32R)
    g.yblo, o = g.at("yb_lo", o, [P, WT, TOK], F32R)
    g.gt, o = g.at("gates_in", o, [P, 2, 2, TOK])
    g.mt, o = g.at("merge_t", o, [P, 2, TOK])
    g.mm, o = g.at("merged", o, [P, 1, TOK])
    assert o <= g.u_off, (o, g.u_off)
    g.zhi, g.zlo = g.hhi[:, 0:WT, :], g.hhi[:, WT:2 * WT, :]
    S = nc.alloc_semaphore
    g.ya_in, g.ya_hi_s, g.ya_split = S("ya_in"), S("ya_hi"), S("ya_split")
    g.gl_sq, g.gl_scaled, g.gl_in, g.gl_tanh = S("gelu_squared"), S("gelu_scaled"), S("gelu_inner"), S("gelu_tanh")
    g.z2_ready, g.z_hi, g.z_split = S("z2_ready"), S("z2_hi"), S("z2_split")
    g.yb_ready, g.yb_hi, g.yb_split = S("yb_ready"), S("yb_hi"), S("yb_split")
    g.gt_in, g.gt_used = [S("gates_in0"), S("gates_in1")], S("gates_used")
    g.m_ready, g.m_hi, g.m_split = S("merged_ready"), S("merged_hi"), S("merged_split")
    g.x_back = [S("x_back0"), S("x_back1")]


def merge_block(nc, g, w_glu, w_ab, w_out, ya_dram, gate_dram, x_dram):
    u0 = g.units
    ua = u0 + WT
    uo = ua + 2 * DT
    use = list(g.uses)
    use_a = [n + WT // 2 for n in use]
    use_o = [n + DT for n in use_a]
    u, t = g.u, g.mt

    def part(x):
        return lambda k, b: x[:, k, b * BLK:(b + 1) * BLK]

    with nc.Block() as block:
        @block.sync
        def _(sp):
            sp.dma_start(g.gt[:, :, :, :].rearrange("p a b c -> p (a b) c"), ya_dram).then_inc(g.ya_in, 16)
            load_units(sp, g, u0, WT // 2, 2, WT,
                       lambda i, j: w_glu[bass.ds(i * 2 + j, 1), :, :].rearrange("a p k -> p (a k)"))
            with sp.Fori(0, DT // 2) as ii:
                for par in range(2):
                    for j in range(2):
                        sp.wait_ge(g.w_split, ii * 4 + (ua + 2 * par + j + 1))
                        sp.dma_start(g.wraw[:, j, 0:WT * P],
                                     w_ab[bass.ds(ii * 4 + (2 * par + j), 1), :, :].rearrange("a p k -> p (a k)"))\
                          .then_inc(g.w_in[j], 16)
                    sp.wait_ge(g.gt_used, ii * 2 + (par + 1))
                    for q in range(2):
                        sp.dma_start(g.gt[:, par, q, :],
                                     gate_dram[bass.ds(ii * 2 + (par + DT * q), 1), :, :].rearrange("a p k -> p (a k)"))\
                          .then_inc(g.gt_in[par], 16)
            load_units(sp, g, uo, DT // 2, 2, DT,
                       lambda i, j: w_out[bass.ds(i * 2 + j, 1), :, :].rearrange("a p k -> p (a k)"))

        @block.gpsimd
        def _(pool):
            def split_ya(k):
                pool.tensor_tensor(g.yahi[:, k, :], g.gt[:, k // 2, k % 2, :], g.zero.to_broadcast([P, TOK]),
                                   ALU.add).then_inc(g.ya_hi_s, 1)
                pool.wait_ge(g.ya_hi_s, k + 1)
                pool.tensor_tensor(g.yalo[:, k, :], g.gt[:, k // 2, k % 2, :], g.yahi[:, k, :].bitcast(F32),
                                   ALU.subtract).then_inc(g.ya_split, 1)

            split_units(pool, g, u0, 1, 2, WT)
            pool.wait_ge(g.ya_in, 16)
            split_ya(0)
            split_ya(1)
            split_units(pool, g, u0 + 2, 1, 2, WT)
            split_ya(2)
            split_ya(3)
            pool.wait_ge(g.ya_split, WT)
            pool.sem_inc(g.gt_used, 2)
            split_units(pool, g, ua, DT, 2, WT)
            split_units(pool, g, uo, DT // 2, 2, DT)

        @block.scalar
        def _(act):
            for n in range(2):
                act.activation(t[:, n, :], u[:, n, :], ACT.Square).then_inc(g.gl_sq, 1)
            for n in range(WT):
                act.wait_ge(g.gl_in, n + 1)
                act.activation(t[:, n % 2, :], t[:, n % 2, :], ACT.Tanh, scale=GLU_IN).then_inc(g.gl_tanh, 1)
                act.wait_ge(g.z2_ready, n + 1)
                act.activation(g.zhi[:, n, :], u[:, n, :], ACT.Copy).then_inc(g.z_hi, 1)
                if n + 2 < WT:
                    act.activation(t[:, n % 2, :], u[:, n + 2, :], ACT.Square).then_inc(g.gl_sq, 1)
            for n in range(WT):
                act.wait_ge(g.unit_done, u0 + n + 1 + WSLOTS)
                if n >= 2:
                    act.wait_ge(g.yb_ready, n - 1)
                act.activation(blocks(t[:, n % 2, :]), acc(g, n % 2), ACT.Tanh, scale=0.25)\
                   .then_inc(g.set_free[n % 2], 1)
                act.wait_ge(g.yb_ready, n + 1)
                act.activation(g.ybhi[:, n, :], u[:, n, :], ACT.Copy).then_inc(g.yb_hi, 1)
            with act.Fori(0, DT) as i:
                act.wait_ge(g.m_ready, i + 1)
                act.activation(g.hhi[:, bass.ds(i, 1), :], g.mm[:, :, :], ACT.Copy).then_inc(g.m_hi, 1)
            act.wait_ge(g.unit_done, uo - 1 + WSLOTS)
            for n in range(2):
                half = slice(n * DT // 2, (n + 1) * DT // 2)
                act.dma_start(g.x[:, half, :], x_dram[:, half, :]).then_inc(g.x_back[n], 16)

        @block.vector
        def _(v):
            def inner(n):
                v.wait_ge(g.gl_sq, n + 1)
                v.tensor_scalar(t[:, n % 2, :], t[:, n % 2, :], GLU_CUBE, 1.0, ALU.mult, ALU.add)\
                 .then_inc(g.gl_scaled, 1)
                v.wait_ge(g.gl_scaled, n + 1)
                v.tensor_tensor(t[:, n % 2, :], t[:, n % 2, :], u[:, n, :], ALU.mult).then_inc(g.gl_in, 1)

            inner(0)
            inner(1)
            for n in range(WT):
                v.wait_ge(g.gl_tanh, n + 1)
                v.scalar_tensor_tensor(u[:, n, :], t[:, n % 2, :], 1.0, u[:, n, :], ALU.add, ALU.mult)\
                 .then_inc(g.z2_ready, 1)
                v.wait_ge(g.z_hi, n + 1)
                v.tensor_tensor(g.zlo[:, n, :], u[:, n, :], g.zhi[:, n, :].bitcast(F32),
                                ALU.subtract).then_inc(g.z_split, 1)
                if n + 2 < WT:
                    inner(n + 2)
            for n in range(WT):
                v.wait_ge(g.set_free[n % 2], use[n % 2] + n // 2 + 2)
                v.scalar_tensor_tensor(u[:, n, :], t[:, n % 2, :], 1.0, u[:, n, :], ALU.add, ALU.mult)\
                 .then_inc(g.yb_ready, 1)
                v.wait_ge(g.yb_hi, n + 1)
                v.tensor_tensor(g.yblo[:, n, :], u[:, n, :], g.ybhi[:, n, :].bitcast(F32),
                                ALU.subtract).then_inc(g.yb_split, 1)
            with v.Fori(0, DT // 2) as ii:
                for par in range(2):
                    gates = [g.gt[:, par, q, :] for q in range(2)]
                    v.wait_ge(g.gt_in[par], ii * 32 + 32)
                    v.wait_ge(g.unit_done, ii * 4 + (ua + 2 * par + 1 + WSLOTS))
                    v.scalar_tensor_tensor(blocks(t[:, 0, :]), blocks(gates[0]), 1.0, acc(g, 0), ALU.add, ALU.mult)\
                     .then_inc(g.set_free[0], 1)
                    v.wait_ge(g.unit_done, ii * 4 + (ua + 2 * par + 2 + WSLOTS))
                    v.scalar_tensor_tensor(blocks(t[:, 1, :]), blocks(gates[1]), 1.0, acc(g, 1), ALU.add, ALU.mult)\
                     .then_inc(g.set_free[1], 1)
                    v.wait_ge(g.set_free[0], ii * 2 + (use_a[0] + par + 2))
                    v.wait_ge(g.set_free[1], ii * 2 + (use_a[1] + par + 2))
                    v.sem_inc(g.gt_used, 1)
                    v.scalar_tensor_tensor(g.mm[:, 0, :], t[:, 1, :], 0.25, t[:, 0, :], ALU.mult, ALU.add)\
                     .then_inc(g.m_ready, 1)
                    v.wait_ge(g.m_hi, ii * 2 + (par + 1))
                    v.tensor_tensor(g.hlo[:, bass.ds(ii * 2 + par, 1), :], g.mm[:, :, :],
                                    g.hhi[:, bass.ds(ii * 2 + par, 1), :].bitcast(F32),
                                    ALU.subtract).then_inc(g.m_split, 1)
                    v.wait_ge(g.m_split, ii * 2 + (par + 1))
            for n in range(DT):
                if n % (DT // 2) == 0:
                    v.wait_ge(g.x_back[n // (DT // 2)], 16)
                v.wait_ge(g.unit_done, uo + n + 1 + WSLOTS)
                v.scalar_tensor_tensor(blocks(g.x[:, n, :]), acc(g, n % 2), 0.5, blocks(g.x[:, n, :]),
                                       ALU.mult, ALU.add).then_inc(g.set_free[n % 2], 1)

        @block.tensor
        def _(pe):
            for n in range(WT):
                product(pe, g, 0, 0, u0 + n, WT, n % 2, use[n % 2] + n // 2, 0, part(g.zhi), part(g.zlo),
                        (g.z_split, lambda i, k: k + 1))
            with pe.Fori(0, DT) as i:
                product(pe, g, i, 2, ua, WT, 0, use_a[0], 1, part(g.yahi), part(g.yalo),
                        (g.ya_split, lambda i, k: k + 1))
                product(pe, g, i, 2, ua + 1, WT, 1, use_a[1], 1, part(g.ybhi), part(g.yblo),
                        (g.yb_split, lambda i, k: k + 1))
            with pe.Fori(0, DT // 2) as i:
                for j in range(2):
                    product(pe, g, i, 2, uo + j, DT, j, use_o[j], 1, part(g.hhi), part(g.hlo),
                            (g.m_split, lambda i, k: k + 1))

    g.units = uo + DT
    g.uses = [n + DT // 2 for n in use_o]


def build(nc, a, o):
    g = Ctx()
    plan(nc, g)
    plan_mid(nc, g)
    plan_s5(nc, g)
    plan_rwkv(nc, g)
    plan_sample(nc, g)
    plan_merge(nc, g)

    def dram(name, shape):
        return nc.dram_tensor(name, shape, F32, kind="Internal").ap()

    f_dram = dram("f_mixed", (RT, P, TOK))
    x_dram = dram("x_mid", (P, DT, TOK))
    gate_dram = dram("gates", (2 * DT, P, TOK))
    ya_dram = dram("ya", (P, WT, TOK))

    def first_loads(sp):
        sp.dma_start(g.x[:, :, :], a["x"]).then_inc(g.x_in, 16)
        sp.dma_start(g.ident[:, :], a["tabs"][:, T_ID, :]).then_inc(g.c_in, 16)
        sp.dma_start(g.seg[:, :], a["tabs"][:, T_SEG, :]).then_inc(g.c_in, 16)
        sp.dma_start(g.vec[:, :], a["vec"]).then_inc(g.c_in, 16)

    ffn_block(nc, g, a["ffn1_up"], a["ffn1_down"], V_G1,
              before={"sync": first_loads, "scalar": lambda act: act.wait_ge(g.x_in, 16)})
    proj_block(nc, g, a["w_mix"], a["shift"], f_dram, x_dram, o["last"])
    s5_block(nc, g, a["w_gates"], gate_dram, a["s5_b"], a["s5_c"], a["s5_x0"], o["s5_prompt"], o["s5_sample"])
    rwkv_block(nc, g, a["w_gates"], gate_dram, f_dram, a["tabs"], a["lora_up"], a["g_up"], a["lnx_w"], a["lnx_b"],
               ya_dram, o["wkv_prompt"])
    sample_block(nc, g, f_dram, a["wkv"], ya_dram, o["wkv_sample"])
    merge_block(nc, g, a["w_glu"], a["w_ab"], a["w_out"], ya_dram, gate_dram, x_dram)

    n1 = g.norms + 1
    use = [n + k + FT + len(FFN_GROUPS) * DT // 2 for k, n in zip((1, 0), g.uses)]

    def final_act(act):
        for j in range(2):
            act.wait_ge(g.set_free[j], use[j] + 1)
        norm_act(act, g, n1)

    def final_dve(v, st):
        norm_dve(v, g, st, n1)
        for k in range(DT):
            v.scalar_tensor_tensor(blocks(g.x[:, k, :]), blocks(g.x[:, k, :]), g.vec[:, V_GF + k:V_GF + k + 1],
                                   acc(g, 0), ALU.mult, ALU.mult).then_inc(g.y_ready, 1)

    def final_out(sp):
        for k in range(DT):
            sp.wait_ge(g.y_ready, k + 1)
            sp.dma_start(o["y"][:, k, :], g.x[:, k, :]).then_inc(g.out_done, 16)
        sp.wait_ge(g.out_done, 16 * DT)

    g.y_ready = nc.alloc_semaphore("y_ready")
    ffn_block(nc, g, a["ffn2_up"], a["ffn2_down"], V_G2,
              after={"sync": final_out, "scalar": final_act, "vector": final_dve,
                     "tensor": lambda pe: norm_pe(pe, g, n1, use[0])})


OUTPUTS = {"y": (P, DT, TOK), "last": (P, RT, NB + 1), "wkv_prompt": (P, 4, N), "wkv_sample": (P, 4 * NB, N),
           "s5_prompt": (P, 2, J), "s5_sample": (P, 2, J, NB)}


def tile_w(w):
    k, m = w.shape
    return w.reshape(k // P, P, m // P, P).transpose(2, 1, 0, 3).reshape(m // P, P, k)


def fold(v):
    return v.reshape(-1, P).T


def pairs(a):
    a = a.reshape(J, 2, N, *a.shape[2:])
    return a.transpose(1, 2, 0, *range(3, a.ndim)).reshape(P, J, *a.shape[3:])


def unpairs(a):
    a = a.reshape(2, N, J, *a.shape[2:])
    return a.transpose(2, 0, 1, *range(3, a.ndim)).reshape(2 * J, N, *a.shape[3:])


def kernel(x_prompt, x_sample, state_shift, state_wkv, state_s5_re, state_s5_im,
           g_ffn1, ffn1_gate, ffn1_up, ffn1_down, g_mix, w_in, mu_shift,
           w0, w_up, a0, a_up, g_up, k_k, k_a, r_k, lnx_w, lnx_b,
           A_re, A_im, log_dt, B_re, B_im, C_re, C_im, D_skip, w_glu,
           w_a_up, w_b_up, w_out, g_ffn2, ffn2_gate, ffn2_up, ffn2_down, g_final):
    from concourse import bacc as _bacc
    from concourse.bass_utils import run_bass_kernel_spmd

    A = np.asarray
    x = np.concatenate([A(x_prompt)[0], A(x_sample)[:, 0]], 0)
    win = A(w_in)[0]
    mix_cols = RT * P + UT * P
    vec = np.concatenate([
        fold(A(g_ffn1)[0]), fold(A(g_mix)[0]), fold(A(g_ffn2)[0]), fold(A(g_final)), fold(A(mu_shift)[0]),
        fold(A(w0)[0]), fold(A(a0)[0]), fold(A(k_k)[0]), fold(A(k_a)[0]), fold(A(r_k)[0].reshape(-1)),
        fold(A(D_skip)[0]), pairs(A(A_re)[0]), pairs(A(A_im)[0]),
        pairs(np.repeat(A(log_dt)[0][:, None], N, 1))], 1)

    def up(gate, w):
        return np.stack([tile_w(A(gate)[0]), tile_w(A(w)[0])], 1).reshape(2 * FT, P, D)

    data = {
        "x": x.T.reshape(DT, P, TOK).transpose(1, 0, 2),
        "tabs": make_tables(),
        "vec": vec,
        "shift": A(state_shift)[0].T.reshape(RT, P, NB).transpose(1, 0, 2),
        "wkv": A(state_wkv)[0].reshape(NB, 4, 2, N, N).transpose(2, 4, 1, 0, 3).reshape(P, 4 * NB, N),
        "ffn1_up": up(ffn1_gate, ffn1_up), "ffn1_down": tile_w(A(ffn1_down)[0]),
        "ffn2_up": up(ffn2_gate, ffn2_up), "ffn2_down": tile_w(A(ffn2_down)[0]),
        "w_mix": tile_w(win[:, :mix_cols]), "w_gates": tile_w(win[:, mix_cols:]),
        "lora_up": np.concatenate([A(w_up)[0], A(a_up)[0]], 0), "g_up": A(g_up)[0],
        "lnx_w": A(lnx_w)[0][None], "lnx_b": A(lnx_b)[0][None],
        "s5_b": np.stack([pairs(A(B_re)[0]), pairs(A(B_im)[0])], 1),
        "s5_c": np.stack([pairs(A(C_re)[0].transpose(0, 2, 1)), pairs(A(C_im)[0].transpose(0, 2, 1))], 1),
        "s5_x0": np.stack([pairs(A(s)[0].transpose(1, 2, 0)) for s in (state_s5_re, state_s5_im)], 1),
        "w_glu": tile_w(A(w_glu)[0]),
        "w_ab": np.stack([tile_w(A(w_a_up)[0]), tile_w(A(w_b_up)[0])], 1).reshape(2 * DT, P, W),
        "w_out": tile_w(A(w_out)[0]),
    }
    data = {n: np.ascontiguousarray(v) for n, v in data.items()}
    nc = _bacc.Bacc("TRN2", target_bir_lowering=False, num_devices=1)
    ins = {n: nc.dram_tensor(n, v.shape, F32, kind="ExternalInput").ap() for n, v in data.items()}
    outs = {n: nc.dram_tensor(n, s, F32, kind="ExternalOutput").ap() for n, s in OUTPUTS.items()}
    build(nc, ins, outs)
    nc.finalize()
    res = run_bass_kernel_spmd(nc, [data], core_ids=[0]).results[0]

    y = res["y"].transpose(1, 0, 2).reshape(D, TOK).T
    last = res["last"].transpose(1, 0, 2).reshape(RT * P, NB + 1).T
    wkv_p = res["wkv_prompt"].reshape(2, N, 4, N).transpose(2, 0, 3, 1).reshape(H, N, N)
    wkv_s = res["wkv_sample"].reshape(2, N, 4, NB, N).transpose(3, 2, 0, 4, 1).reshape(NB, H, N, N)
    s5_p = [unpairs(res["s5_prompt"][:, n]) for n in range(2)]
    s5_s = [unpairs(res["s5_sample"][:, n]).transpose(2, 0, 1) for n in range(2)]
    out = (y[None, :SEQ], y[SEQ:, None], last[None, 0:1], wkv_p[None, None], s5_p[0][None, None], s5_p[1][None, None],
           last[None, 1:], wkv_s[None], s5_s[0][None], s5_s[1][None])
    return tuple(np.ascontiguousarray(r) for r in out)
```

```python
import concourse.bass as bass
from concourse import mybir
import numpy as np

F32 = mybir.dt.float32
F32R = mybir.dt.float32r
I32 = mybir.dt.int32
ALU = mybir.AluOpType
ACT = mybir.ActivationFunctionType
AXX = mybir.AxisListType.X

P = 128
D = 1024
SEQ = 1024
NB = 8
TOK = SEQ + NB
DT = D // P
NBLK = 3
BLK = TOK // NBLK
FT = 2816 // P
FFN_GROUPS = (6, 6, 5, 5)
W = 512
WT = W // P
H = 8
N = 64
RT = 14
UT = 4
CH = 128
NCH = SEQ // CH
J = 16
SS = 86
NSS = TOK // SS
NORM_EPS = 1e-6
LNX_EPS = 64e-5
DECAY = float(np.exp(-0.5))

V_G1, V_GMIX, V_G2, V_GF = 0, 8, 16, 24
V_MU = 32
V_W0, V_A0, V_KK, V_KA, V_RK, V_DS = 46, 50, 54, 58, 62, 66
V_LR, V_LI, V_DT = 70, 86, 102
NVEC = 118

T_ID, T_STRICT, T_INCL, T_L0, T_L0T = 0, 1, 2, 3, 4
T_LEV = 5
T_SEG = 11
T_BLK = 12
T_IST = 13
NTAB = 14

WSLOTS = 2
RSQRT_MAGIC = float(0x5F3759DF)


class Ctx:
    pass


class Steps:

    def __init__(self, eng, sem, start=0):
        self.eng, self.sem, self.n, self.turn = eng, sem, start, 0

    def did(self, ins):
        ins.then_inc(self.sem, 1)
        self.n += 1
        return self.n

    def wait(self, n=None):
        self.eng.wait_ge(self.sem, self.turn + (self.n if n is None else n))

    def do(self, ins):
        self.did(ins)
        self.wait()

    def enter(self, i, per):
        self.first, self.per, self.turn = self.n, per, i * per

    def leave(self, turns):
        used = self.n - self.first
        assert used <= self.per, used
        if used < self.per:
            self.eng.sem_inc(self.sem, self.per - used)
        self.n, self.turn = self.first + self.per * turns, 0


def plan(nc, g):
    base = (nc.sbuf_base + 31) // 32 * 32
    g.limit = nc.sbuf_usable_end - base

    def at(name, off, shape, dt=F32):
        t = nc.alloc_sbuf_tensor_at(name, shape, dt, offset=base + off)
        return t, off + (int(np.prod(shape[1:])) * 4 + 31) // 32 * 32

    g.at = at
    o = 0
    g.wraw, o = at("wraw", o, [P, WSLOTS, 1024])
    g.whi_off = o
    g.whi, o = at("whi", o, [P, WSLOTS, 1024], F32R)
    g.wlo, o = at("wlo", o, [P, WSLOTS, 1024], F32R)
    g.vec, o = at("vec", o, [P, NVEC])
    g.ident, o = at("ident", o, [P, P])
    g.seg, o = at("seg", o, [P, P])
    g.small, o = at("small", o, [P, 6, 16])
    g.zero = g.small[:, 5, 0:1]
    g.hhi, o = at("hhi", o, [P, DT, TOK], F32R)
    g.hlo, o = at("hlo", o, [P, DT, TOK], F32R)
    g.h_end = o
    g.x, o = at("x", o, [P, DT, TOK])
    g.x_end = o
    ga = max(FFN_GROUPS)
    g.ahi, o = at("ahi", o, [P, ga, TOK], F32R)
    g.alo, o = at("alo", o, [P, ga, TOK], F32R)
    g.tmp, o = at("tmp", o, [P, 2, TOK])
    g.ssum, o = at("ssum", o, [P, TOK])
    assert o <= g.limit, (o, g.limit)
    g.ps = nc.alloc_psum_tensor("ps", [P, 8, 512], F32)

    S = nc.alloc_semaphore
    g.w_in = [S("weights_in0"), S("weights_in1")]
    g.w_hi = S("weights_hi")
    g.zero_set = S("zero_set")
    g.w_split = S("weights_split")
    g.unit_done = S("unit_done")
    g.set_free = [S("set_free0"), S("set_free1")]
    g.dve_s, g.act_s, g.pool_s = S("dve_steps"), S("act_steps"), S("pool_steps")
    g.x_in, g.c_in, g.out_done = S("x_in"), S("consts_in"), S("out_done")
    g.sq_ready, g.ssum_step, g.norm_ss = S("squares_ready"), S("square_sums"), S("norm_sums")
    g.rstd_ready, g.rstd_b = S("rstd_ready"), S("rstd_broadcast")
    g.hf_ready, g.hhi_ready, g.h_ready = S("h_full"), S("h_hi"), S("h_ready")
    g.silu_done, g.a_ready = S("silu_done"), S("a_ready")
    g.dve_n = g.act_n = g.pool_n = 0
    g.units = 0
    g.uses = [0, 0]
    g.norms = 0
    g.a_tiles = 0


def load_units(eng, g, u0, turns, per, kt, src):
    with eng.Fori(0, turns) as i:
        for j in range(per):
            eng.wait_ge(g.w_split, i * per + (u0 + j + 1))
            eng.dma_start(g.wraw[:, j % 2, 0:kt * P], src(i, j)).then_inc(g.w_in[j % 2], 16)


def split_units(pool, g, u0, turns, per, kt):
    n = kt * P
    with pool.Fori(0, turns) as i:
        for j in range(per):
            s = j % 2
            pool.wait_ge(g.w_in[s], i * (16 * per // 2) + 16 * ((u0 + j) // 2 + 1))
            pool.wait_ge(g.unit_done, i * per + (u0 + j + 1))
            pool.tensor_tensor(g.whi[:, s, 0:n], g.wraw[:, s, 0:n], g.zero.to_broadcast([P, n]),
                               ALU.add).then_inc(g.w_hi, 1)
            pool.wait_ge(g.w_hi, i * per + (u0 + j + 1))
            pool.tensor_tensor(g.wlo[:, s, 0:n], g.wraw[:, s, 0:n], g.whi[:, s, 0:n].bitcast(F32),
                               ALU.subtract).then_inc(g.w_split, 1)


def product(pe, g, i, per, u, kt, bank_set, use, uses_per, xhi, xlo, k_wait=None):
    s = u % 2
    pe.wait_ge(g.w_split, i * per + (u + 1 + WSLOTS))
    pe.wait_ge(g.set_free[bank_set], i * uses_per + (use + 1))
    for k in range(kt):
        if k_wait:
            pe.wait_ge(k_wait[0], k_wait[1](i, k))
        for w, x, first in ((g.whi, xhi, True), (g.whi, xlo, False), (g.wlo, xhi, False)):
            for b in range(NBLK):
                last = pe.matmul(g.ps[:, 3 * bank_set + b, 0:BLK], w[:, s, k * P:(k + 1) * P],
                                 x(k, b), start=(k == 0 and first),
                                 stop=(k == kt - 1 and w is g.wlo))
    last.then_inc(g.unit_done, 1)


def acc(g, bank_set):
    return g.ps[:, 3 * bank_set:3 * bank_set + 3, 0:BLK]


def blocks(ap):
    return ap.rearrange("p (b t) -> p b t", b=NBLK)


def rsqrt(v, st, y, x, t, scale, eps, floor=None):
    if floor is None:
        st.do(v.tensor_scalar(x, x, scale, eps, ALU.mult, ALU.add))
    else:
        st.do(v.tensor_scalar(x, x, scale, floor, ALU.mult, ALU.max))
    st.do(v.tensor_scalar(t.bitcast(I32), x.bitcast(I32), 1, None, ALU.logical_shift_right))
    st.do(v.tensor_scalar(y.bitcast(I32), t.bitcast(I32), -1.0, RSQRT_MAGIC, ALU.mult, ALU.add))
    for _ in range(4):
        st.do(v.scalar_tensor_tensor(t, y, -0.5, y, ALU.mult, ALU.mult))
        st.do(v.tensor_tensor(t, t, x, ALU.mult))
        st.do(v.scalar_tensor_tensor(y, t, 1.5, y, ALU.add, ALU.mult))


def norm_act(act, g, n):
    for k in range(DT):
        if k >= 2:
            act.wait_ge(g.ssum_step, DT * n + k - 1)
        act.activation(g.tmp[:, k % 2, :], g.x[:, k, :], ACT.Square).then_inc(g.sq_ready, 1)


def norm_pe(pe, g, n, use):
    pe.wait_ge(g.ssum_step, DT * (n + 1))
    pe.wait_ge(g.set_free[0], use + 1)
    for j in range(NSS):
        last = pe.matmul(g.ps[0:SS, 6, j:j + 1], g.ssum[:, j * SS:(j + 1) * SS], g.seg[:, 2:3],
                         start=True, stop=True)
    last.then_inc(g.norm_ss, 1)
    pe.wait_ge(g.rstd_ready, n + 1)
    for j in range(NSS):
        last = pe.matmul(g.ps[:, j // 4, (j % 4) * SS:(j % 4 + 1) * SS],
                         g.small[0:SS, 1, j:j + 1].to_broadcast([SS, P]), g.ident[0:SS, 0:SS],
                         start=True, stop=True)
    last.then_inc(g.rstd_b, 1)


def norm_dve(v, g, st, n):
    for k in range(DT):
        v.wait_ge(g.sq_ready, DT * n + k + 1)
        if k == 0:
            v.tensor_copy(g.ssum[:, :], g.tmp[:, 0, :]).then_inc(g.ssum_step, 1)
        else:
            v.wait_ge(g.ssum_step, DT * n + k)
            v.tensor_tensor(g.ssum[:, :], g.ssum[:, :], g.tmp[:, k % 2, :], ALU.add)\
                .then_inc(g.ssum_step, 1)
    v.wait_ge(g.norm_ss, n + 1)
    x, y, t = (g.small[0:SS, a, 0:NSS] for a in range(3))
    st.do(v.tensor_copy(x, g.ps[0:SS, 6, 0:NSS]))
    rsqrt(v, st, y, x, t, 1.0 / D, NORM_EPS)
    v.sem_inc(g.rstd_ready, 1)
    v.wait_ge(g.rstd_b, n + 1)


def h_dve(v, g, gcol, n):

    def low(k):
        v.wait_ge(g.hhi_ready, DT * n + k + 1)
        v.tensor_tensor(g.hlo[:, k, :], g.tmp[:, k % 2, :], g.hhi[:, k, :].bitcast(F32),
                        ALU.subtract).then_inc(g.h_ready, 1)

    for k in range(DT):
        if k >= 2:
            v.wait_ge(g.h_ready, DT * n + k - 1)
        ins = v.scalar_tensor_tensor(blocks(g.tmp[:, k % 2, :]), blocks(g.x[:, k, :]),
                                     g.vec[:, gcol + k:gcol + k + 1], acc(g, 0), ALU.mult, ALU.mult)
        ins.then_inc(g.hf_ready, 1)
        v.wait_ge(g.hf_ready, DT * n + k + 1)
        if k == DT - 1:
            v.sem_inc(g.set_free[0], 1)
        if k:
            low(k - 1)
    low(DT - 1)


def h_act(act, g, n):
    for k in range(DT):
        act.wait_ge(g.hf_ready, DT * n + k + 1)
        act.activation(g.hhi[:, k, :], g.tmp[:, k % 2, :], ACT.Copy).then_inc(g.hhi_ready, 1)


def ffn_block(nc, g, w_up, w_down, gcol, before=None, after=None):
    u0, s0, a0, n0 = g.units, list(g.uses), g.a_tiles, g.norms
    s0[0] += 1

    def groups():
        u, a, k0, use = u0, a0, 0, s0[0]
        use1 = s0[1]
        for size in FFN_GROUPS:
            yield size, k0, u, a, use, use1
            u, a, k0 = u + 2 * size + DT, a + size, k0 + size
            use, use1 = use + size + DT // 2, use1 + size + DT // 2

    with nc.Block() as block:
        @block.sync
        def _(sp):
            if before:
                before["sync"](sp)
            for size, k0, u, a, use, use1 in groups():
                load_units(sp, g, u, size, 2, DT,
                           lambda i, j: w_up[bass.ds(i * 2 + (2 * k0 + j), 1), :, :].rearrange("a p k -> p (a k)"))
                load_units(sp, g, u + 2 * size, DT // 2, 2, size,
                           lambda i, j: w_down[bass.ds(i * 2 + j, 1), :, k0 * P:(k0 + size) * P].rearrange("a p k -> p (a k)"))
            if after:
                after["sync"](sp)

        @block.gpsimd
        def _(pool):
            if before:
                pool.sem_inc(g.w_split, WSLOTS)
                pool.memset(g.zero, 0.0).then_inc(g.zero_set, 1)
                pool.wait_ge(g.zero_set, 1)
            for size, k0, u, a, use, use1 in groups():
                split_units(pool, g, u, size, 2, DT)
                split_units(pool, g, u + 2 * size, DT // 2, 2, size)

        @block.scalar
        def _(act):
            if before:
                before["scalar"](act)
            norm_act(act, g, n0)
            h_act(act, g, n0)
            for size, k0, u, a, use, use1 in groups():
                with act.Fori(0, size) as i:
                    act.wait_ge(g.unit_done, i * 2 + (u + 1 + WSLOTS))
                    act.wait_ge(g.set_free[1], i + (use1 + 1))
                    act.activation(blocks(g.tmp[:, 0, :]), acc(g, 0), ACT.Silu)\
                       .then_inc(g.set_free[0], 1)
            if after:
                after["scalar"](act)

        @block.vector
        def _(v):
            st = Steps(v, g.dve_s, g.dve_n)
            norm_dve(v, g, st, n0)
            h_dve(v, g, gcol, n0)
            for size, k0, u, a, use, use1 in groups():
                with v.Fori(0, size) as i:
                    v.wait_ge(g.set_free[0], i + (use + 2))
                    v.wait_ge(g.unit_done, i * 2 + (u + 2 + WSLOTS))
                    v.tensor_tensor(blocks(g.tmp[:, 1, :]), acc(g, 1), blocks(g.tmp[:, 0, :]),
                                    ALU.mult).then_inc(g.set_free[1], 1)
                    v.wait_ge(g.set_free[1], i + (use1 + 2))
                    st.enter(i, 1)
                    st.do(v.tensor_copy(g.ahi[:, bass.ds(i, 1), :], g.tmp[:, 1:2, :]))
                    v.tensor_tensor(g.alo[:, bass.ds(i, 1), :], g.tmp[:, 1:2, :],
                                    g.ahi[:, bass.ds(i, 1), :].bitcast(F32),
                                    ALU.subtract).then_inc(g.a_ready, 1)
                    v.wait_ge(g.a_ready, i + (a + 1))
                st.leave(size)
                ud = u + 2 * size
                with v.Fori(0, DT // 2) as i:
                    for j in range(2):
                        v.wait_ge(g.unit_done, i * 2 + (ud + j + 1 + WSLOTS))
                        xt = g.x[:, bass.ds(i * 2 + j, 1), :].rearrange("p a (b t) -> p (a b) t", b=NBLK)
                        v.scalar_tensor_tensor(xt, acc(g, j), 0.5, xt, ALU.mult, ALU.add)\
                            .then_inc(g.set_free[j], 1)
            if after:
                after["vector"](v, st)
            g.dve_end = st.n

        @block.tensor
        def _(pe):
            if before:
                pe.sem_inc(g.unit_done, WSLOTS)
                pe.sem_inc(g.set_free[0], 1)
                pe.sem_inc(g.set_free[1], 1)
                pe.wait_ge(g.c_in, 16 * 3)
            norm_pe(pe, g, n0, s0[0] - 1)
            for size, k0, u, a, use, use1 in groups():
                with pe.Fori(0, size) as i:
                    for j in range(2):
                        product(pe, g, i, 2, u + j, DT, j, (use, use1)[j], 1,
                                lambda k, b: g.hhi[:, k, b * BLK:(b + 1) * BLK],
                                lambda k, b: g.hlo[:, k, b * BLK:(b + 1) * BLK],
                                (g.h_ready, lambda i, k: DT * n0 + k + 1) if k0 == 0 else None)
                with pe.Fori(0, DT // 2) as i:
                    for j in range(2):
                        product(pe, g, i, 2, u + 2 * size + j, size, j, (use, use1)[j] + size, 1,
                                lambda k, b: g.ahi[:, k, b * BLK:(b + 1) * BLK],
                                lambda k, b: g.alo[:, k, b * BLK:(b + 1) * BLK],
                                (g.a_ready, lambda i, k: a + k + 1))
            if after:
                after["tensor"](pe)

    g.units = u0 + 2 * FT + len(FFN_GROUPS) * DT
    g.uses = [s0[0] + FT + len(FFN_GROUPS) * DT // 2, s0[1] + FT + len(FFN_GROUPS) * DT // 2]
    g.a_tiles, g.norms, g.dve_n = a0 + FT, n0 + 1, g.dve_end


def plan_mid(nc, g):
    g.u = g.at("u", g.limit // 32 * 32 - UT * TOK * 4, [P, UT, TOK])[0]
    g.u_off = g.limit // 32 * 32 - UT * TOK * 4
    o = g.x_end
    g.raw, o = g.at("fraw", o, [P, 2, TOK + 8])
    g.mix, o = g.at("fmix", o, [P, 2, TOK])
    g.shift, o = g.at("shift", o, [P, RT, NB])
    g.last, o = g.at("last", o, [P, RT, NB + 1])
    assert o <= g.u_off
    S = nc.alloc_semaphore
    g.sh_in, g.raw_ready, g.mix_ready, g.mix_out = S("shift_in"), S("raw_ready"), S("mix_ready"), [S("mix_out0"), S("mix_out1")]
    g.diff_ready, g.last_ready, g.x_out, g.last_out = S("diff_ready"), S("last_ready"), S("x_out"), S("last_out")
    g.zero_ready = S("zero_ready")
    g.ucopy = S("u_ready")


def proj_block(nc, g, w_in, shift, f_dram, x_dram, last_out):
    u0, n0 = g.units, g.norms
    use = [g.uses[0] + 1, g.uses[1]]
    HALF = RT // 2

    with nc.Block() as block:
        @block.sync
        def _(sp):
            sp.dma_start(g.shift[:, :, :], shift).then_inc(g.sh_in, 16)
            load_units(sp, g, u0, HALF + UT // 2, 2, DT,
                       lambda i, j: w_in[bass.ds(i * 2 + j, 1), :, :].rearrange("a p k -> p (a k)"))
            sp.wait_ge(g.last_ready, RT)
            sp.dma_start(last_out, g.last[:, :, :]).then_inc(g.last_out, 16)
            sp.wait_ge(g.last_out, 16)
            sp.wait_ge(g.x_out, 16)
            for j in range(2):
                sp.wait_ge(g.mix_out[j], 16 * (HALF + 1))

        @block.gpsimd
        def _(pool):
            split_units(pool, g, u0, HALF + UT // 2, 2, DT)

        @block.scalar
        def _(act):
            act.dma_start(x_dram, g.x[:, :, :]).then_inc(g.x_out, 16)
            act.sem_inc(g.mix_out[0], 16)
            act.sem_inc(g.mix_out[1], 16)
            norm_act(act, g, n0)
            h_act(act, g, n0)
            act.wait_ge(g.zero_ready, 2)
            act.wait_ge(g.h_ready, DT * (n0 + 1))
            with act.Fori(0, HALF) as i:
                for j in range(2):
                    act.wait_ge(g.unit_done, i * 2 + (u0 + j + 1 + WSLOTS))
                    act.wait_ge(g.mix_ready, i * 2 + (j + 1))
                    act.activation(blocks(g.raw[:, j, 8:8 + TOK]), acc(g, j), ACT.Copy)\
                       .then_inc(g.set_free[j], 1)
                    act.wait_ge(g.set_free[j], i + (use[j] + 2))
                    act.activation(g.last[:, bass.ds(i * 2 + j, 1), :],
                                   g.raw[:, j:j + 1, 7 + SEQ:8 + TOK], ACT.Copy).then_inc(g.last_ready, 1)
                    act.wait_ge(g.mix_ready, i * 2 + (j + 3))
                    act.dma_start(f_dram[bass.ds(i * 2 + j, 1), :, :].rearrange("a p k -> p (a k)"),
                                  g.mix[:, j, :]).then_inc(g.mix_out[j], 16)
            for n in range(UT):
                j = n % 2
                act.wait_ge(g.unit_done, u0 + RT + n + 1 + WSLOTS)
                act.activation(blocks(g.u[:, n, :]), acc(g, j), ACT.Copy).then_inc(g.set_free[j], 1)

        @block.vector
        def _(v):
            st = Steps(v, g.dve_s, g.dve_n)
            for j in range(2):
                v.memset(g.raw[:, j, 7:8], 0.0).then_inc(g.zero_ready, 1)
            norm_dve(v, g, st, n0)
            h_dve(v, g, V_GMIX, n0)
            v.sem_inc(g.mix_ready, 2)
            v.wait_ge(g.sh_in, 16)
            with v.Fori(0, HALF) as i:
                for j in range(2):
                    r = g.raw[:, j, :]
                    v.wait_ge(g.set_free[j], i + (use[j] + 2))
                    v.wait_ge(g.last_ready, i * 2 + (j + 1))
                    v.wait_ge(g.mix_out[j], i * 16 + 16)
                    v.tensor_tensor(g.mix[:, j, 0:SEQ], r[:, 7:7 + SEQ], r[:, 8:8 + SEQ],
                                    ALU.subtract).then_inc(g.diff_ready, 1)
                    v.tensor_tensor(g.mix[:, j:j + 1, SEQ:TOK], g.shift[:, bass.ds(i * 2 + j, 1), :],
                                    g.raw[:, j:j + 1, 8 + SEQ:8 + TOK], ALU.subtract).then_inc(g.diff_ready, 1)
                    v.wait_ge(g.diff_ready, i * 4 + (2 * j + 2))
                    v.scalar_tensor_tensor(g.mix[:, j, :], g.mix[:, j, :],
                                           g.vec[:, bass.ds(i * 2 + (V_MU + j), 1)],
                                           r[:, 8:8 + TOK], ALU.mult, ALU.add).then_inc(g.mix_ready, 1)
            g.dve_end = st.n

        @block.tensor
        def _(pe):
            norm_pe(pe, g, n0, use[0] - 1)
            with pe.Fori(0, HALF + UT // 2) as i:
                for j in range(2):
                    product(pe, g, i, 2, u0 + j, DT, j, use[j], 1,
                            lambda k, b: g.hhi[:, k, b * BLK:(b + 1) * BLK],
                            lambda k, b: g.hlo[:, k, b * BLK:(b + 1) * BLK],
                            (g.h_ready, lambda i, k: DT * n0 + k + 1))

    g.units, g.norms, g.dve_n = u0 + RT + UT, n0 + 1, g.dve_end
    g.uses = [use[0] + HALF + UT // 2, use[1] + HALF + UT // 2]


def gate_products(pe, g, i, banks=2):
    u, m = g.units, g.gates * NBLK
    pe.wait_ge(g.w_split, i * 2 + (u + 2 + WSLOTS))
    for b in range(NBLK):
        pe.wait_ge(g.gate_free, i * NBLK + (m + b + ((2, 1, 1)[b] if banks == 2 else 2)))
        for k in range(DT):
            s, kk = k // 4, k % 4
            for w, x in ((g.whi, g.hhi), (g.whi, g.hlo), (g.wlo, g.hhi)):
                last = pe.matmul(g.ps[:, b % banks, 0:BLK], w[:, s, kk * P:(kk + 1) * P],
                                 x[:, k, b * BLK:(b + 1) * BLK],
                                 start=(k == 0 and w is g.whi and x is g.hhi),
                                 stop=(k == DT - 1 and w is g.wlo))
                if k < DT - 1 or w is g.whi:
                    yield
        last.then_inc(g.gate_done, 1)
        yield
    pe.wait_ge(g.gate_done, i * NBLK + (m + NBLK))
    pe.sem_inc(g.unit_done, 2)


def run(ops, n):
    for _ in range(n):
        next(ops, None)


def gate_take(act, g, i, b, banks=2):
    m = g.gates * NBLK
    if b == 0:
        act.wait_ge(g.gate_out, i * 16 + (g.gates + 1) * 16)
    act.wait_ge(g.gate_done, i * NBLK + (m + b + 1))
    act.activation(g.gout[:, b * BLK:(b + 1) * BLK], g.ps[:, b % banks, 0:BLK], ACT.Tanh, scale=0.5)\
       .then_inc(g.gate_free, 1)


def gate_stream(sp, g, w_gate, gate_dram):
    u, m = g.units, g.gates * NBLK
    with sp.Fori(0, NCH) as i:
        for j in range(2):
            sp.wait_ge(g.w_split, i * 2 + (u + j + 1))
            sp.dma_start(g.wraw[:, j, 0:4 * P],
                         w_gate[bass.ds(i + g.gates, 1), :, j * 4 * P:(j + 1) * 4 * P].rearrange("a p k -> p (a k)"))\
              .then_inc(g.w_in[j], 16)
        sp.wait_ge(g.gate_free, i * NBLK + (m + NBLK + 2))
        sp.dma_start(gate_dram[bass.ds(i + g.gates, 1), :, :].rearrange("a p k -> p (a k)"), g.gout[:, :])\
          .then_inc(g.gate_out, 16)


def gates_done(g):
    g.units += 2 * NCH
    g.gates += NCH


def plan_s5(nc, g):
    o = g.x_off = g.h_end
    g.s5c, o = g.at("s5_cos", o, [P, J, CH])
    g.s5s, o = g.at("s5_sin", o, [P, J, CH])
    g.BT = []
    g.CT = []
    for n in range(2):
        t, o = g.at(f"s5_b{n}", o, [P, J, P]); g.BT.append(t)
    for n in range(2):
        t, o = g.at(f"s5_c{n}", o, [P, J, 32]); g.CT.append(t)
    g.rot, o = g.at("s5_rot", o, [P, 4, 4, 4, CH])
    g.z, o = g.at("s5_z", o, [P, 2, 2, 4, CH])
    g.xs, o = g.at("s5_x", o, [P, 2, 2, 4, CH])
    g.uc, o = g.at("s5_u", o, [P, UT, CH])
    g.gout, o = g.at("gate_out_s", o, [P, TOK])
    g.xl, o = g.at("s5_last", o, [P, 2, J])
    g.par, o = g.at("s5_par", o, [P, 12, J])
    assert o <= g.u_off, (o, g.u_off)
    off = g.x_off + 2 * J * CH * 4 + 2 * J * P * 4 + 2 * J * 32 * 4
    g.braw, off = g.at("b_raw", off, [P, 2, J, 16])
    g.bbar, off = g.at("b_bar", off, [P, 2, J, 16])
    g.bm, off = g.at("b_masked", off, [P, 2, J, 32])
    g.craw, off = g.at("c_raw", off, [P, 2, J, 16])
    g.stm, off = g.at("s5_tmp", off, [P, 4, J, P // 2])
    g.x0, off = g.at("s5_x0", g.x_off + 2 * J * CH * 4 + 2 * J * P * 4 + 2 * J * 32 * 4, [P, 2, J, NB])
    g.x1, off = g.at("s5_x1", off, [P, 2, J, NB])
    g.xt, off = g.at("s5_xt", off, [P, 2, J, NB])
    S = nc.alloc_semaphore
    g.gate_free, g.gate_done, g.gate_out = S("gate_free"), S("gate_done"), S("gate_out")
    g.s5_in, g.s5_fwd, g.s5_tr, g.s5_bt = S("s5_in"), S("s5_bbar"), S("s5_transposed"), S("s5_set_up")
    g.uc_ready, g.bu_done, g.bu_free = S("s5_u_ready"), S("s5_bu_done"), S("s5_bu_free")
    g.rin, g.w_ready, g.z_ready, g.xc_ready, g.c_done = (S("s5_turned"), S("s5_w"), S("s5_z_ready"),
                                                         S("s5_x_ready"), S("s5_c_done"))
    g.y_free, g.x0_in, g.xs_ready, g.s5_out = S("s5_y_taken"), S("s5_x0_in"), S("s5_xs"), S("s5_out")
    g.s5_zero = S("s5_zero")
    g.gates = 0


def s5_exp(v, st, y, x, a, b):
    st.do(v.tensor_scalar(a, x, float(1 / np.log(2)), None, ALU.mult))
    st.do(v.tensor_scalar(a, a, 12582912.0, None, ALU.add))
    st.do(v.tensor_scalar(a, a, -12582912.0, None, ALU.add))
    st.do(v.scalar_tensor_tensor(b, a, -0.693359375, x, ALU.mult, ALU.add))
    st.do(v.scalar_tensor_tensor(b, a, 2.12194440e-4, b, ALU.mult, ALU.add))
    st.do(v.tensor_scalar(y, b, 1.0 / 9, 1.0, ALU.mult, ALU.add))
    for n in range(8, 0, -1):
        st.do(v.scalar_tensor_tensor(y, y, 1.0 / n, b, ALU.mult, ALU.mult))
        st.do(v.tensor_scalar(y, y, 1.0, None, ALU.add))
    st.do(v.tensor_scalar(b.bitcast(I32), a, float(1 << 23), float(127 << 23), ALU.mult, ALU.add))
    st.do(v.tensor_tensor(y, y, b, ALU.mult))


def s5_sincos(v, st, s, c, x, a, b):
    st.do(v.tensor_scalar(a, x, float(1 / (2 * np.pi)), None, ALU.mult))
    st.do(v.tensor_scalar(a, a, 12582912.0, None, ALU.add))
    st.do(v.tensor_scalar(a, a, -12582912.0, None, ALU.add))
    c1 = 6.28125
    c2 = float(np.float32(np.round((2 * np.pi - c1) * 2 ** 20) / 2 ** 20))
    c3 = float(2 * np.pi - c1 - c2)
    st.do(v.scalar_tensor_tensor(b, a, -c1, x, ALU.mult, ALU.add))
    st.do(v.scalar_tensor_tensor(b, a, -c2, b, ALU.mult, ALU.add))
    st.do(v.scalar_tensor_tensor(b, a, -c3, b, ALU.mult, ALU.add))
    st.do(v.tensor_scalar(b, b, 0.25, None, ALU.mult))
    st.do(v.tensor_tensor(a, b, b, ALU.mult))
    for y, divs in ((s, (110, 72, 42, 20, 6)), (c, (90, 56, 30, 12, 2))):
        st.do(v.tensor_scalar(y, a, -1.0 / divs[0], 1.0, ALU.mult, ALU.add))
        for n in divs[1:]:
            st.do(v.scalar_tensor_tensor(y, y, -1.0 / n, a, ALU.mult, ALU.mult))
            st.do(v.tensor_scalar(y, y, 1.0, None, ALU.add))
    st.do(v.tensor_tensor(s, s, b, ALU.mult))
    for _ in range(2):
        st.do(v.tensor_tensor(b, s, s, ALU.mult))
        st.do(v.scalar_tensor_tensor(s, s, 2.0, c, ALU.mult, ALU.mult))
        st.do(v.tensor_scalar(c, b, -2.0, 1.0, ALU.mult, ALU.add))


def cmul(v, st, outr, outi, ar, ai, br, bi, t0, t1):
    st.do(v.tensor_tensor(t0, ar, br, ALU.mult))
    st.do(v.tensor_tensor(t1, ai, bi, ALU.mult))
    st.do(v.tensor_tensor(outr, t0, t1, ALU.subtract))
    st.do(v.tensor_tensor(t0, ar, bi, ALU.mult))
    st.do(v.tensor_tensor(t1, ai, br, ALU.mult))
    st.do(v.tensor_tensor(outi, t0, t1, ALU.add))


def s5_setup_dve(v, g, st):
    par = [g.par[:, n, :] for n in range(12)]
    dt, m, th, s, c, a, b, abr, abi, qr, qi, den = par
    lr, li, ldt = (g.vec[:, o:o + J] for o in (V_LR, V_LI, V_DT))
    s5_exp(v, st, dt, ldt, a, b)
    st.do(v.tensor_tensor(th, li, dt, ALU.mult))
    st.do(v.tensor_tensor(den, lr, dt, ALU.mult))
    s5_exp(v, st, m, den, a, b)
    s5_sincos(v, st, s, c, th, a, b)
    st.do(v.tensor_tensor(abr, m, c, ALU.mult))
    st.do(v.tensor_tensor(abi, m, s, ALU.mult))
    st.do(v.tensor_tensor(den, lr, lr, ALU.mult))
    st.do(v.tensor_tensor(a, li, li, ALU.mult))
    st.do(v.tensor_tensor(den, den, a, ALU.add))
    st.do(v.reciprocal(den, den))
    st.do(v.tensor_scalar(a, abr, -1.0, None, ALU.add))
    st.do(v.tensor_tensor(qr, a, lr, ALU.mult))
    st.do(v.tensor_tensor(b, abi, li, ALU.mult))
    st.do(v.tensor_tensor(qr, qr, b, ALU.add))
    st.do(v.tensor_tensor(qr, qr, den, ALU.mult))
    st.do(v.tensor_tensor(qi, abi, lr, ALU.mult))
    st.do(v.tensor_tensor(b, a, li, ALU.mult))
    st.do(v.tensor_tensor(qi, qi, b, ALU.subtract))
    st.do(v.tensor_tensor(qi, qi, den, ALU.mult))
    v.wait_ge(g.s5_in, 16 * 2)
    full = lambda x: x.unsqueeze(2).to_broadcast([P, J, 16])
    cmul(v, st, g.bbar[:, 0], g.bbar[:, 1], full(qr), full(qi), g.braw[:, 0], g.braw[:, 1],
         g.stm[:, 0, :, 0:16], g.stm[:, 1, :, 0:16])
    st.do(v.memset(g.bm[:, :, :, :], 0.0))
    for n in range(2):
        st.do(v.memset(g.BT[n][:, :, :], 0.0))
        st.do(v.memset(g.CT[n][:, :, :], 0.0))
        for q in range(2):
            rows = slice(64 * q, 64 * q + 64)
            st.do(v.tensor_copy(g.bm[rows, n, :, 16 * q:16 * q + 16], g.bbar[rows, n]))
            st.do(v.tensor_scalar(g.CT[n][rows, :, 16 * q:16 * q + 16], g.craw[rows, n], 1.0 - 2 * n, None, ALU.mult))
    v.sem_inc(g.s5_fwd, 1)
    st.do(v.tensor_copy(g.s5c[:, :, 0:1], c.unsqueeze(2)))
    st.do(v.tensor_copy(g.s5s[:, :, 0:1], s.unsqueeze(2)))
    n = 1
    while n < CH:
        er, ei = (t[:, :, n - 1:n].to_broadcast([P, J, n]) for t in (g.s5c, g.s5s))
        cmul(v, st, g.s5c[:, :, n:2 * n], g.s5s[:, :, n:2 * n], g.s5c[:, :, 0:n], g.s5s[:, :, 0:n],
             er, ei, g.stm[:, 0, :, 0:n], g.stm[:, 1, :, 0:n])
        n *= 2
    v.wait_ge(g.s5_tr, 1)
    for n in range(2):
        for q in range(4):
            rows = slice(32 * q, 32 * q + 32)
            st.do(v.tensor_copy(g.BT[n][rows, q:J:4, :],
                                g.ps[rows, 2 + n, :].rearrange("p (t c) -> p t c", t=4)))
    st.do(v.memset(g.xl[:, :, :], 0.0))
    v.sem_inc(g.s5_bt, 1)


def s5_block(nc, g, w_gate, gate_dram, b_in, c_in, x0_in, s5p_out, s5s_out):
    per_x = UT

    with nc.Block() as block:
        @block.sync
        def _(sp):
            sp.dma_start(g.braw[:, :, :, :], b_in).then_inc(g.s5_in, 16)
            sp.dma_start(g.craw[:, :, :, :], c_in).then_inc(g.s5_in, 16)
            gate_stream(sp, g, w_gate, gate_dram)
            sp.wait_ge(g.xc_ready, UT * NCH + 2)
            sp.dma_start(g.x0[:, :, :, :], x0_in).then_inc(g.x0_in, 16)
            sp.dma_start(s5p_out, g.xl[:, :, :]).then_inc(g.s5_out, 16)
            sp.wait_ge(g.xs_ready, 1)
            sp.dma_start(s5s_out, g.x1[:, :, :, :]).then_inc(g.s5_out, 16)
            sp.wait_ge(g.s5_out, 32)
            sp.wait_ge(g.gate_out, 16 * (g.gates + NCH + 1))

        @block.gpsimd
        def _(pool):
            st = Steps(pool, g.pool_s, g.pool_n)

            def w_piece(i, p):
                t = [g.rot[:, p, n].rearrange("p a c -> p (a c)") for n in range(4)]
                z = [g.z[:, n, p % 2].rearrange("p a c -> p (a c)") for n in range(2)]
                pool.wait_ge(g.rin, i * 4 + (p + 1))
                pool.wait_ge(g.xc_ready, i * 4 + (p + 1))
                st.do(pool.tensor_tensor(z[0], t[0], t[1], ALU.add))
                pool.tensor_tensor(z[1], t[2], t[3], ALU.subtract).then_inc(g.w_ready, 1)

            def x_piece(i, p):
                t = [g.rot[:, p, n].rearrange("p a c -> p (a c)") for n in range(4)]
                z = [g.z[:, n, p % 2].rearrange("p a c -> p (a c)") for n in range(2)]
                x = [g.xs[:, n, p % 2].rearrange("p a c -> p (a c)") for n in range(2)]
                cos, sin = (t_[:, 4 * p:4 * p + 4, :].rearrange("p a c -> p (a c)") for t_ in (g.s5c, g.s5s))
                pool.wait_ge(g.z_ready, i * 4 + (p + 1))
                st.do(pool.tensor_tensor(t[1], sin, z[1], ALU.mult))
                st.do(pool.tensor_tensor(t[3], cos, z[1], ALU.mult))
                pool.wait_ge(g.c_done, i * 4 + (p + 1))
                st.do(pool.tensor_tensor(x[0], t[0], t[1], ALU.subtract))
                st.do(pool.tensor_tensor(x[1], t[2], t[3], ALU.add))
                pool.tensor_tensor(g.xl[:, :, 4 * p:4 * p + 4], g.xs[:, :, p % 2, :, CH - 1],
                                   g.zero.unsqueeze(2).to_broadcast([P, 2, 4]), ALU.add)\
                    .then_inc(g.xc_ready, 1)

            pool.sem_inc(g.xc_ready, 2)
            pool.wait_ge(g.s5_bt, 1)
            u0 = g.units
            w_piece(0, 0)
            w_piece(0, 1)

            def turn(i, more):
                split_turn(pool, g, i, u0, 4)
                x_piece(i, 0)
                w_piece(i, 2)
                x_piece(i, 1)
                w_piece(i, 3)
                x_piece(i, 2)
                if more:
                    w_piece(i + 1, 0)
                x_piece(i, 3)
                if more:
                    w_piece(i + 1, 1)

            with pool.Fori(0, NCH - 1) as i:
                st.enter(i, 24)
                turn(i, True)
                st.leave(NCH - 1)
            turn(NCH - 1, False)
            g.pool_end = st.n

        @block.scalar
        def _(act):
            act.sem_inc(g.gate_free, 2)
            act.sem_inc(g.gate_out, 16)
            act.wait_ge(g.s5_bt, 1)
            act.activation(g.uc[:, :, :], g.u[:, :, 0:CH], ACT.Copy).then_inc(g.uc_ready, 1)

            def turn(i, more):
                gate_take(act, g, i, 0)
                if more:
                    act.wait_ge(g.bu_done, i * 4 + 8)
                    act.activation(g.uc[:, :, :], g.u[:, :, bass.ds(i * CH + CH, CH)], ACT.Copy)\
                       .then_inc(g.uc_ready, 1)
                gate_take(act, g, i, 1)
                gate_take(act, g, i, 2)

            with act.Fori(0, NCH - 1) as i:
                turn(i, True)
            turn(NCH - 1, False)
            act.wait_ge(g.bu_done, NCH * 4 + 4)
            act.activation(g.uc[:, :, 0:NB], g.u[:, :, SEQ:TOK], ACT.Copy).then_inc(g.uc_ready, 1)

        @block.vector
        def _(v):
            st = Steps(v, g.dve_s, g.dve_n)
            s5_setup_dve(v, g, st)
            v.sem_inc(g.bu_free, 2)
            v.sem_inc(g.y_free, 1)

            def turn_in(i, p):
                t = [g.rot[:, p, n].rearrange("p a c -> p (a c)") for n in range(4)]
                cos, sin = (t_[:, 4 * p:4 * p + 4, :].rearrange("p a c -> p (a c)") for t_ in (g.s5c, g.s5s))
                br, bi = g.ps[:, 2 + 2 * (p % 2), :], g.ps[:, 3 + 2 * (p % 2), :]
                v.wait_ge(g.bu_done, i * 4 + (p + 5))
                if not isinstance(i, int) or i > 0:
                    v.wait_ge(g.xc_ready, i * 4 + (p - 1))
                st.do(v.tensor_tensor(t[0], cos, br, ALU.mult))
                st.do(v.tensor_tensor(t[1], sin, bi, ALU.mult))
                st.do(v.tensor_tensor(t[2], cos, bi, ALU.mult))
                st.do(v.tensor_tensor(t[3], sin, br, ALU.mult))
                v.sem_inc(g.bu_free, 1)
                v.sem_inc(g.rin, 1)

            def scans(i, p):
                t = [g.rot[:, p, n].rearrange("p a c -> p (a c)") for n in range(4)]
                cos, sin = (t_[:, 4 * p:4 * p + 4, :].rearrange("p a c -> p (a c)") for t_ in (g.s5c, g.s5s))
                v.wait_ge(g.w_ready, i * 4 + (p + 1))
                for n in range(2):
                    for a in range(4):
                        zt = g.z[:, n, p % 2, a, :]
                        st.did(v.tensor_tensor_scan(zt, g.par[:, 1, 4 * p + a:4 * p + a + 1].to_broadcast([P, CH]), zt,
                                                    g.xl[:, n, 4 * p + a:4 * p + a + 1], ALU.mult, ALU.add))
                st.wait()
                z0 = g.z[:, 0, p % 2].rearrange("p a c -> p (a c)")
                st.do(v.tensor_tensor(t[0], cos, z0, ALU.mult))
                st.do(v.tensor_tensor(t[2], sin, z0, ALU.mult))
                v.sem_inc(g.z_ready, 1)

            turn_in(0, 0)
            turn_in(0, 1)

            def turn(i, more):
                for p in range(4):
                    scans(i, p)
                    if p + 2 < 4:
                        turn_in(i, p + 2)
                    elif more:
                        turn_in(i + 1, p - 2)
                v.wait_ge(g.c_done, i * 4 + 6)
                for p in range(4):
                    uv = g.u[:, p:p + 1, bass.ds(i * CH, CH)]
                    st.did(v.scalar_tensor_tensor(uv, uv, g.vec[:, V_DS + p:V_DS + p + 1],
                                                  g.ps[:, 6:7, p * CH:(p + 1) * CH], ALU.mult, ALU.add))
                st.wait()
                v.sem_inc(g.y_free, 1)

            with v.Fori(0, NCH - 1) as i:
                st.enter(i, 64)
                turn(i, True)
                st.leave(NCH - 1)
            turn(NCH - 1, False)
            abr, abi = (g.par[:, n, :].unsqueeze(2).to_broadcast([P, J, NB]) for n in (7, 8))
            v.wait_ge(g.x0_in, 16)
            cmul(v, st, g.x1[:, 0], g.x1[:, 1], abr, abi, g.x0[:, 0], g.x0[:, 1], g.xt[:, 0], g.xt[:, 1])
            v.wait_ge(g.bu_done, (NCH + 1) * 4 + 1)
            for n in range(2):
                st.do(v.tensor_tensor(g.x1[:, n], g.x1[:, n],
                                      g.ps[:, 2 + n, 0:P].rearrange("p (j b) -> p j b", j=J), ALU.add))
            v.sem_inc(g.xs_ready, 1)
            v.wait_ge(g.c_done, NCH * 4 + 3)
            for p in range(4):
                st.did(v.scalar_tensor_tensor(g.u[:, p, SEQ:TOK], g.u[:, p, SEQ:TOK],
                                              g.vec[:, V_DS + p:V_DS + p + 1],
                                              g.ps[:, 6, p * NB:(p + 1) * NB], ALU.mult, ALU.add))
            st.wait()
            g.dve_end = st.n

        @block.tensor
        def _(pe):
            pe.wait_ge(g.s5_fwd, 1)
            for n in range(2):
                for t in range(4):
                    last = pe.transpose(g.ps[:, 2 + n, t * P:(t + 1) * P],
                                        g.bm[:, n, 4 * t:4 * t + 4, :].rearrange("p a c -> p (a c)"),
                                        g.ident[:, :])
            last.then_inc(g.s5_tr, 1)
            pe.sem_inc(g.bu_done, 4)
            pe.sem_inc(g.c_done, 2)
            pe.wait_ge(g.s5_bt, 1)

            def bu(i, p):
                if p == 0:
                    pe.wait_ge(g.uc_ready, i + 1)
                pe.wait_ge(g.bu_free, i * 4 + (p + 1))
                for a in range(4):
                    for n in range(2):
                        last = pe.matmul(g.ps[:, 2 + 2 * (p % 2) + n, a * CH:(a + 1) * CH],
                                         g.BT[n][:, 4 * p + a, :], g.uc[:, p, :], start=True, stop=True)
                last.then_inc(g.bu_done, 1)

            def c(i, p):
                if p == 0:
                    pe.wait_ge(g.y_free, i + 1)
                pe.wait_ge(g.xc_ready, i * 4 + (p + 3))
                for n in range(2):
                    for a in range(4):
                        last = pe.matmul(g.ps[32 * a:32 * a + 32, 6, p * CH:(p + 1) * CH],
                                         g.CT[n][:, 4 * p + a, :], g.xs[:, n, p % 2, a, :],
                                         start=n == 0, stop=n == 1, skip_group_check=True)
                last.then_inc(g.c_done, 1)

            bu(0, 0)
            bu(0, 1)

            def turn(i, more):
                ops = gate_products(pe, g, i)
                bu(i, 2)
                run(ops, 24)
                c(i, 0)
                bu(i, 3)
                run(ops, 12)
                c(i, 1)
                if more:
                    bu(i + 1, 0)
                run(ops, 16)
                c(i, 2)
                if more:
                    bu(i + 1, 1)
                run(ops, 200)
                c(i, 3)

            with pe.Fori(0, NCH - 1) as i:
                turn(i, True)
            turn(NCH - 1, False)
            pe.wait_ge(g.uc_ready, NCH + 1)
            pe.wait_ge(g.bu_free, NCH * 4 + 2)
            for a in range(J):
                for n in range(2):
                    last = pe.matmul(g.ps[:, 2 + n, a * NB:(a + 1) * NB], g.BT[n][:, a, :],
                                     g.uc[:, a // 4, 0:NB], start=True, stop=True)
            last.then_inc(g.bu_done, 1)
            pe.wait_ge(g.xs_ready, 1)
            pe.wait_ge(g.y_free, NCH + 1)
            for p in range(4):
                for n in range(2):
                    for a in range(4):
                        last = pe.matmul(g.ps[32 * a:32 * a + 32, 6, p * NB:(p + 1) * NB],
                                         g.CT[n][:, 4 * p + a, :], g.x1[:, n, 4 * p + a, :],
                                         start=n == 0, stop=n == 1, skip_group_check=True)
            last.then_inc(g.c_done, 1)

    gates_done(g)
    g.dve_n, g.pool_n = g.dve_end, g.pool_end


def split_turn(pool, g, i, u0, kt):
    n = kt * P
    for s in range(2):
        pool.wait_ge(g.w_in[s], i * 16 + 16 * (u0 // 2 + 1))
        pool.wait_ge(g.unit_done, i * 2 + (u0 + s + 1))
        pool.tensor_tensor(g.whi[:, s, 0:n], g.wraw[:, s, 0:n], g.zero.to_broadcast([P, n]),
                               ALU.add).then_inc(g.w_hi, 1)
        pool.wait_ge(g.w_hi, i * 2 + (u0 + s + 1))
        pool.tensor_tensor(g.wlo[:, s, 0:n], g.wraw[:, s, 0:n], g.whi[:, s, 0:n].bitcast(F32),
                           ALU.subtract).then_inc(g.w_split, 1)


class Events:

    def __init__(self, sem, names):
        self.sem, self.names, self.k = sem, names, 0

    def on(self, ins, name):
        assert self.names[self.k % len(self.names)] == name, name
        self.k += 1
        ins.then_inc(self.sem, 1)

    def mark(self, eng, name):
        assert self.names[self.k % len(self.names)] == name, name
        self.k += 1
        eng.sem_inc(self.sem, 1)

    def wait(self, eng, i, name):
        n = len(self.names)
        eng.wait_ge(self.sem, i * n + (n + self.names.index(name) + 1))


LEVELS = range(1, 7)
LEV = [f"{a}{j}{n}" for j in LEVELS for a in "xt" for n in range(2)]
SCORES = [f"score{n}" for n in range(4)]
PRE = {"pe": ["norms", "lw", "la", "gate", "rn", "bonus"],
       "act": ["sq", "th", "tw", "ta", "gate", "exp"],
       "dve": ["kraw", "norms", "rn", "th", "cum", "kk", "kr", "rk", "bonus"]}
MAIN = {"pe": ["tok"] + SCORES + ["m"] + LEV + ["r0", "sa", "o", "s"],
        "act": ["tok", "r0", "sa", "o"],
        "dve": SCORES + ["m0", "m1", "state"] + LEV + ["s"]}
POST = {"pe": ["yt"], "act": ["osq"], "dve": ["oc", "y", "yt"]}
R_MID, R_SCALE, R_NORM, R_RN, R_TMP, R_MEAN, R_VAR, R_RSTD, R_BIAS, R_RK, R_BONUS, R_END = (
    0, (1, 12), 2, 3, 4, 5, 6, 7, 8, 9, (11, 13), (14, 15))


def plan_rwkv(nc, g):
    o = g.x_off
    g.fc, o = g.at("rw_f", o, [P, 2, RT, CH])
    g.th, o = g.at("rw_lora", o, [P, 2, CH])
    g.E = []
    for n in range(8):
        t, o = g.at(f"rw_e{n}", o, [P, 4, CH])
        g.E.append(t)
    g.KR, o = g.at("rw_kr", o, [P, 2, 4, 2, CH])
    g.ktok, o = g.at("rw_ktok", o, [P, W])
    g.btok, o = g.at("rw_btok", o, [P, W])
    g.vtok, o = g.at("rw_vtok", o, [P, 2, W])
    g.SC, o = g.at("rw_scores", o, [P, H, 2, 2, CH])
    g.T, o = g.at("rw_t", o, [P, H, CH])
    g.TT, o = g.at("rw_tt", o, [P, H, CH])
    g.X, o = g.at("rw_x", o, [P, H, CH])
    g.r0, o = g.at("rw_r0", o, [P, 2, 4 * N])
    g.sa, o = g.at("rw_sa", o, [P, 2, 4 * N])
    g.S, o = g.at("rw_s", o, [P, 4, N])
    g.rtab, o = g.at("rw_tab", o, [P, NTAB, P])
    g.wa, o = g.at("rw_wa", o, [P, W])
    g.gup, o = g.at("rw_gup", o, [P, W])
    g.lnw, o = g.at("rw_lnw", o, [P, W])
    g.lnb, o = g.at("rw_lnb", o, [P, W])
    g.rs, o = g.at("rw_small", o, [P, 16, 8])
    g.goutr, o = g.at("gate_out_r", o, [P, TOK])
    g.oc, g.osq = g.E[1], g.E[4]
    g.gs = [g.wraw[:, n, 4 * P:8 * P].rearrange("p (a c) -> p a c", a=4) for n in range(2)]
    g.yt = g.at("rw_y", g.whi_off + 4 * P * 4, [P, 4, CH])[0]
    assert o <= g.u_off, (o, g.u_off)
    S = nc.alloc_semaphore
    g.rw_in, g.f_in, g.ya_out, g.rw_out = S("rwkv_consts_in"), [S("f_in0"), S("f_in1")], S("ya_out"), S("wkv_out")
    g.rw_set = S("rwkv_set_up")
    g.pre, g.main, g.post = ({e: Events(S(f"rwkv_{part}_{e}"), names[e]) for e in names}
                             for part, names in (("pre", PRE), ("main", MAIN), ("post", POST)))


def bc(ap, n):
    return ap.unsqueeze(2).to_broadcast([ap.shape[0], ap.shape[1], n])


def flat(ap):
    return ap.rearrange("p a c -> p (a c)")


def by_head(x):
    return x.rearrange("p (h c) -> p h c", h=H)


def norm_centre(v, g, st, rows):
    r = slice(0, rows)
    mean, oh = g.rs[r, R_MEAN, :], by_head(flat(g.oc[:, :, :])[r])
    st.do(v.tensor_reduce(mean, oh, AXX, ALU.add))
    st.do(v.tensor_scalar(mean, mean, -1.0 / N, None, ALU.mult))
    st.do(v.tensor_tensor(oh, oh, bc(mean, N), ALU.add))


def norm_scale(v, g, st, rows):
    r = slice(0, rows)
    st.do(v.tensor_reduce(g.rs[r, R_VAR, :], by_head(flat(g.osq[:, :, :])[r]), AXX, ALU.add))
    rsqrt(v, st, g.rs[r, R_RSTD, :], g.rs[r, R_VAR, :], g.rs[r, R_TMP, :], 1.0 / N, LNX_EPS)


def norm_finish(v, g, st, rows, par, step=None):
    r = slice(0, rows)
    o2, oh = flat(g.oc[:, :, :])[r], by_head(flat(g.oc[:, :, :])[r])
    qh = by_head(flat(g.osq[:, :, :])[r])
    if step in (None, 0):
        st.do(v.tensor_tensor(oh, oh, bc(g.rs[r, R_RSTD, :], N), ALU.mult))
        st.do(v.tensor_tensor(o2, o2, g.lnw[r, :], ALU.mult))
    if step in (None, 1):
        st.did(v.tensor_tensor(o2, o2, g.lnb[r, :], ALU.add))
        st.do(v.tensor_tensor(qh, by_head(g.vtok[r, par, :]), bc(g.rs[r, R_BONUS[par], :], N), ALU.mult))
        st.do(v.tensor_tensor(oh, oh, qh, ALU.add))


def rwkv_block(nc, g, w_gate, gate_dram, f_dram, tabs, wa_in, gup_in, lnw_in, lnb_in, ya_dram, wkvp_out):
    E = g.E
    pre, main, post = g.pre, g.main, g.post
    g.gout = g.goutr
    one = g.seg[:, 2:3]

    def bank(n, a=4):
        return g.ps[:, n, :].rearrange("p (a c) -> p a c", a=a)

    def rows(q):
        return slice(64 * q, 64 * q + 64)

    def turns(eng, body, st=None, per=0):
        body(0, 0, 16, False, True)
        with eng.Fori(0, NCH // 2 - 1) as ii:
            if st:
                st.enter(ii, per)
            body(ii * 2 + 1, 1, ii * 16 + 32, True, True)
            body(ii * 2 + 2, 0, ii * 16 + 32, True, True)
            if st:
                st.leave(NCH // 2 - 1)
        body(NCH - 1, 1, 0, True, False)

    with nc.Block() as block:
        @block.sync
        def _(sp):
            for dst, src in ((g.rtab[:, :, :], tabs), (g.wa[:, :], wa_in), (g.gup[:, :], gup_in),
                             (g.lnw[:, :], lnw_in.to_broadcast([P, W])), (g.lnb[:, :], lnb_in.to_broadcast([P, W]))):
                sp.dma_start(dst, src).then_inc(g.rw_in, 16)
            u, m = g.units, g.gates * NBLK

            def load(i, par):
                sp.dma_start(g.fc[:, par, :, :],
                             f_dram[:, :, bass.ds(i * CH, CH)].rearrange("a p k -> p a k")).then_inc(g.f_in[par], 16)

            def ya(i):
                post["dve"].wait(sp, i, "yt")
                sp.dma_start(ya_dram[:, :, bass.ds(i * CH, CH)], g.yt[:, :, :]).then_inc(g.ya_out, 16)

            def turn(i, par, before=True, after2=True):
                for j in range(2):
                    sp.wait_ge(g.w_split, i * 2 + (u + j + 1))
                    sp.dma_start(g.wraw[:, j, 0:4 * P],
                                 w_gate[bass.ds(i + g.gates, 1), :, j * 4 * P:(j + 1) * 4 * P].rearrange("a p k -> p (a k)"))\
                      .then_inc(g.w_in[j], 16)
                if after2:
                    main["pe"].wait(sp, i, "tok")
                    pre["dve"].wait(sp, i, "bonus")
                    load(i + 2, par)
                if before:
                    ya(i - 1)
                sp.wait_ge(g.gate_free, i * NBLK + (m + NBLK + 2))
                sp.dma_start(gate_dram[bass.ds(i + g.gates, 1), :, :].rearrange("a p k -> p (a k)"), g.gout[:, :])\
                  .then_inc(g.gate_out, 16)

            load(0, 0)
            load(1, 1)
            turn(0, 0, before=False)
            with sp.Fori(0, NCH // 2 - 2) as ii:
                turn(ii * 2 + 1, 1)
                turn(ii * 2 + 2, 0)
            turn(NCH - 3, 1)
            turn(NCH - 2, 0, after2=False)
            turn(NCH - 1, 1, after2=False)
            ya(NCH - 1)
            main["dve"].wait(sp, NCH - 1, "s")
            sp.dma_start(wkvp_out, g.S[:, :, :]).then_inc(g.rw_out, 16)
            sp.wait_ge(g.rw_out, 16)
            sp.wait_ge(g.ya_out, 16 * (NCH + 1))
            sp.wait_ge(g.gate_out, 16 * (g.gates + NCH + 1))

        @block.gpsimd
        def _(pool):
            with pool.Fori(0, NCH) as i:
                split_turn(pool, g, i, g.units, 4)

        @block.scalar
        def _(act):
            ev_pre, ev, ev_post = pre["act"], main["act"], post["act"]
            for part, names in ((ev_pre, PRE), (ev, MAIN), (ev_post, POST)):
                act.sem_inc(part.sem, len(names["act"]))
            act.wait_ge(g.rw_in, 16 * 5)
            act.wait_ge(g.rw_set, 1)

            def lora_in(c, par, count):
                f = g.fc[:, par]
                pre["dve"].wait(act, c, "kraw")
                ev_pre.on(act.activation(E[7][:, :, :], E[6][:, :, :], ACT.Square), "sq")
                act.wait_ge(g.f_in[par], count)
                pre["pe"].wait(act, c - 1, "gate")
                act.activation(g.th[64:P, 0, :], f[64:P, 12, :], ACT.Copy)
                act.activation(g.th[0:64, 0, :], f[0:64, 12, :], ACT.Tanh)
                ev_pre.on(act.activation(g.th[:, 1, :], f[:, 13, :], ACT.Tanh, scale=0.5), "th")

            def lora_out(c):
                for n, name, prod, e in ((0, "tw", "lw", E[0]), (1, "ta", "la", E[5])):
                    pre["pe"].wait(act, c, prod)
                    for p in range(4):
                        ins = act.activation(e[:, p, :], g.ps[:, 1, p * CH:(p + 1) * CH], ACT.Tanh,
                                             bias=g.rs[:, R_BIAS, 4 * n + p:4 * n + p + 1], scale=0.5)
                    ev_pre.on(ins, name)

            def gate_exp(c, par):
                pre["pe"].wait(act, c, "gate")
                ev_pre.on(act.activation(flat(g.gs[par]), g.ps[:, 1, :], ACT.Copy), "gate")
                pre["dve"].wait(act, c, "cum")
                act.activation(E[2][:, :, :], E[1][:, :, :], ACT.Exp, scale=-DECAY)
                act.activation(E[3][:, :, :], E[1][:, :, :], ACT.Exp, scale=DECAY)
                act.activation(g.rs[:, R_SCALE[par], 0:4], g.rs[:, R_MID, 0:4], ACT.Exp, scale=-DECAY)
                ev_pre.on(act.activation(E[4][:, :, :], E[4][:, :, :], ACT.Exp, scale=-DECAY), "exp")

            def squares(i):
                post["dve"].wait(act, i, "oc")
                ev_post.on(act.activation(g.osq[:, :, :], g.oc[:, :, :], ACT.Square), "osq")

            def turn(i, par, count, before, after):
                main["pe"].wait(act, i, "tok")
                act.activation(g.vtok[:, par, :], g.ps[:, 2, :], ACT.Copy)
                act.activation(g.ktok[:, :], g.ps[:, 3, :], ACT.Copy)
                ev.on(act.activation(g.btok[:, :], g.ps[:, 4, :], ACT.Copy), "tok")
                if before:
                    squares(i - 1)
                if after:
                    lora_in(i + 1, 1 - par, count)
                gate_take(act, g, i, 0, 1)
                if after:
                    lora_out(i + 1)
                gate_take(act, g, i, 1, 1)
                if after:
                    gate_exp(i + 1, 1 - par)
                gate_take(act, g, i, 2, 1)
                main["pe"].wait(act, i, "r0")
                ev.on(act.activation(g.r0[:, :, :], g.ps[:, 2:4, 0:4 * N], ACT.Copy, scale=-1.0), "r0")
                main["pe"].wait(act, i, "sa")
                ev.on(act.activation(g.sa[:, :, :].rearrange("p a c -> p (a c)"), g.ps[:, 4, :], ACT.Copy), "sa")
                main["pe"].wait(act, i, "o")
                ev.on(act.activation(flat(g.oc[:, :, :]).rearrange("p (a q c) -> p q a c", q=2, c=N),
                                     g.ps[:, 5:7, 0:4 * N].rearrange("p q (a c) -> p q a c", a=4), ACT.Copy), "o")

            lora_in(0, 0, 16)
            lora_out(0)
            gate_exp(0, 0)
            turns(act, turn)
            squares(NCH - 1)

        @block.vector
        def _(v):
            st = Steps(v, g.dve_s, g.dve_n)
            ev_pre, ev, ev_post = pre["dve"], main["dve"], post["dve"]
            for part, names in ((ev_pre, PRE), (ev, MAIN), (ev_post, POST)):
                v.sem_inc(part.sem, len(names["dve"]))
            v.sem_inc(g.ya_out, 16)
            v.wait_ge(g.rw_in, 16 * 5)
            st.do(v.tensor_scalar(g.rs[:, R_BIAS, :], g.vec[:, V_W0:V_W0 + 8], 0.5, None, ALU.mult))
            for p in range(4):
                st.do(v.tensor_scalar(g.rs[:, R_RK, 2 * p:2 * p + 2], g.seg[:, 0:2], g.vec[:, V_RK + p:V_RK + p + 1],
                                      None, ALU.mult))
            st.do(v.memset(g.S[:, :, :], 0.0))
            v.sem_inc(g.rw_set, 2)
            mask2 = g.rtab[:, T_STRICT:T_INCL + 1, :].unsqueeze(1).to_broadcast([P, 2, 2, CH])

            def mk(t):
                return g.rtab[:, t:t + 1, :].to_broadcast([P, 4, CH])

            def tt(o, a, b, op, wait=True):
                (st.do if wait else st.did)(v.tensor_tensor(o, a, b, op))

            def kraw(c, par, count):
                v.wait_ge(g.f_in[par], count)
                tt(E[6][:, :, :], g.fc[:, par, 4:8, :], bc(g.vec[:, V_KK:V_KK + 4], CH), ALU.mult)
                ev_pre.mark(v, "kraw")

            def lora_gate(c):
                pre["act"].wait(v, c, "th")
                st.do(v.tensor_scalar(g.th[:, 1, :], g.th[:, 1, :], 0.5, 0.5, ALU.mult, ALU.add))
                ev_pre.mark(v, "th")

            def norms(c):
                pre["pe"].wait(v, c, "norms")
                st.do(v.tensor_copy(g.rs[:, R_NORM, :], g.ps[:, 1, 0:8]))
                ev_pre.mark(v, "norms")
                rsqrt(v, st, g.rs[:, R_RN, :], g.rs[:, R_NORM, :], g.rs[:, R_TMP, :], 1.0, 0.0, floor=1e-24)
                ev_pre.mark(v, "rn")

            def decay_sum(c):
                pre["act"].wait(v, c, "tw")
                st.do(v.tensor_scalar(E[0][:, :, :], E[0][:, :, :], 0.5, 0.5, ALU.mult, ALU.add))
                for p in range(4):
                    st.did(v.tensor_tensor_scan(E[1][:, p, :], one.to_broadcast([P, CH]), E[0][:, p, :], 0.0,
                                                ALU.mult, ALU.add))
                st.wait()

            def decay_mid(c):
                st.do(v.tensor_copy(g.rs[:, R_MID, 0:4], E[1][:, :, CH // 2 - 1]))
                tt(E[1][:, :, :], E[1][:, :, :], bc(g.rs[:, R_MID, 0:4], CH), ALU.subtract)
                tt(E[4][:, :, :], E[1][:, :, :], E[0][:, :, :], ALU.subtract)
                ev_pre.mark(v, "cum")

            def a_gate(c):
                pre["act"].wait(v, c, "ta")
                st.do(v.tensor_scalar(E[5][:, :, :], E[5][:, :, :], 0.5, 0.5, ALU.mult, ALU.add))
                st.do(v.scalar_tensor_tensor(E[7][:, :, :], E[5][:, :, :], -1.0, bc(g.vec[:, V_KA:V_KA + 4], CH),
                                             ALU.add, ALU.mult))

            def key(c, par):
                st.do(v.scalar_tensor_tensor(E[7][:, :, :], E[7][:, :, :], 1.0, g.fc[:, par, 4:8, :], ALU.add, ALU.mult))

            def kappa(c):
                pre["pe"].wait(v, c, "rn")
                tt(E[6][:, :, :], E[6][:, :, :], bank(1), ALU.mult)
                ev_pre.mark(v, "kk")
                tt(E[5][:, :, :], E[6][:, :, :], E[5][:, :, :], ALU.mult)

            def decayed(c, par):
                r = g.fc[:, par, 0:4, :]
                pre["act"].wait(v, c, "exp")
                tt(g.KR[:, par, :, 0, :], E[6][:, :, :], E[4][:, :, :], ALU.mult, False)
                tt(g.KR[:, par, :, 1, :], r, E[2][:, :, :], ALU.mult, False)
                st.did(v.tensor_copy(g.rs[:, R_END[par], 0:4], E[2][:, :, CH - 1]))
                tt(E[0][:, :, :], r, E[7][:, :, :], ALU.mult, False)

            def decayed_back(c):
                tt(E[5][:, :, :], E[5][:, :, :], E[3][:, :, :], ALU.mult)
                tt(E[3][:, :, :], E[7][:, :, :], E[3][:, :, :], ALU.mult)
                ev_pre.mark(v, "kr")
                ev_pre.mark(v, "rk")

            def bonus(c, par):
                pre["pe"].wait(v, c, "bonus")
                st.do(v.tensor_copy(g.rs[:, R_BONUS[par], :], g.ps[:, 1, 0:8]))
                ev_pre.mark(v, "bonus")

            def centre(i):
                main["act"].wait(v, i, "o")
                norm_centre(v, g, st, P)
                ev_post.mark(v, "oc")

            def scale(i):
                post["act"].wait(v, i, "osq")
                norm_scale(v, g, st, P)

            def finish(i, par, step):
                norm_finish(v, g, st, P, par, step)
                if step == 1:
                    ev_post.mark(v, "y")

            def gated(i, par):
                post["pe"].wait(v, i, "yt")
                v.wait_ge(g.ya_out, i * 16 + 16)
                tt(g.yt[:, :, :], g.gs[par], bank(1), ALU.mult)
                ev_post.mark(v, "yt")

            def turn(i, par, count, before, after):
                c, cp = i + 1, 1 - par
                if after:
                    kraw(c, cp, count)
                if before:
                    centre(i - 1)
                for n in range(4):
                    main["pe"].wait(v, i, f"score{n}")
                    for q in range(2):
                        tt(g.SC[:, 4 * q + n], g.ps[:, 4 + 2 * (n % 2) + q, :].rearrange("p (x a c) -> p x a c", x=2, a=2),
                           mask2, ALU.mult, q == 1)
                    ev.mark(v, f"score{n}")
                main["pe"].wait(v, i, "m")
                for n in range(2):
                    hs = slice(4 * n, 4 * n + 4)
                    tt(g.T[:, hs], bank(2 + n), mk(T_L0), ALU.mult, False)
                    tt(g.TT[:, hs], g.SC[:, hs, 1, 0, :], mk(T_L0T), ALU.mult)
                    tt(g.T[:, hs], g.T[:, hs], mk(T_ID), ALU.add, False)
                    tt(g.TT[:, hs], g.TT[:, hs], mk(T_ID), ALU.add)
                    ev.mark(v, f"m{n}")
                tt(g.S[:, :, :], g.S[:, :, :], bc(g.rs[:, R_SCALE[par], 0:4], N), ALU.mult)
                ev.mark(v, "state")
                beside = {}
                if before:
                    b, bp = i - 1, 1 - par
                    beside = {"t1": [lambda: scale(b)], "x2": [lambda: finish(b, bp, 0)],
                              "t2": [lambda: finish(b, bp, 1)], "t3": [lambda: gated(b, bp)]}
                if after:
                    for slot, f in (("x1", lambda: norms(c)), ("x2", lambda: lora_gate(c)), ("x4", lambda: decay_sum(c)),
                                    ("x5", lambda: decay_mid(c)), ("t6", lambda: a_gate(c)), ("t6", lambda: key(c, cp)),
                                    ("t6", lambda: kappa(c)), ("t6", lambda: decayed(c, cp)),
                                    ("t6", lambda: decayed_back(c))):
                        beside.setdefault(slot, []).append(f)
                for j in LEVELS:
                    for n in range(2):
                        main["pe"].wait(v, i, f"x{j}{n}")
                        tt(g.X[:, 4 * n:4 * n + 4], bank(2 + n), mk(T_LEV + j - 1), ALU.mult)
                        ev.mark(v, f"x{j}{n}")
                    for f in beside.get(f"x{j}", []):
                        f()
                    for n in range(2):
                        hs = slice(4 * n, 4 * n + 4)
                        main["pe"].wait(v, i, f"t{j}{n}")
                        if j < 6:
                            tt(g.T[:, hs], g.T[:, hs], bank(4 + 2 * n), ALU.add, False)
                        tt(g.TT[:, hs], g.TT[:, hs], bank(5 + 2 * n), ALU.add)
                        ev.mark(v, f"t{j}{n}")
                    for f in beside.get(f"t{j}", []):
                        f()
                main["pe"].wait(v, i, "s")
                tt(g.S[:, :, :], g.S[:, :, :], g.ps[:, 7, 0:4 * N].rearrange("p (a c) -> p a c", a=4), ALU.add)
                tt(g.S[:, :, :], g.S[:, :, :], bc(g.rs[:, R_END[par], 0:4], N), ALU.mult)
                ev.mark(v, "s")
                if after:
                    bonus(c, cp)

            kraw(0, 0, 16)
            norms(0)
            lora_gate(0)
            decay_sum(0)
            decay_mid(0)
            a_gate(0)
            key(0, 0)
            kappa(0)
            decayed(0, 0)
            decayed_back(0)
            bonus(0, 0)
            turns(v, turn, st=st, per=300)
            last = NCH - 1
            centre(last)
            scale(last)
            finish(last, 1, 0)
            finish(last, 1, 1)
            gated(last, 1)
            g.dve_end = st.n

        @block.tensor
        def _(pe):
            ev_pre, ev, ev_post = pre["pe"], main["pe"], post["pe"]
            for part, names in ((ev_pre, PRE), (ev, MAIN), (ev_post, POST)):
                pe.sem_inc(part.sem, len(names["pe"]))
            pe.wait_ge(g.rw_set, 2)

            def norms(c):
                pre["act"].wait(pe, c, "sq")
                pre["dve"].wait(pe, c - 1, "bonus")
                for p in range(4):
                    last = pe.matmul(g.ps[:, 1, 2 * p:2 * p + 2], E[7][:, p, :], g.seg[:, 0:2], start=True, stop=True)
                ev_pre.on(last, "norms")

            def lora(c, n):
                if n == 0:
                    pre["act"].wait(pe, c, "th")
                    pre["dve"].wait(pe, c, "norms")
                else:
                    pre["act"].wait(pe, c, "tw")
                for p in range(4):
                    last = pe.matmul(g.ps[:, 1, p * CH:(p + 1) * CH], g.wa[rows(n), p * P:(p + 1) * P],
                                     g.th[rows(n), 0, :], start=True, stop=True)
                ev_pre.on(last, ("lw", "la")[n])

            def gate(c, before):
                pre["act"].wait(pe, c, "ta")
                pre["dve"].wait(pe, c, "th")
                if before:
                    post["dve"].wait(pe, c - 2, "yt")
                for p in range(4):
                    last = pe.matmul(g.ps[:, 1, p * CH:(p + 1) * CH], g.gup[:, p * P:(p + 1) * P], g.th[:, 1, :],
                                     start=True, stop=True)
                ev_pre.on(last, "gate")

            def rn(c):
                pre["act"].wait(pe, c, "gate")
                pre["dve"].wait(pe, c, "rn")
                for p in range(4):
                    for q in range(2):
                        last = pe.matmul(g.ps[rows(q), 1, p * CH:(p + 1) * CH],
                                         g.rs[:, R_RN, 2 * p + q:2 * p + q + 1].to_broadcast([P, 64]),
                                         g.ident[:, :], start=True, stop=True)
                ev_pre.on(last, "rn")

            def bonus(c):
                pre["dve"].wait(pe, c, "rk")
                for p in range(4):
                    last = pe.matmul(g.ps[:, 1, 2 * p:2 * p + 2], E[0][:, p, :], g.rs[:, R_RK, 2 * p:2 * p + 2],
                                     start=True, stop=True)
                ev_pre.on(last, "bonus")

            def yt(i, after):
                post["dve"].wait(pe, i, "y")
                if after:
                    pre["act"].wait(pe, i + 2, "ta")
                else:
                    pre["dve"].wait(pe, NCH - 1, "bonus")
                for p in range(4):
                    last = pe.transpose(g.ps[:, 1, p * CH:(p + 1) * CH], g.oc[:, p, :], g.ident[:, :])
                ev_post.on(last, "yt")

            def turn(i, par, count, before, after):
                ops = gate_products(pe, g, i, 1)
                c = i + 1
                KR = g.KR[:, par]
                pre["dve"].wait(pe, i, "kr")
                for n, src in enumerate((g.fc[:, par, 8:12], E[3], E[5])):
                    for p in range(4):
                        last = pe.transpose(g.ps[:, 2 + n, p * P:(p + 1) * P], src[:, p, :], g.ident[:, :])
                ev.on(last, "tok")
                run(ops, 12)
                main["act"].wait(pe, i, "tok")
                main["act"].wait(pe, i - 1, "o")
                main["dve"].wait(pe, i - 1, "s")
                for p in range(4):
                    if p >= 2:
                        main["dve"].wait(pe, i, f"score{p - 2}")
                    for x, src in enumerate((E[3], E[5])):
                        for q in range(2):
                            last = pe.matmul(g.ps[:, 4 + 2 * (p % 2) + q, 256 * x:256 * x + 256], src[rows(q), p, :],
                                             KR[rows(q), p, :, :].rearrange("p a c -> p (a c)"), start=True, stop=True)
                    ev.on(last, f"score{p}")
                for p in range(4):
                    for q in range(2):
                        last = pe.matmul(g.ps[:, 2 + q, p * CH:(p + 1) * CH], KR[rows(q), p, 0, :], E[5][rows(q), p, :],
                                         start=True, stop=True)
                ev.on(last, "m")
                run(ops, 20)
                beside = {}
                gate_ops = {"x1": 6, "t1": 8, "x2": 8, "t2": 6, "x3": 2, "t3": 4, "x4": 4}
                if after:
                    beside = {"m": [lambda: norms(c)], "t1": [lambda: lora(c, 0)], "x2": [lambda: lora(c, 1)],
                              "x4": [lambda: gate(c, before)], "x5": [lambda: rn(c)]}
                if before:
                    beside.setdefault("x3", []).append(lambda: yt(i - 1, after))
                for f in beside.get("m", []):
                    f()
                for j in LEVELS:
                    for n in range(2):
                        main["dve"].wait(pe, i, f"m{n}" if j == 1 else f"t{j - 1}{n}")
                        for p in range(4):
                            h = 4 * n + p
                            last = pe.matmul(g.ps[:, 2 + n, p * CH:(p + 1) * CH], g.SC[:, h, 1, 0, :], g.T[:, h, :],
                                             start=True, stop=True)
                        ev.on(last, f"x{j}{n}")
                    for f in beside.get(f"x{j}", []):
                        f()
                    run(ops, gate_ops.get(f"x{j}", 0))
                    for n in range(2):
                        main["dve"].wait(pe, i, f"x{j}{n}")
                        for p in range(4):
                            h = 4 * n + p
                            if j < 6:
                                pe.matmul(g.ps[:, 4 + 2 * n, p * CH:(p + 1) * CH], g.TT[:, h, :], g.X[:, h, :],
                                          start=True, stop=True)
                            last = pe.matmul(g.ps[:, 5 + 2 * n, p * CH:(p + 1) * CH], g.X[:, h, :], g.TT[:, h, :],
                                             start=True, stop=True)
                        ev.on(last, f"t{j}{n}")
                    for f in beside.get(f"t{j}", []):
                        f()
                    run(ops, gate_ops.get(f"t{j}", 0))
                run(ops, 200)
                main["dve"].wait(pe, i, "state")
                for p in range(4):
                    for q in range(2):
                        pe.matmul(g.ps[:, 2 + q, p * N:(p + 1) * N], KR[rows(q), p, 0, :], g.S[rows(q), p, :],
                                  start=True, stop=False)
                    for q in range(2):
                        h = 2 * p + q
                        last = pe.matmul(g.ps[:, 2 + q, p * N:(p + 1) * N], g.SC[:, 4 * q + p, 0, 0, :],
                                         g.vtok[:, par, h * N:(h + 1) * N], start=False, stop=True)
                ev.on(last, "r0")
                main["act"].wait(pe, i, "r0")
                main["dve"].wait(pe, i, "t61")
                for h in range(H):
                    last = pe.matmul(g.ps[:, 4, h * N:(h + 1) * N], g.TT[:, h, :],
                                     flat(g.r0[:, :, :])[:, h * N:(h + 1) * N], start=True, stop=True)
                ev.on(last, "sa")
                main["act"].wait(pe, i, "sa")
                for p in range(4):
                    for q in range(2):
                        pe.matmul(g.ps[:, 5 + q, p * N:(p + 1) * N], KR[rows(q), p, 1, :], g.S[rows(q), p, :],
                                  start=True, stop=False)
                    for q in range(2):
                        h, hq = 2 * p + q, 4 * q + p
                        pe.matmul(g.ps[:, 5 + q, p * N:(p + 1) * N], g.SC[:, hq, 0, 1, :],
                                  g.vtok[:, par, h * N:(h + 1) * N], start=False, stop=False)
                        last = pe.matmul(g.ps[:, 5 + q, p * N:(p + 1) * N], g.SC[:, hq, 1, 1, :],
                                         flat(g.sa[:, :, :])[:, hq * N:(hq + 1) * N], start=False, stop=True)
                ev.on(last, "o")
                for p in range(4):
                    for q in range(2):
                        h, hq = 2 * p + q, 4 * q + p
                        pe.matmul(g.ps[rows(q), 7, p * N:(p + 1) * N], g.ktok[:, h * N:(h + 1) * N],
                                  g.vtok[:, par, h * N:(h + 1) * N], start=True, stop=False)
                        last = pe.matmul(g.ps[rows(q), 7, p * N:(p + 1) * N], g.btok[:, h * N:(h + 1) * N],
                                         flat(g.sa[:, :, :])[:, hq * N:(hq + 1) * N], start=False, stop=True)
                ev.on(last, "s")
                if after:
                    bonus(c)

            norms(0)
            lora(0, 0)
            lora(0, 1)
            gate(0, False)
            rn(0)
            bonus(0)
            turns(pe, turn)
            yt(NCH - 1, False)
    gates_done(g)
    g.dve_n = g.dve_end


def plan_sample(nc, g):
    o = g.h_end - 2 * DT * TOK * 4
    g.sS, o = g.at("sm_state", o, [P, 4 * NB, N])
    g.sK, o = g.at("sm_kappa", o, [P, 4 * NB, P])
    g.sV, o = g.at("sm_v", o, [P, 4 * NB, N])
    g.sT, o = g.at("sm_tmp", o, [P, 4 * NB, N])
    g.sR, o = g.at("sm_r", o, [P, 2, 4, NB * NB])
    g.sF, o = g.at("sm_f", o, [P, RT, NB])
    assert o <= g.h_end
    S = nc.alloc_semaphore
    g.sm_in, g.sm_act, g.sm_pe, g.sm_dve, g.sm_out = (S("sample_in"), S("sample_act"), S("sample_pe"),
                                                      S("sample_dve"), S("sample_out"))


SM_ACT = ["th", "tanh", "exp", "sq", "tok", "o", "osq", "g"]
SM_PE = ["lora", "norms", "rn", "bonus", "tok", "sa", "o", "g", "yt"]
SM_DVE = ["th", "xw", "kraw", "rn", "rk", "bonus", "kv", "state", "r", "oc", "y", "yt"]


def sample_block(nc, g, f_dram, wkv_in, ya_dram, wkv_out):
    E = g.E
    a_ev, p_ev, d_ev = Events(g.sm_act, SM_ACT), Events(g.sm_pe, SM_PE), Events(g.sm_dve, SM_DVE)
    f = g.sF
    C8 = slice(0, NB)
    st32 = lambda t: t[:, :, :].rearrange("p (a b) c -> p a b c", a=4)

    def over(ap, n):
        return ap.unsqueeze(3).to_broadcast([P, 4, NB, n])

    def rows(q):
        return slice(64 * q, 64 * q + 64)

    with nc.Block() as block:
        @block.sync
        def _(sp):
            sp.dma_start(f[:, :, :], f_dram[:, :, SEQ:TOK].rearrange("a p k -> p a k")).then_inc(g.sm_in, 16)
            sp.dma_start(g.sS[:, :, :], wkv_in).then_inc(g.sm_in, 16)
            d_ev.wait(sp, 0, "state")
            sp.dma_start(wkv_out, g.sS[:, :, :]).then_inc(g.sm_out, 16)
            d_ev.wait(sp, 0, "yt")
            sp.dma_start(ya_dram[:, :, SEQ:TOK], g.yt[:, :, C8]).then_inc(g.sm_out, 16)
            sp.wait_ge(g.sm_out, 32)

        @block.scalar
        def _(act):
            act.sem_inc(g.sm_act, len(SM_ACT))
            act.wait_ge(g.sm_in, 32)
            act.activation(g.th[64:P, 0, C8], f[64:P, 12, :], ACT.Copy)
            act.activation(g.th[0:64, 0, C8], f[0:64, 12, :], ACT.Tanh)
            a_ev.on(act.activation(g.th[:, 1, C8], f[:, 13, :], ACT.Tanh, scale=0.5), "th")
            p_ev.wait(act, 0, "lora")
            for p in range(4):
                act.activation(E[0][:, p, C8], g.ps[:, 2, p * NB:(p + 1) * NB], ACT.Tanh,
                               bias=g.rs[:, 8, p:p + 1], scale=0.5)
                ins = act.activation(E[5][:, p, C8], g.ps[:, 3, p * NB:(p + 1) * NB], ACT.Tanh,
                                     bias=g.rs[:, 8, 4 + p:5 + p], scale=0.5)
            a_ev.on(ins, "tanh")
            d_ev.wait(act, 0, "xw")
            a_ev.on(act.activation(E[2][:, :, C8], E[0][:, :, C8], ACT.Exp, scale=-DECAY), "exp")
            d_ev.wait(act, 0, "kraw")
            a_ev.on(act.activation(E[7][:, :, C8], E[6][:, :, C8], ACT.Square), "sq")
            p_ev.wait(act, 0, "tok")
            a_ev.on(act.activation(g.vtok[C8, 0, :], g.ps[C8, 2, :], ACT.Copy), "tok")
            p_ev.wait(act, 0, "o")
            a_ev.on(act.activation(flat(g.oc[:, :, :])[C8], g.ps[C8, 0, :], ACT.Copy), "o")
            d_ev.wait(act, 0, "oc")
            a_ev.on(act.activation(flat(g.osq[:, :, :])[C8], flat(g.oc[:, :, :])[C8], ACT.Square), "osq")
            p_ev.wait(act, 0, "g")
            a_ev.on(act.activation(flat(g.gs[0])[:, 0:4 * NB], g.ps[:, 1, 0:4 * NB], ACT.Copy), "g")

        @block.vector
        def _(v):
            st = Steps(v, g.dve_s, g.dve_n)
            v.sem_inc(g.sm_dve, len(SM_DVE))
            v.wait_ge(g.sm_in, 32)
            r, k, vv = f[:, 0:4, :], f[:, 4:8, :], f[:, 8:12, :]
            e = [t[:, :, C8] for t in E]

            def tt(o, a, b, op):
                st.do(v.tensor_tensor(o, a, b, op))

            a_ev.wait(v, 0, "th")
            st.do(v.tensor_scalar(g.th[:, 1, C8], g.th[:, 1, C8], 0.5, 0.5, ALU.mult, ALU.add))
            d_ev.mark(v, "th")
            a_ev.wait(v, 0, "tanh")
            st.do(v.tensor_scalar(e[0], e[0], 0.5, 0.5, ALU.mult, ALU.add))
            d_ev.mark(v, "xw")
            tt(e[6], k, bc(g.vec[:, V_KK:V_KK + 4], NB), ALU.mult)
            d_ev.mark(v, "kraw")
            st.do(v.tensor_scalar(e[5], e[5], 0.5, 0.5, ALU.mult, ALU.add))
            p_ev.wait(v, 0, "norms")
            st.do(v.tensor_copy(g.rs[C8, 2, :], g.ps[C8, 5, 0:8]))
            rsqrt(v, st, g.rs[C8, 3, :], g.rs[C8, 2, :], g.rs[C8, 4, :], 1.0, 0.0, floor=1e-24)
            d_ev.mark(v, "rn")
            st.do(v.scalar_tensor_tensor(e[7], e[5], -1.0, bc(g.vec[:, V_KA:V_KA + 4], NB), ALU.add, ALU.mult))
            st.do(v.scalar_tensor_tensor(e[7], e[7], 1.0, k, ALU.add, ALU.mult))
            p_ev.wait(v, 0, "rn")
            tt(e[6], e[6], g.ps[:, 6, 0:4 * NB].rearrange("p (a c) -> p a c", a=4), ALU.mult)
            tt(e[5], e[6], e[5], ALU.mult)
            a_ev.wait(v, 0, "exp")
            tt(e[0], r, e[7], ALU.mult)
            d_ev.mark(v, "rk")
            p_ev.wait(v, 0, "bonus")
            st.do(v.tensor_copy(g.rs[C8, 11, :], g.ps[C8, 5, 0:8]))
            d_ev.mark(v, "bonus")
            st.do(v.tensor_scalar(e[6], e[6], -1.0, None, ALU.mult))
            blk = g.rtab[:, T_BLK, :].unsqueeze(1).unsqueeze(1).to_broadcast([P, 4, NB, P])
            eye = g.rtab[:, T_IST, 0:N].unsqueeze(1).unsqueeze(1).to_broadcast([P, 4, NB, N])
            tt(st32(g.sK), blk, over(e[6], P), ALU.mult)
            tt(st32(g.sV), eye, over(vv, N), ALU.mult)
            d_ev.mark(v, "kv")
            S, T = st32(g.sS), st32(g.sT)
            p_ev.wait(v, 0, "sa")
            tt(S, S, over(e[2], N), ALU.mult)
            for first, x in ((0, e[5]), (4, e[7])):
                tt(T, g.ps[:, first:first + 4, :].rearrange("p a (b c) -> p a b c", b=NB), over(x, N), ALU.mult)
                tt(S, S, T, ALU.add)
            d_ev.mark(v, "state")
            eye8 = g.seg[:, 8:72].rearrange("p (b c) -> p b c", b=NB).unsqueeze(1).to_broadcast([P, 4, NB, NB])
            for q in range(2):
                R = g.sR[:, q, :, :].rearrange("p a (b c) -> p a b c", b=NB)
                tt(R, eye8, over(r, NB), ALU.mult)
                st.do(v.tensor_scalar(g.sR[:, q, :, :], g.sR[:, q, :, :], g.seg[:, q:q + 1], None, ALU.mult))
            d_ev.mark(v, "r")
            a_ev.wait(v, 0, "o")
            norm_centre(v, g, st, NB)
            d_ev.mark(v, "oc")
            a_ev.wait(v, 0, "osq")
            norm_scale(v, g, st, NB)
            norm_finish(v, g, st, NB, 0)
            d_ev.mark(v, "y")
            p_ev.wait(v, 0, "yt")
            a_ev.wait(v, 0, "g")
            tt(g.yt[:, :, C8], flat(g.gs[0])[:, 0:4 * NB].rearrange("p (a c) -> p a c", a=4),
               g.ps[:, 2, 0:4 * NB].rearrange("p (a c) -> p a c", a=4), ALU.mult)
            d_ev.mark(v, "yt")
            g.dve_end = st.n

        @block.tensor
        def _(pe):
            pe.sem_inc(g.sm_pe, len(SM_PE))
            a_ev.wait(pe, 0, "th")
            for p in range(4):
                pe.matmul(g.ps[:, 2, p * NB:(p + 1) * NB], g.wa[0:64, p * P:(p + 1) * P], g.th[0:64, 0, C8],
                          start=True, stop=True)
                last = pe.matmul(g.ps[:, 3, p * NB:(p + 1) * NB], g.wa[64:P, p * P:(p + 1) * P],
                                 g.th[64:P, 0, C8], start=True, stop=True)
            p_ev.on(last, "lora")
            a_ev.wait(pe, 0, "sq")
            for p in range(4):
                last = pe.matmul(g.ps[C8, 5, 2 * p:2 * p + 2], E[7][:, p, C8], g.seg[:, 0:2], start=True, stop=True)
            p_ev.on(last, "norms")
            d_ev.wait(pe, 0, "rn")
            for p in range(4):
                for q in range(2):
                    last = pe.matmul(g.ps[rows(q), 6, p * NB:(p + 1) * NB],
                                     g.rs[C8, 3, 2 * p + q:2 * p + q + 1].to_broadcast([NB, 64]),
                                     g.ident[C8, C8], start=True, stop=True)
            p_ev.on(last, "rn")
            d_ev.wait(pe, 0, "rk")
            for p in range(4):
                last = pe.matmul(g.ps[C8, 5, 2 * p:2 * p + 2], E[0][:, p, C8], g.rs[:, 9, 2 * p:2 * p + 2],
                                 start=True, stop=True)
            p_ev.on(last, "bonus")
            for p in range(4):
                last = pe.transpose(g.ps[C8, 2, p * P:(p + 1) * P], f[:, 8 + p, :], g.ident[:, :])
            p_ev.on(last, "tok")
            d_ev.wait(pe, 0, "kv")
            a_ev.wait(pe, 0, "tok")
            for n in range(4 * NB):
                pe.matmul(g.ps[:, n // NB, (n % NB) * N:(n % NB + 1) * N], g.sK[:, n, :], g.sS[:, n, :],
                          start=True, stop=True)
            for p in range(4):
                last = pe.matmul(g.ps[:, 4 + p, :], g.rtab[:, T_BLK, :],
                                 flat(g.sV[:, p * NB:(p + 1) * NB, :]), start=True, stop=True)
            p_ev.on(last, "sa")
            d_ev.wait(pe, 0, "r")
            for p in range(4):
                for q in range(2):
                    for b in range(NB):
                        last = pe.matmul(g.ps[C8, 0, (2 * p + q) * N:(2 * p + q + 1) * N],
                                         g.sR[:, q, p, b * NB:(b + 1) * NB], g.sS[:, p * NB + b, :],
                                         start=b == 0, stop=b == NB - 1)
            p_ev.on(last, "o")
            for p in range(4):
                last = pe.matmul(g.ps[:, 1, p * NB:(p + 1) * NB], g.gup[:, p * P:(p + 1) * P], g.th[:, 1, C8],
                                 start=True, stop=True)
            p_ev.on(last, "g")
            d_ev.wait(pe, 0, "y")
            for p in range(4):
                last = pe.transpose(g.ps[:, 2, p * NB:(p + 1) * NB], g.oc[C8, p, :], g.ident[C8, C8])
            p_ev.on(last, "yt")
    g.dve_n = g.dve_end


def make_tables():
    tab = np.zeros((P, NTAB, P), np.float32)
    a, b = np.meshgrid(np.arange(P), np.arange(P), indexing="ij")
    tab[:, T_ID] = a == b
    tab[:, T_STRICT] = a < b
    tab[:, T_INCL] = a <= b
    low = lambda j: (a >> (j + 1) == b >> (j + 1)) & ((a >> j) & 1 == 1) & ((b >> j) & 1 == 0)
    tab[:, T_L0] = -1.0 * low(0)
    tab[:, T_L0T] = -1.0 * low(0).T
    for j in LEVELS:
        tab[:, T_LEV + j - 1] = -1.0 * low(j)
    tab[:64, T_SEG, 0] = 1
    tab[64:, T_SEG, 1] = 1
    tab[:, T_SEG, 2] = 1
    tab[:, T_SEG, 8:72] = np.eye(8).reshape(1, 64)
    tab[:, T_BLK] = a // 64 == b // 64
    tab[:, T_IST, 0:64] = a[:, 0:64] % 64 == b[:, 0:64]
    return tab


GLU_IN, GLU_CUBE = 0.7978845608028654, 0.044715


def plan_merge(nc, g):
    o = g.h_end
    g.yahi, o = g.at("ya_hi", o, [P, WT, TOK], F32R)
    g.yalo, o = g.at("ya_lo", o, [P, WT, TOK], F32R)
    assert o <= g.x_end
    o = g.x_end
    g.ybhi, o = g.at("yb_hi", o, [P, WT, TOK], F32R)
    g.yblo, o = g.at("yb_lo", o, [P, WT, TOK], F32R)
    g.gt, o = g.at("gates_in", o, [P, 2, 2, TOK])
    g.mt, o = g.at("merge_t", o, [P, 2, TOK])
    g.mm, o = g.at("merged", o, [P, 1, TOK])
    assert o <= g.u_off, (o, g.u_off)
    g.zhi, g.zlo = g.hhi[:, 0:WT, :], g.hhi[:, WT:2 * WT, :]
    S = nc.alloc_semaphore
    g.ya_in, g.ya_hi_s, g.ya_split = S("ya_in"), S("ya_hi"), S("ya_split")
    g.gl_sq, g.gl_scaled, g.gl_in, g.gl_tanh = S("gelu_squared"), S("gelu_scaled"), S("gelu_inner"), S("gelu_tanh")
    g.z2_ready, g.z_hi, g.z_split = S("z2_ready"), S("z2_hi"), S("z2_split")
    g.yb_ready, g.yb_hi, g.yb_split = S("yb_ready"), S("yb_hi"), S("yb_split")
    g.gt_in, g.gt_used = [S("gates_in0"), S("gates_in1")], S("gates_used")
    g.m_ready, g.m_hi, g.m_split = S("merged_ready"), S("merged_hi"), S("merged_split")
    g.x_back = [S("x_back0"), S("x_back1")]


def merge_block(nc, g, w_glu, w_ab, w_out, ya_dram, gate_dram, x_dram):
    u0 = g.units
    ua = u0 + WT
    uo = ua + 2 * DT
    use = list(g.uses)
    use_a = [n + WT // 2 for n in use]
    use_o = [n + DT for n in use_a]
    u, t = g.u, g.mt

    def part(x):
        return lambda k, b: x[:, k, b * BLK:(b + 1) * BLK]

    with nc.Block() as block:
        @block.sync
        def _(sp):
            sp.dma_start(g.gt[:, :, :, :].rearrange("p a b c -> p (a b) c"), ya_dram).then_inc(g.ya_in, 16)
            load_units(sp, g, u0, WT // 2, 2, WT,
                       lambda i, j: w_glu[bass.ds(i * 2 + j, 1), :, :].rearrange("a p k -> p (a k)"))
            with sp.Fori(0, DT // 2) as ii:
                for par in range(2):
                    for j in range(2):
                        sp.wait_ge(g.w_split, ii * 4 + (ua + 2 * par + j + 1))
                        sp.dma_start(g.wraw[:, j, 0:WT * P],
                                     w_ab[bass.ds(ii * 4 + (2 * par + j), 1), :, :].rearrange("a p k -> p (a k)"))\
                          .then_inc(g.w_in[j], 16)
                    sp.wait_ge(g.gt_used, ii * 2 + (par + 1))
                    for q in range(2):
                        sp.dma_start(g.gt[:, par, q, :],
                                     gate_dram[bass.ds(ii * 2 + (par + DT * q), 1), :, :].rearrange("a p k -> p (a k)"))\
                          .then_inc(g.gt_in[par], 16)
            load_units(sp, g, uo, DT // 2, 2, DT,
                       lambda i, j: w_out[bass.ds(i * 2 + j, 1), :, :].rearrange("a p k -> p (a k)"))

        @block.gpsimd
        def _(pool):
            def split_ya(k):
                pool.tensor_tensor(g.yahi[:, k, :], g.gt[:, k // 2, k % 2, :], g.zero.to_broadcast([P, TOK]),
                                   ALU.add).then_inc(g.ya_hi_s, 1)
                pool.wait_ge(g.ya_hi_s, k + 1)
                pool.tensor_tensor(g.yalo[:, k, :], g.gt[:, k // 2, k % 2, :], g.yahi[:, k, :].bitcast(F32),
                                   ALU.subtract).then_inc(g.ya_split, 1)

            split_units(pool, g, u0, 1, 2, WT)
            pool.wait_ge(g.ya_in, 16)
            split_ya(0)
            split_ya(1)
            split_units(pool, g, u0 + 2, 1, 2, WT)
            split_ya(2)
            split_ya(3)
            pool.wait_ge(g.ya_split, WT)
            pool.sem_inc(g.gt_used, 2)
            split_units(pool, g, ua, DT, 2, WT)
            split_units(pool, g, uo, DT // 2, 2, DT)

        @block.scalar
        def _(act):
            for n in range(2):
                act.activation(t[:, n, :], u[:, n, :], ACT.Square).then_inc(g.gl_sq, 1)
            for n in range(WT):
                act.wait_ge(g.gl_in, n + 1)
                act.activation(t[:, n % 2, :], t[:, n % 2, :], ACT.Tanh, scale=GLU_IN).then_inc(g.gl_tanh, 1)
                act.wait_ge(g.z2_ready, n + 1)
                act.activation(g.zhi[:, n, :], u[:, n, :], ACT.Copy).then_inc(g.z_hi, 1)
                if n + 2 < WT:
                    act.activation(t[:, n % 2, :], u[:, n + 2, :], ACT.Square).then_inc(g.gl_sq, 1)
            for n in range(WT):
                act.wait_ge(g.unit_done, u0 + n + 1 + WSLOTS)
                if n >= 2:
                    act.wait_ge(g.yb_ready, n - 1)
                act.activation(blocks(t[:, n % 2, :]), acc(g, n % 2), ACT.Tanh, scale=0.25)\
                   .then_inc(g.set_free[n % 2], 1)
                act.wait_ge(g.yb_ready, n + 1)
                act.activation(g.ybhi[:, n, :], u[:, n, :], ACT.Copy).then_inc(g.yb_hi, 1)
            with act.Fori(0, DT) as i:
                act.wait_ge(g.m_ready, i + 1)
                act.activation(g.hhi[:, bass.ds(i, 1), :], g.mm[:, :, :], ACT.Copy).then_inc(g.m_hi, 1)
            act.wait_ge(g.unit_done, uo - 1 + WSLOTS)
            for n in range(2):
                half = slice(n * DT // 2, (n + 1) * DT // 2)
                act.dma_start(g.x[:, half, :], x_dram[:, half, :]).then_inc(g.x_back[n], 16)

        @block.vector
        def _(v):
            def inner(n):
                v.wait_ge(g.gl_sq, n + 1)
                v.tensor_scalar(t[:, n % 2, :], t[:, n % 2, :], GLU_CUBE, 1.0, ALU.mult, ALU.add)\
                 .then_inc(g.gl_scaled, 1)
                v.wait_ge(g.gl_scaled, n + 1)
                v.tensor_tensor(t[:, n % 2, :], t[:, n % 2, :], u[:, n, :], ALU.mult).then_inc(g.gl_in, 1)

            inner(0)
            inner(1)
            for n in range(WT):
                v.wait_ge(g.gl_tanh, n + 1)
                v.scalar_tensor_tensor(u[:, n, :], t[:, n % 2, :], 1.0, u[:, n, :], ALU.add, ALU.mult)\
                 .then_inc(g.z2_ready, 1)
                v.wait_ge(g.z_hi, n + 1)
                v.tensor_tensor(g.zlo[:, n, :], u[:, n, :], g.zhi[:, n, :].bitcast(F32),
                                ALU.subtract).then_inc(g.z_split, 1)
                if n + 2 < WT:
                    inner(n + 2)
            for n in range(WT):
                v.wait_ge(g.set_free[n % 2], use[n % 2] + n // 2 + 2)
                v.scalar_tensor_tensor(u[:, n, :], t[:, n % 2, :], 1.0, u[:, n, :], ALU.add, ALU.mult)\
                 .then_inc(g.yb_ready, 1)
                v.wait_ge(g.yb_hi, n + 1)
                v.tensor_tensor(g.yblo[:, n, :], u[:, n, :], g.ybhi[:, n, :].bitcast(F32),
                                ALU.subtract).then_inc(g.yb_split, 1)
            with v.Fori(0, DT // 2) as ii:
                for par in range(2):
                    gates = [g.gt[:, par, q, :] for q in range(2)]
                    v.wait_ge(g.gt_in[par], ii * 32 + 32)
                    v.wait_ge(g.unit_done, ii * 4 + (ua + 2 * par + 1 + WSLOTS))
                    v.scalar_tensor_tensor(blocks(t[:, 0, :]), blocks(gates[0]), 1.0, acc(g, 0), ALU.add, ALU.mult)\
                     .then_inc(g.set_free[0], 1)
                    v.wait_ge(g.unit_done, ii * 4 + (ua + 2 * par + 2 + WSLOTS))
                    v.scalar_tensor_tensor(blocks(t[:, 1, :]), blocks(gates[1]), 1.0, acc(g, 1), ALU.add, ALU.mult)\
                     .then_inc(g.set_free[1], 1)
                    v.wait_ge(g.set_free[0], ii * 2 + (use_a[0] + par + 2))
                    v.wait_ge(g.set_free[1], ii * 2 + (use_a[1] + par + 2))
                    v.sem_inc(g.gt_used, 1)
                    v.scalar_tensor_tensor(g.mm[:, 0, :], t[:, 1, :], 0.25, t[:, 0, :], ALU.mult, ALU.add)\
                     .then_inc(g.m_ready, 1)
                    v.wait_ge(g.m_hi, ii * 2 + (par + 1))
                    v.tensor_tensor(g.hlo[:, bass.ds(ii * 2 + par, 1), :], g.mm[:, :, :],
                                    g.hhi[:, bass.ds(ii * 2 + par, 1), :].bitcast(F32),
                                    ALU.subtract).then_inc(g.m_split, 1)
                    v.wait_ge(g.m_split, ii * 2 + (par + 1))
            for n in range(DT):
                if n % (DT // 2) == 0:
                    v.wait_ge(g.x_back[n // (DT // 2)], 16)
                v.wait_ge(g.unit_done, uo + n + 1 + WSLOTS)
                v.scalar_tensor_tensor(blocks(g.x[:, n, :]), acc(g, n % 2), 0.5, blocks(g.x[:, n, :]),
                                       ALU.mult, ALU.add).then_inc(g.set_free[n % 2], 1)

        @block.tensor
        def _(pe):
            for n in range(WT):
                product(pe, g, 0, 0, u0 + n, WT, n % 2, use[n % 2] + n // 2, 0, part(g.zhi), part(g.zlo),
                        (g.z_split, lambda i, k: k + 1))
            with pe.Fori(0, DT) as i:
                product(pe, g, i, 2, ua, WT, 0, use_a[0], 1, part(g.yahi), part(g.yalo),
                        (g.ya_split, lambda i, k: k + 1))
                product(pe, g, i, 2, ua + 1, WT, 1, use_a[1], 1, part(g.ybhi), part(g.yblo),
                        (g.yb_split, lambda i, k: k + 1))
            with pe.Fori(0, DT // 2) as i:
                for j in range(2):
                    product(pe, g, i, 2, uo + j, DT, j, use_o[j], 1, part(g.hhi), part(g.hlo),
                            (g.m_split, lambda i, k: k + 1))

    g.units = uo + DT
    g.uses = [n + DT // 2 for n in use_o]


def build(nc, a, o):
    g = Ctx()
    plan(nc, g)
    plan_mid(nc, g)
    plan_s5(nc, g)
    plan_rwkv(nc, g)
    plan_sample(nc, g)
    plan_merge(nc, g)

    def dram(name, shape):
        return nc.dram_tensor(name, shape, F32, kind="Internal").ap()

    f_dram = dram("f_mixed", (RT, P, TOK))
    x_dram = dram("x_mid", (P, DT, TOK))
    gate_dram = dram("gates", (2 * DT, P, TOK))
    ya_dram = dram("ya", (P, WT, TOK))

    def first_loads(sp):
        sp.dma_start(g.x[:, :, :], a["x"]).then_inc(g.x_in, 16)
        sp.dma_start(g.ident[:, :], a["tabs"][:, T_ID, :]).then_inc(g.c_in, 16)
        sp.dma_start(g.seg[:, :], a["tabs"][:, T_SEG, :]).then_inc(g.c_in, 16)
        sp.dma_start(g.vec[:, :], a["vec"]).then_inc(g.c_in, 16)

    ffn_block(nc, g, a["ffn1_up"], a["ffn1_down"], V_G1,
              before={"sync": first_loads, "scalar": lambda act: act.wait_ge(g.x_in, 16)})
    proj_block(nc, g, a["w_mix"], a["shift"], f_dram, x_dram, o["last"])
    s5_block(nc, g, a["w_gates"], gate_dram, a["s5_b"], a["s5_c"], a["s5_x0"], o["s5_prompt"], o["s5_sample"])
    rwkv_block(nc, g, a["w_gates"], gate_dram, f_dram, a["tabs"], a["lora_up"], a["g_up"], a["lnx_w"], a["lnx_b"],
               ya_dram, o["wkv_prompt"])
    sample_block(nc, g, f_dram, a["wkv"], ya_dram, o["wkv_sample"])
    merge_block(nc, g, a["w_glu"], a["w_ab"], a["w_out"], ya_dram, gate_dram, x_dram)

    n1 = g.norms + 1
    use = [n + k + FT + len(FFN_GROUPS) * DT // 2 for k, n in zip((1, 0), g.uses)]

    def final_act(act):
        for j in range(2):
            act.wait_ge(g.set_free[j], use[j] + 1)
        norm_act(act, g, n1)

    def final_dve(v, st):
        norm_dve(v, g, st, n1)
        for k in range(DT):
            v.scalar_tensor_tensor(blocks(g.x[:, k, :]), blocks(g.x[:, k, :]), g.vec[:, V_GF + k:V_GF + k + 1],
                                   acc(g, 0), ALU.mult, ALU.mult).then_inc(g.y_ready, 1)

    def final_out(sp):
        for k in range(DT):
            sp.wait_ge(g.y_ready, k + 1)
            sp.dma_start(o["y"][:, k, :], g.x[:, k, :]).then_inc(g.out_done, 16)
        sp.wait_ge(g.out_done, 16 * DT)

    g.y_ready = nc.alloc_semaphore("y_ready")
    ffn_block(nc, g, a["ffn2_up"], a["ffn2_down"], V_G2,
              after={"sync": final_out, "scalar": final_act, "vector": final_dve,
                     "tensor": lambda pe: norm_pe(pe, g, n1, use[0])})


OUTPUTS = {"y": (P, DT, TOK), "last": (P, RT, NB + 1), "wkv_prompt": (P, 4, N), "wkv_sample": (P, 4 * NB, N),
           "s5_prompt": (P, 2, J), "s5_sample": (P, 2, J, NB)}


def tile_w(w):
    k, m = w.shape
    return w.reshape(k // P, P, m // P, P).transpose(2, 1, 0, 3).reshape(m // P, P, k)


def fold(v):
    return v.reshape(-1, P).T


def pairs(a):
    a = a.reshape(J, 2, N, *a.shape[2:])
    return a.transpose(1, 2, 0, *range(3, a.ndim)).reshape(P, J, *a.shape[3:])


def unpairs(a):
    a = a.reshape(2, N, J, *a.shape[2:])
    return a.transpose(2, 0, 1, *range(3, a.ndim)).reshape(2 * J, N, *a.shape[3:])


def kernel(x_prompt, x_sample, state_shift, state_wkv, state_s5_re, state_s5_im,
           g_ffn1, ffn1_gate, ffn1_up, ffn1_down, g_mix, w_in, mu_shift,
           w0, w_up, a0, a_up, g_up, k_k, k_a, r_k, lnx_w, lnx_b,
           A_re, A_im, log_dt, B_re, B_im, C_re, C_im, D_skip, w_glu,
           w_a_up, w_b_up, w_out, g_ffn2, ffn2_gate, ffn2_up, ffn2_down, g_final):
    from concourse import bacc as _bacc
    from concourse.bass_utils import run_bass_kernel_spmd

    A = np.asarray
    x = np.concatenate([A(x_prompt)[0], A(x_sample)[:, 0]], 0)
    win = A(w_in)[0]
    mix_cols = RT * P + UT * P
    vec = np.concatenate([
        fold(A(g_ffn1)[0]), fold(A(g_mix)[0]), fold(A(g_ffn2)[0]), fold(A(g_final)), fold(A(mu_shift)[0]),
        fold(A(w0)[0]), fold(A(a0)[0]), fold(A(k_k)[0]), fold(A(k_a)[0]), fold(A(r_k)[0].reshape(-1)),
        fold(A(D_skip)[0]), pairs(A(A_re)[0]), pairs(A(A_im)[0]),
        pairs(np.repeat(A(log_dt)[0][:, None], N, 1))], 1)

    def up(gate, w):
        return np.stack([tile_w(A(gate)[0]), tile_w(A(w)[0])], 1).reshape(2 * FT, P, D)

    data = {
        "x": x.T.reshape(DT, P, TOK).transpose(1, 0, 2),
        "tabs": make_tables(),
        "vec": vec,
        "shift": A(state_shift)[0].T.reshape(RT, P, NB).transpose(1, 0, 2),
        "wkv": A(state_wkv)[0].reshape(NB, 4, 2, N, N).transpose(2, 4, 1, 0, 3).reshape(P, 4 * NB, N),
        "ffn1_up": up(ffn1_gate, ffn1_up), "ffn1_down": tile_w(A(ffn1_down)[0]),
        "ffn2_up": up(ffn2_gate, ffn2_up), "ffn2_down": tile_w(A(ffn2_down)[0]),
        "w_mix": tile_w(win[:, :mix_cols]), "w_gates": tile_w(win[:, mix_cols:]),
        "lora_up": np.concatenate([A(w_up)[0], A(a_up)[0]], 0), "g_up": A(g_up)[0],
        "lnx_w": A(lnx_w)[0][None], "lnx_b": A(lnx_b)[0][None],
        "s5_b": np.stack([pairs(A(B_re)[0]), pairs(A(B_im)[0])], 1),
        "s5_c": np.stack([pairs(A(C_re)[0].transpose(0, 2, 1)), pairs(A(C_im)[0].transpose(0, 2, 1))], 1),
        "s5_x0": np.stack([pairs(A(s)[0].transpose(1, 2, 0)) for s in (state_s5_re, state_s5_im)], 1),
        "w_glu": tile_w(A(w_glu)[0]),
        "w_ab": np.stack([tile_w(A(w_a_up)[0]), tile_w(A(w_b_up)[0])], 1).reshape(2 * DT, P, W),
        "w_out": tile_w(A(w_out)[0]),
    }
    data = {n: np.ascontiguousarray(v) for n, v in data.items()}
    nc = _bacc.Bacc("TRN2", target_bir_lowering=False, num_devices=1)
    ins = {n: nc.dram_tensor(n, v.shape, F32, kind="ExternalInput").ap() for n, v in data.items()}
    outs = {n: nc.dram_tensor(n, s, F32, kind="ExternalOutput").ap() for n, s in OUTPUTS.items()}
    build(nc, ins, outs)
    nc.finalize()
    res = run_bass_kernel_spmd(nc, [data], core_ids=[0]).results[0]

    y = res["y"].transpose(1, 0, 2).reshape(D, TOK).T
    last = res["last"].transpose(1, 0, 2).reshape(RT * P, NB + 1).T
    wkv_p = res["wkv_prompt"].reshape(2, N, 4, N).transpose(2, 0, 3, 1).reshape(H, N, N)
    wkv_s = res["wkv_sample"].reshape(2, N, 4, NB, N).transpose(3, 2, 0, 4, 1).reshape(NB, H, N, N)
    s5_p = [unpairs(res["s5_prompt"][:, n]) for n in range(2)]
    s5_s = [unpairs(res["s5_sample"][:, n]).transpose(2, 0, 1) for n in range(2)]
    out = (y[None, :SEQ], y[SEQ:, None], last[None, 0:1], wkv_p[None, None], s5_p[0][None, None], s5_p[1][None, None],
           last[None, 1:], wkv_s[None], s5_s[0][None], s5_s[1][None])
    return tuple(np.ascontiguousarray(r) for r in out)
```
